# Optimizing a Trainium2 kernel written in Bass

```python
import math
import jax
import jax.numpy as jnp
from jax import lax
import numpy as np

D_MODEL = 1024
BATCH = 1
SEQ = 1024
DEPTH = 1
DEC_BATCH = 8
DEC_SEQ = 4
PAST_LEN = 4096
PAGE_SIZE = 128

M_HEADS = 4
M_HEAD_DIM = D_MODEL // M_HEADS
M_WIDTH = M_HEADS * M_HEAD_DIM
M_CHUNK = 128
A_HEADS = 16
A_KV_HEADS = 4
A_GROUP = A_HEADS // A_KV_HEADS
A_HEAD_DIM = D_MODEL // A_HEADS
A_Q_WIDTH = A_HEADS * A_HEAD_DIM
A_KV_WIDTH = A_KV_HEADS * A_HEAD_DIM
WINDOW = 128
ROPE_DIM = A_HEAD_DIM // 4
ROPE_THETA = 500000.0
N_GROUPS = 4
EXPERTS_PER_GROUP = 8
N_EXPERTS = N_GROUPS * EXPERTS_PER_GROUP
TOP_K = 2
EXPERT_FF = D_MODEL // 4
MOE_BLOCK = 128
EPS = 1e-6
SPLITS = (M_WIDTH, M_WIDTH, M_WIDTH, M_WIDTH, 2 * M_HEADS, A_Q_WIDTH, A_KV_WIDTH, A_KV_WIDTH, D_MODEL, D_MODEL)
IN_WIDTH = sum(SPLITS)

kernel_name = 'hybrid_mlstm_swa_hmoe_step'

def _rmsnorm(x, g):
    xf = x.astype(jnp.float32)
    y = xf * lax.rsqrt(jnp.mean(xf * xf, axis=-1, keepdims=True) + EPS)
    return (y * g.astype(jnp.float32)).astype(x.dtype)

def _rope_partial(x, pos):
    half = ROPE_DIM // 2
    inv_freq = jnp.power(jnp.float32(ROPE_THETA), -jnp.arange(0, ROPE_DIM, 2, dtype=jnp.float32) / ROPE_DIM)
    ang = pos.astype(jnp.float32)[:, None] * inv_freq[None, :]
    cos = jnp.cos(ang)[:, None, :]
    sin = jnp.sin(ang)[:, None, :]
    xf = x.astype(jnp.float32)
    x1 = xf[..., :half]
    x2 = xf[..., half:ROPE_DIM]
    out = jnp.concatenate([x1 * cos - x2 * sin, x2 * cos + x1 * sin, xf[..., ROPE_DIM:]], axis=-1)
    return out.astype(x.dtype)

def _sink_attention(q, k, v, qpos, kpos, sinks):
    s = jnp.einsum('...qkgd,...skd->...kgqs', q, k).astype(jnp.float32) * (A_HEAD_DIM ** -0.5)
    rel = qpos[..., :, None] - kpos[..., None, :]
    mask = (rel >= 0) & (rel < WINDOW) & (kpos[..., None, :] >= 0)
    s = jnp.where(mask[..., None, None, :, :], s, -jnp.inf)
    sink = sinks.astype(jnp.float32).reshape(A_KV_HEADS, A_GROUP)[:, :, None]
    m = jnp.maximum(jnp.max(s, axis=-1), sink)
    p = jnp.exp(s - m[..., None])
    den = jnp.sum(p, axis=-1) + jnp.exp(sink - m)
    probs = (p / den[..., None]).astype(v.dtype)
    return jnp.einsum('...kgqs,...skd->...qkgd', probs, v)

def _swa_prompt(q, k, v, sinks):
    b, t = q.shape[:2]
    nb = t // WINDOW
    qb = q.reshape(b, nb, WINDOW, A_KV_HEADS, A_GROUP, A_HEAD_DIM)
    kb = k.reshape(b, nb, WINDOW, A_KV_HEADS, A_HEAD_DIM)
    vb = v.reshape(b, nb, WINDOW, A_KV_HEADS, A_HEAD_DIM)

    def with_prev(a):
        prev = jnp.pad(a[:, :-1], ((0, 0), (1, 0), (0, 0), (0, 0), (0, 0)))
        return jnp.concatenate([prev, a], axis=2)

    pos = jnp.arange(t, dtype=jnp.int32).reshape(nb, WINDOW)
    kpos = jnp.concatenate([pos - WINDOW, pos], axis=-1)
    o = _sink_attention(qb, with_prev(kb), with_prev(vb), pos, kpos, sinks)
    return o.reshape(b, t, A_Q_WIDTH)

def _mlstm(q, k, v, ig, logf, c0, n0, m0):
    b, t, h, d = q.shape
    L = math.gcd(t, M_CHUNK)
    nc = t // L

    def chunks(a):
        a = jnp.moveaxis(a, 2, 1).astype(jnp.float32)
        return jnp.moveaxis(a.reshape(a.shape[:2] + (nc, L) + a.shape[3:]), 2, 0)

    causal = jnp.tril(jnp.ones((L, L), dtype=bool))

    def step(carry, xs):
        c, n, m = carry
        qc, kc, vc, ic, fc = xs
        bcum = jnp.cumsum(fc, axis=-1)
        dlog = jnp.where(causal, bcum[..., :, None] - bcum[..., None, :] + ic[..., None, :], -jnp.inf)
        mt = jnp.maximum(bcum + m[..., None], jnp.max(dlog, axis=-1))
        dmat = jnp.exp(dlog - mt[..., None])
        sc = jnp.exp(bcum + m[..., None] - mt)
        s = jnp.einsum('bhld,bhsd->bhls', qc, kc) * dmat
        num = jnp.einsum('bhls,bhsd->bhld', s, vc) + sc[..., None] * jnp.einsum('bhld,bhde->bhle', qc, c)
        den = jnp.sum(s, axis=-1) + sc * jnp.einsum('bhld,bhd->bhl', qc, n)
        hout = num / jnp.maximum(jnp.abs(den), jnp.exp(-mt))[..., None]
        m_end = mt[..., -1]
        ws = jnp.exp(bcum[..., -1:] - bcum + ic - m_end[..., None])
        wc = jnp.exp(bcum[..., -1] + m - m_end)
        kw = kc * ws[..., None]
        c_new = wc[..., None, None] * c + jnp.einsum('bhsd,bhse->bhde', kw, vc)
        n_new = wc[..., None] * n + jnp.sum(kw, axis=-2)
        return (c_new, n_new, m_end), hout

    init = (c0.astype(jnp.float32), n0.astype(jnp.float32), m0.astype(jnp.float32))
    (c, n, m), hs = lax.scan(step, init, (chunks(q), chunks(k), chunks(v), chunks(ig), chunks(logf)))
    hs = jnp.moveaxis(jnp.moveaxis(hs, 0, 2).reshape(b, h, t, d), 1, 2)
    return hs, c, n, m

def _hier_moe(hx, w_group, b_group, w_router, b_router, w_gate_e, w_up_e, w_down_e):
    n_tok, d = hx.shape
    g_logits = (hx @ w_group).astype(jnp.float32) + b_group.astype(jnp.float32)
    p_group = jax.nn.softmax(g_logits, axis=-1)
    grp = jnp.argmax(g_logits, axis=-1)
    e_logits = ((hx @ w_router).astype(jnp.float32) + b_router.astype(jnp.float32)).reshape(n_tok, N_GROUPS, EXPERTS_PER_GROUP)
    in_grp = jnp.take_along_axis(e_logits, grp[:, None, None], axis=1)[:, 0]
    top_v, top_i = lax.top_k(in_grp, TOP_K)
    gate = jax.nn.softmax(top_v, axis=-1) * jnp.take_along_axis(p_group, grp[:, None], axis=1)
    flat_e = (grp[:, None] * EXPERTS_PER_GROUP + top_i).reshape(-1).astype(jnp.int32)
    flat_w = gate.reshape(-1)
    n_asg = n_tok * TOP_K
    flat_tok = jnp.arange(n_asg, dtype=jnp.int32) // TOP_K
    order = jnp.argsort(flat_e)
    se = flat_e[order]
    counts = jnp.bincount(flat_e, length=N_EXPERTS)
    padded = (counts + MOE_BLOCK - 1) // MOE_BLOCK * MOE_BLOCK
    pad_end = jnp.cumsum(padded)
    pad_start = pad_end - padded
    start = jnp.cumsum(counts) - counts
    dest = pad_start[se] + jnp.arange(n_asg, dtype=jnp.int32) - start[se]
    n_blocks = -(-n_asg // MOE_BLOCK) + N_EXPERTS
    rows = n_blocks * MOE_BLOCK
    row_tok = jnp.full((rows,), n_tok, dtype=jnp.int32).at[dest].set(flat_tok[order])
    row_w = jnp.zeros((rows,), jnp.float32).at[dest].set(flat_w[order])
    blk_e = jnp.minimum(jnp.searchsorted(pad_end, jnp.arange(n_blocks, dtype=jnp.int32) * MOE_BLOCK, side='right'), N_EXPERTS - 1)
    h_pad = jnp.concatenate([hx, jnp.zeros((1, d), hx.dtype)], axis=0)
    xs = h_pad[row_tok].reshape(n_blocks, MOE_BLOCK, d)

    def expert(args):
        xb, e = args
        return (jax.nn.silu(xb @ w_gate_e[e]) * (xb @ w_up_e[e])) @ w_down_e[e]

    ys = lax.map(expert, (xs, blk_e)).reshape(rows, d)
    out = jnp.zeros((n_tok + 1, d), jnp.float32).at[row_tok].add(ys.astype(jnp.float32) * row_w[:, None])
    return out[:n_tok].astype(hx.dtype)

def _decoder_layer(x, pos, mstate, kv_past, w_in, b_if, norm_mix, mlstm_norm, attn_sinks,
                   w_proj_a, w_proj_b, w_out, norm_ffn, w_group, b_group, w_router, b_router,
                   w_gate_e, w_up_e, w_down_e):
    b, t, _ = x.shape
    h = _rmsnorm(x, norm_mix)
    z = h @ w_in
    cuts = [int(c) for c in np.cumsum(SPLITS)[:-1]]
    mq, mk, mv, mo, mif, aq, ak, av, ga, gb = jnp.split(z, cuts, axis=-1)
    gates = mif.astype(jnp.float32) + b_if.astype(jnp.float32)
    ig = gates[..., :M_HEADS]
    logf = jax.nn.log_sigmoid(gates[..., M_HEADS:])
    heads = lambda a, nh, hd: a.reshape(b, t, nh, hd)
    hm, c_new, n_new, m_new = _mlstm(heads(mq, M_HEADS, M_HEAD_DIM),
                                     heads(mk, M_HEADS, M_HEAD_DIM) * (M_HEAD_DIM ** -0.5),
                                     heads(mv, M_HEADS, M_HEAD_DIM), ig, logf, *mstate)
    hm = hm * lax.rsqrt(jnp.mean(hm * hm, axis=-1, keepdims=True) + EPS) * mlstm_norm.astype(jnp.float32).reshape(M_HEADS, M_HEAD_DIM)
    hm = (hm.reshape(b, t, M_WIDTH) * jax.nn.sigmoid(mo.astype(jnp.float32))).astype(x.dtype)
    branch_a = hm @ w_proj_a
    q = _rope_partial(heads(aq, A_HEADS, A_HEAD_DIM), pos)
    k = _rope_partial(heads(ak, A_KV_HEADS, A_HEAD_DIM), pos)
    v = heads(av, A_KV_HEADS, A_HEAD_DIM)
    if kv_past is None:
        o = _swa_prompt(q, k, v, attn_sinks)
        new_k, new_v = k[:, -WINDOW:], v[:, -WINDOW:]
    else:
        ck, cv = kv_past
        wc = ck.shape[1]
        k_all = jnp.concatenate([ck.astype(k.dtype), k], axis=1)
        v_all = jnp.concatenate([cv.astype(v.dtype), v], axis=1)
        kpos = jnp.concatenate([pos[0] - wc + jnp.arange(wc, dtype=jnp.int32), pos])
        o = _sink_attention(q.reshape(b, t, A_KV_HEADS, A_GROUP, A_HEAD_DIM), k_all, v_all, pos, kpos, attn_sinks)
        o = o.reshape(b, t, A_Q_WIDTH)
        new_k, new_v = k_all[:, -wc:], v_all[:, -wc:]
    branch_b = o @ w_proj_b
    mixed = jax.nn.sigmoid(ga) * branch_a + jax.nn.sigmoid(gb) * branch_b
    x = x + mixed @ w_out
    f = _hier_moe(_rmsnorm(x, norm_ffn).reshape(b * t, D_MODEL), w_group, b_group, w_router, b_router,
                  w_gate_e, w_up_e, w_down_e)
    x = x + f.reshape(b, t, D_MODEL)
    return x, (c_new, n_new, m_new), (new_k, new_v)

def setup_inputs(seed: int = 0) -> dict:
    key = jax.random.key(seed)
    ks = jax.random.split(key, 32)
    f32 = jnp.float32
    nrm = lambda k, shape, scale: jax.random.normal(k, shape, f32) * scale
    cache_rows = min(WINDOW, PAST_LEN)
    b_if = jnp.concatenate([
        nrm(ks[8], (DEPTH, M_HEADS), 0.1),
        jnp.broadcast_to(jnp.linspace(3.0, 6.0, M_HEADS, dtype=f32), (DEPTH, M_HEADS)) + nrm(ks[9], (DEPTH, M_HEADS), 0.1),
    ], axis=-1)
    return {
        'x_prompt': nrm(ks[0], (BATCH, SEQ, D_MODEL), 1.0),
        'x_sample': nrm(ks[1], (DEC_BATCH, DEC_SEQ, D_MODEL), 1.0),
        'state_C': nrm(ks[2], (DEPTH, DEC_BATCH, M_HEADS, M_HEAD_DIM, M_HEAD_DIM), 0.05),
        'state_n': nrm(ks[3], (DEPTH, DEC_BATCH, M_HEADS, M_HEAD_DIM), 0.05),
        'state_m': nrm(ks[4], (DEPTH, DEC_BATCH, M_HEADS), 1.0),
        'cache_k': nrm(ks[5], (DEPTH, DEC_BATCH, cache_rows, A_KV_HEADS, A_HEAD_DIM), 1.0),
        'cache_v': nrm(ks[6], (DEPTH, DEC_BATCH, cache_rows, A_KV_HEADS, A_HEAD_DIM), 1.0),
        'w_in': nrm(ks[7], (DEPTH, D_MODEL, IN_WIDTH), D_MODEL ** -0.5),
        'b_if': b_if,
        'norm_mix': 1.0 + nrm(ks[10], (DEPTH, D_MODEL), 0.05),
        'mlstm_norm': 1.0 + nrm(ks[11], (DEPTH, M_WIDTH), 0.05),
        'attn_sinks': nrm(ks[12], (DEPTH, A_HEADS), 0.5),
        'w_proj_a': nrm(ks[13], (DEPTH, M_WIDTH, D_MODEL), M_WIDTH ** -0.5),
        'w_proj_b': nrm(ks[14], (DEPTH, A_Q_WIDTH, D_MODEL), A_Q_WIDTH ** -0.5),
        'w_out': nrm(ks[15], (DEPTH, D_MODEL, D_MODEL), D_MODEL ** -0.5),
        'norm_ffn': 1.0 + nrm(ks[16], (DEPTH, D_MODEL), 0.05),
        'w_group': nrm(ks[17], (DEPTH, D_MODEL, N_GROUPS), D_MODEL ** -0.5),
        'b_group': nrm(ks[18], (DEPTH, N_GROUPS), 0.01),
        'w_router': nrm(ks[19], (DEPTH, D_MODEL, N_EXPERTS), D_MODEL ** -0.5),
        'b_router': nrm(ks[20], (DEPTH, N_EXPERTS), 0.01),
        'w_gate_e': nrm(ks[21], (DEPTH, N_EXPERTS, D_MODEL, EXPERT_FF), D_MODEL ** -0.5),
        'w_up_e': nrm(ks[22], (DEPTH, N_EXPERTS, D_MODEL, EXPERT_FF), D_MODEL ** -0.5),
        'w_down_e': nrm(ks[23], (DEPTH, N_EXPERTS, EXPERT_FF, D_MODEL), EXPERT_FF ** -0.5),
        'norm_final': 1.0 + nrm(ks[24], (D_MODEL,), 0.05),
    }

def reference(x_prompt, x_sample, state_C, state_n, state_m, cache_k, cache_v, w_in, b_if, norm_mix,
              mlstm_norm, attn_sinks, w_proj_a, w_proj_b, w_out, norm_ffn, w_group, b_group, w_router,
              b_router, w_gate_e, w_up_e, w_down_e, norm_final):
    bp, tp = x_prompt.shape[:2]
    ts = x_sample.shape[1]
    pos_p = jnp.arange(tp, dtype=jnp.int32)
    pos_s = PAST_LEN + jnp.arange(ts, dtype=jnp.int32)
    xp, xs = x_prompt, x_sample
    pc, pn, pm, pk, pv = [], [], [], [], []
    sc, sn, sm, sk, sv = [], [], [], [], []
    for layer in range(DEPTH):
        lw = (w_in[layer], b_if[layer], norm_mix[layer], mlstm_norm[layer], attn_sinks[layer],
              w_proj_a[layer], w_proj_b[layer], w_out[layer], norm_ffn[layer], w_group[layer],
              b_group[layer], w_router[layer], b_router[layer], w_gate_e[layer], w_up_e[layer],
              w_down_e[layer])
        empty = (jnp.zeros((bp, M_HEADS, M_HEAD_DIM, M_HEAD_DIM), jnp.float32),
                 jnp.zeros((bp, M_HEADS, M_HEAD_DIM), jnp.float32),
                 jnp.zeros((bp, M_HEADS), jnp.float32))
        xp, (c1, n1, m1), (k1, v1) = _decoder_layer(xp, pos_p, empty, None, *lw)
        xs, (c2, n2, m2), (k2, v2) = _decoder_layer(
            xs, pos_s, (state_C[layer], state_n[layer], state_m[layer]), (cache_k[layer], cache_v[layer]), *lw)
        pc.append(c1); pn.append(n1); pm.append(m1); pk.append(k1); pv.append(v1)
        sc.append(c2); sn.append(n2); sm.append(m2); sk.append(k2); sv.append(v2)
    y_prompt = _rmsnorm(xp, norm_final)
    y_sample = _rmsnorm(xs, norm_final)
    p_C = jnp.stack(pc).astype(state_C.dtype)
    p_n = jnp.stack(pn).astype(state_n.dtype)
    p_m = jnp.stack(pm).astype(state_m.dtype)
    p_k = jnp.stack(pk).astype(cache_k.dtype)
    p_v = jnp.stack(pv).astype(cache_v.dtype)
    s_C = jnp.stack(sc).astype(state_C.dtype)
    s_n = jnp.stack(sn).astype(state_n.dtype)
    s_m = jnp.stack(sm).astype(state_m.dtype)
    s_k = jnp.stack(sk).astype(cache_k.dtype)
    s_v = jnp.stack(sv).astype(cache_v.dtype)
    return (y_prompt, y_sample, p_C, p_n, p_m, p_k, p_v, s_C, s_n, s_m, s_k, s_v)


_drawn_inputs = setup_inputs


def setup_inputs(seed=0):
    import zlib

    import numpy as np

    out = dict(_drawn_inputs(seed))
    spreads = {}
    factors = {'attn_sinks': 7.528, 'b_group': 3.593, 'b_router': 3.135}
    for name, (base, spread) in spreads.items():
        noise = np.random.default_rng([zlib.crc32(name.encode()), seed]).standard_normal(out[name].shape)
        drawn = base * np.exp(spread * noise) if base else spread * noise
        out[name] = jnp.asarray(drawn.astype(out[name].dtype))
    for name, factor in factors.items():
        out[name] = (out[name] * factor).astype(out[name].dtype)
    return out
```

```python
from contextlib import ExitStack

import numpy as np

import concourse.bass as bass
from concourse import mybir

F32 = mybir.dt.float32
F32R = mybir.dt.float32r
BF16 = mybir.dt.bfloat16
I32 = mybir.dt.int32
U32 = mybir.dt.uint32
ALU = mybir.AluOpType
ACT = mybir.ActivationFunctionType
AX = mybir.AxisListType

D = 1024
KT = D // 128
TP = 1024
NPT = TP // 128
NB, DS = 8, 4
TS = NB * DS
T = TP + TS
NT = NPT + 1
NC = 352
NG = T // NC
MH, MD = 4, 256
AH, AG, AD = 16, 4, 64
WIN = 128
NGRP, EPG, NE, FF = 4, 8, 32, 256
CW = 256
CHUNK = KT * CW
NOVER = (2 * T) // 128
NBLK = NE + NOVER
EPS = 1e-6
BIG = -1e30
C_MQ, C_MK, C_MV, C_MO, C_IF = 0, 1024, 2048, 3072, 4096
C_AQ, C_AK, C_AV, C_GA, C_GB = 4104, 5128, 5384, 5640, 6664
ZQ, ZK, ZV, ZO, ZW = 0, 1024, 1280, 1536, 2560
_c = 0
OFF = {}
for _n, _w in (("ident", 128), ("ustrict", 128), ("mcaus", 128), ("msamp", TS), ("amask", 256),
               ("amask0", 256), ("cos", NT * 8), ("sin", NT * 8), ("iota", 128), ("valid", NT),
               ("tokid", NT), ("bmq", NB * TS), ("bmk", NB)):
    OFF[_n] = (_c, _w)
    _c += _w
CSTW = _c
SMW = 2 * WIN + TS

N_D, N_G, N_PA, N_PB, N_WO, N_MOE = 16, 22, 30, 34, 38, 42
G_M, G_D, G_G, G_END = 3, 3 + 4 * 30, 3 + 120 + 54, 3 + 120 + 54 + 48


def rows(t):
    return 128 if t < NPT else TS


def build(nc, x_prompt, x_sample, state_C, state_n, state_m, cache_k, cache_v, w_in, b_if, norm_mix,
          mlstm_norm, attn_sinks, w_proj_a, w_proj_b, w_out, norm_ffn, w_group, b_group, w_router,
          b_router, w_gate_e, w_up_e, w_down_e, norm_final, cst_d, smask_d, rowc_d,
          y_prompt, y_sample, p_C, p_n, p_m, p_k, p_v, s_C, s_n, s_m, s_k, s_v):
    zt_d = nc.dram_tensor("zt_scratch", (T, ZW), F32, kind="Internal").ap()
    zg_d = nc.dram_tensor("zg_scratch", (2 * D, T), F32, kind="Internal").ap()
    hm_d = nc.dram_tensor("hm_scratch", (T, D), F32, kind="Internal").ap()
    o_d = nc.dram_tensor("o_scratch", (T, D), F32, kind="Internal").ap()
    h2_d = nc.dram_tensor("h2_scratch", (T, D), F32, kind="Internal").ap()
    pad_d = nc.dram_tensor("pad_scratch", (1, 16), F32, kind="Internal").ap()
    x2_d = nc.dram_tensor("x2_scratch", (T, D), F32, kind="Internal").ap()
    ys_d = nc.dram_tensor("ys_scratch", (NBLK * 128, D), F32, kind="Internal").ap()

    xp = x_prompt[0]
    xs_ = x_sample.rearrange("b t d -> (b t) d")
    yp = y_prompt[0]
    ys_out = y_sample.rearrange("b t d -> (b t) d")

    def xrows(t):
        return xp[t * 128:(t + 1) * 128, :] if t < NPT else xs_[:, :]

    wi = w_in[0].rearrange("(k p) n -> p k n", p=128)
    proj = [w[0].rearrange("(k p) n -> p k n", p=128) for w in (w_proj_a, w_proj_b, w_out)]
    wg = w_gate_e[0].rearrange("e (k p) n -> e p k n", p=128)
    wu = w_up_e[0].rearrange("e (k p) n -> e p k n", p=128)
    wd = w_down_e[0].rearrange("e (k p) n -> e p k n", p=128)

    ctx = ExitStack()
    with ctx:
        def sem(name):
            return ctx.enter_context(nc.semaphore(name))

        def alloc(stack, name, shape, dt=F32):
            return stack.enter_context(nc.sbuf_tensor(name, shape, dt))

        def sb(name, shape, dt=F32):
            return alloc(ctx, name, shape, dt)

        cst = sb("cst", [128, CSTW])
        rstd = sb("rstd", [128, NT])
        ssum = sb("ssum", [128, NT])
        msq = sb("msq", [128, NT])
        mhalf = sb("mhalf", [128, 16])
        stage = [sb(f"stage{i}", [128, CHUNK]) for i in range(2)]
        whi = [sb(f"whi{i}", [128, CHUNK], F32R) for i in range(2)]
        wlo = [sb(f"wlo{i}", [128, CHUNK], F32R) for i in range(2)]
        aTh = sb("aTh", [128, KT, T], F32R)
        aTl = sb("aTl", [128, KT, T], F32R)

        def C(name, p=128):
            o, w = OFF[name]
            return cst[0:p, o:o + w]

        s1 = ExitStack()
        with s1:
            a1 = lambda n, s, dt=F32: alloc(s1, n, s, dt)
            qT = a1("qT", [128, 2, T])
            kT = a1("kT", [128, 2, T])
            v1 = a1("v1", [128, NT, MD + 1])
            identb = a1("identb", [128, 128], BF16)
            mcausb = a1("mcausb", [128, 128], BF16)
            msampb = a1("msampb", [TS, TS], BF16)
            ones4 = a1("ones4", [MH, 128])
            gcol = a1("gcol", [128, NT, 128])
            hcol = a1("hcol", [128, NT, 4])
            wcb = a1("wcb", [128, 2 * NB])
            nmrow = a1("nmrow", [MH, T + 2 * NB])
            nmh = a1("nmh", [MH, T + 2 * NB])
            Ce = a1("Ce", [128, 2, MD + 1])
            ex = [a1(f"ex{i}", [128, 128]) for i in range(2)]
            stm = [a1(f"stm{i}", [128, 128]) for i in range(2)]
            kw = [a1(f"kw{i}", [128, MD]) for i in range(2)]
            t1 = a1("t1", [128, MD + 1])
            qTm = a1("qTm", [128, 2, NB, TS])
            wsb = a1("wsb", [TS, NB])
            pst = a1("pst", [128, 8, NT])
            zo = [a1(f"zo{i}", [128, CW]) for i in range(2)]
            zo_j = a1("zo_j", [128, MD])
            mout = a1("mout", [MH, 1 + NB])
            bif = a1("bif", [MH, 2])
            sa = ExitStack()
            with sa:
                xt = [alloc(sa, f"xt{i}", [128, D]) for i in range(2)]
                xn = [alloc(sa, f"xn{i}", [128, D]) for i in range(2)]
                gB = alloc(sa, "gB", [128, D])
                xj = alloc(sa, "xj", [128, D])
                wif = alloc(sa, "wif", [128, KT, 36])
                wifh = alloc(sa, "wifh", [128, KT, 36], F32R)
                wifl = alloc(sa, "wifl", [128, KT, 36], F32R)
            sg = ExitStack()
            with sg:
                gi = alloc(sg, "gi", [MH, T])
                gf = alloc(sg, "gf", [MH, T])
                g1 = alloc(sg, "g1", [MH, T])
                g2 = alloc(sg, "g2", [MH, T])
                gM = alloc(sg, "gM", [MH, T])
                rowc = alloc(sg, "rowc", [MH, 2, T])
                mpre = alloc(sg, "mpre", [MH, 2, NB])
                gq = alloc(sg, "gq", [128, T])
            sc_ = ExitStack()
            with sc_:
                nd = alloc(sc_, "nd", [128, NT, MD + 1])
                sC = alloc(sc_, "sC", [128, NB, 2, MD + 1])
                kwb = alloc(sc_, "kwb", [TS, NB, MD])
        s2 = ExitStack()
        with s2:
            a2 = lambda n, s, dt=F32: alloc(s2, n, s, dt)
            X = [a2(f"X{i}", [128, 1536]) for i in range(2)]
            Vw = [a2(f"Vw{i}", [128, 256]) for i in range(2)]
            qTs = a2("qTs", [128, 8, 128])
            kTs = [a2(f"kTs{i}", [128, 2, 128]) for i in range(2)]
            mx = a2("mx", [128, 16])
            nmx = a2("nmx", [128, 16])
            sdf = a2("sdf", [128, 16])
            es = a2("es", [128, 16])
            den = a2("den", [128, 16])
            rden = a2("rden", [128, 16])
            sinks = a2("sinks", [128, 16])
            sinkc = a2("sinkc", [128, 1])
            mcur = a2("mcur", [128, 256])
            rp = a2("rp", [128, 4, 20, 8])
            go = [a2(f"go{i}", [128, NC]) for i in range(2)]
            Xs = a2("Xs", [TS, 1536])
            smask = a2("smask", [128, 4, SMW])
            kc = a2("kc", [128, NB, 256])
            vc = a2("vc", [128, NB, 256])
            kTc = a2("kTc", [128, 2, NB, 128])
            qsT = a2("qsT", [128, 2, 4, 4, 8])
            kTn = a2("kTn", [128, 2, TS])
            s2a = ExitStack()
            with s2a:
                Sm = [alloc(s2a, f"Sm{i}", [128, 2, 256]) for i in range(2)]
                Pm = [alloc(s2a, f"Pm{i}", [128, 2, 256]) for i in range(2)]
                PTs = [alloc(s2a, f"PTs{i}", [128, 4, 128]) for i in range(2)]
                ot = [alloc(s2a, f"ot{i}", [128, D]) for i in range(2)]
            s2b = ExitStack()
            with s2b:
                sSm = alloc(s2b, "sSm", [128, 4, SMW])
                sP = alloc(s2b, "sP", [128, 4, SMW])
                sPT = alloc(s2b, "sPT", [128, 4, 3, 128])
                so = alloc(s2b, "so", [128, 4, AD])
        s3 = ExitStack()
        with s3:
            a3 = lambda n, s, dt=F32: alloc(s3, n, s, dt)
            mixT = a3("mixT", [128, KT, T])
            s3b = ExitStack()
            with s3b:
                b3 = lambda n, s, dt=F32: alloc(s3b, n, s, dt)
                tin = [b3(f"tin{i}", [128, D]) for i in range(2)]
                tmo = [b3(f"tmo{i}", [128, D]) for i in range(2)]
                tng = b3("tng", [128, D])
                sgt = [b3(f"sgt{i}", [128, T]) for i in range(2)]
                tmp3 = b3("tmp3", [128, NC])
        s4 = ExitStack()
        with s4:
            a4 = lambda n, s, dt=F32: alloc(s4, n, s, dt)
            idx = a4("idx", [128, NBLK], I32)
            slot = a4("slot", [128, 2, NT], I32)
            wgt = a4("wgt", [128, 2, NT])
            ovt = a4("ovt", [1, 2, NOVER], I32)
            s4a = ExitStack()
            with s4a:
                b4 = lambda n, s, dt=F32: alloc(s4a, n, s, dt)
                x2 = b4("x2", [128, NT, D])
                gF = b4("gF", [128, D])
                h2 = [b4(f"h2{i}", [128, D]) for i in range(2)]
                h2T = b4("h2T", [128, KT, 128])
                wr = b4("wr", [128, KT, 128])
                rb = b4("rb", [128, 36])
                LG = b4("LG", [128, NT, 8])
                LE = b4("LE", [128, NT, NE])
                m8 = b4("m8", [128, NT, 8])
                i8 = b4("i8", [128, NT, 8], U32)
                v8 = b4("v8", [128, NT, 8])
                j8 = b4("j8", [128, NT, 8], U32)
                r1 = b4("r1", [128, 16, NT])
                gmk = b4("gmk", [128, NT, NGRP])
                ee = b4("ee", [128, 2, NT])
                O = b4("O", [128, 2, NT, NE])
                A = b4("A", [128, NT, NE])
                Ac = b4("Ac", [128, NT + 1, NE])
                R = b4("R", [128, NT + 1, NE])
                RO = b4("RO", [128, 2, NT, NE])
                onesf = b4("onesf", [128, 128])
                cnt = b4("cnt", [128, 4, NE])
                thr = b4("thr", [128, 8])
                cmp8 = b4("cmp8", [128, NE, 8])
                cmpq = b4("cmpq", [128, 2 * NT, 8])
                ge = b4("ge", [128, NT, NGRP])
                sl = b4("sl", [128, 8, 2 * NT])
                ovf = b4("ovf", [1, 2, NOVER])
                cmp = b4("cmp", [1, NOVER, NE])
                OB = b4("OB", [128, 2 * NT, NBLK])
                OR = b4("OR", [128, 2 * NT, 128])
            s4b = ExitStack()
            with s4b:
                c4 = lambda n, s, dt=F32: alloc(s4b, n, s, dt)
                stg = stage + [c4(f"stg{i}", [128, CHUNK]) for i in range(4)]
                xg = [c4(f"xg{i}", [128, D]) for i in range(2)]
                xh = [c4(f"xh{i}", [128, KT, 128], F32R) for i in range(2)]
                xl = [c4(f"xl{i}", [128, KT, 128], F32R) for i in range(2)]
                ixs = [c4(f"ixs{i}", [128, 1], I32) for i in range(2)]
                sg_ = c4("sg_", [128, FF])
                hh = c4("hh", [128, FF])
                hTh = c4("hTh", [128, 2, 128], F32R)
                hTl = c4("hTl", [128, 2, 128], F32R)
                yo = [c4(f"yo{i}", [128, D]) for i in range(2)]
            s4c = ExitStack()
            with s4c:
                d4 = lambda n, s, dt=F32: alloc(s4c, n, s, dt)
                xr = [d4(f"xr{i}", [128, D]) for i in range(2)]
                y1 = [d4(f"y1{i}", [128, D]) for i in range(2)]
                y2 = [d4(f"y2{i}", [128, D]) for i in range(2)]
                gE = d4("gE", [128, D])
                jk = d4("jk", [128, D])

        fh = aTh[:, :, :].rearrange("p k t -> p (k t)")
        fl = aTl[:, :, :].rearrange("p k t -> p (k t)")
        WH = [w[:, :] for w in whi] + [fh[:, i * CHUNK:(i + 1) * CHUNK] for i in range(4)]
        WL = [w[:, :] for w in wlo] + [fl[:, i * CHUNK:(i + 1) * CHUNK] for i in range(4)]

        pb = [ctx.enter_context(nc.psum_tensor(f"pb{i}", [128, 512], F32)) for i in range(4)]
        pw = ctx.enter_context(nc.psum_tensor("pw", [128, 2, 512], F32))
        pq = ctx.enter_context(nc.psum_tensor("pq", [128, 2, 512], F32))
        ZB = [pb[0], pb[1]]
        AB = [pb[2], pb[3]]
        BK = [pb[0], pb[1], pb[2], pb[3], pw[:, 0, :], pw[:, 1, :], pq[:, 0, :], pq[:, 1, :]]

        ld_c = sem("ld_c")
        ld_g = sem("ld_g")
        ld_k = sem("ld_k")
        ld_x = [sem(f"ld_x{i}") for i in range(2)]
        ld_w = [sem(f"ld_w{i}") for i in range(6)]
        carry = [sem(f"carry_{e}") for e in ("pe", "dve", "pool")]
        init_v = sem("init_v")
        x_sq = sem("x_sq")
        x_ms = sem("x_ms")
        x_rs = sem("x_rs")
        x_n = sem("x_n")
        x_t = sem("x_t")
        x_hi = sem("x_hi")
        x_lo = sem("x_lo")
        w_hi = sem("w_hi")
        w_lo = sem("w_lo")
        w_use = sem("w_use")
        z_mm = sem("z_mm")
        z_ev = sem("z_ev")
        z_st = [sem(f"z_st{i}") for i in range(2)]
        gw_h = sem("gw_h")
        gw_l = sem("gw_l")
        gv_s = sem("gv_s")
        gi_r = sem("gi_r")
        gv_r = sem("gv_r")
        gq_t = sem("gq_t")
        gq_c = sem("gq_c")
        h_set = sem("h_set")
        h_wc = sem("h_wc")
        m_s1 = sem("m_s1")
        m_ex = sem("m_ex")
        m_kw = sem("m_kw")
        m_st = sem("m_st")
        m_qc = sem("m_qc")
        m_nu = sem("m_nu")
        m_t1 = sem("m_t1")
        m_nd = sem("m_nd")
        m_cu = sem("m_cu")
        m_ce = sem("m_ce")
        m_qm = sem("m_qm")
        m_kb = sem("m_kb")
        ld_s = sem("ld_s")
        u_cu = sem("u_cu")
        u_sc = sem("u_sc")
        st_s = sem("st_s")
        st_pc = sem("st_pc")
        hp_a = sem("hp_a")
        hp_m = sem("hp_m")
        hp_r = sem("hp_r")
        hp_o = sem("hp_o")
        st_hm = sem("st_hm")
        st_m = sem("st_m")
        o_cp = sem("o_cp")
        ld_X = [sem(f"ld_X{i}") for i in range(2)]
        ld_a = sem("ld_a")
        X_ro = sem("X_ro")
        X_tr = sem("X_tr")
        X_ev = sem("X_ev")
        a_s = sem("a_s")
        a_m = sem("a_m")
        a_e = sem("a_e")
        a_pt = sem("a_pt")
        a_pc = sem("a_pc")
        a_pv = sem("a_pv")
        a_es = sem("a_es")
        a_oe = sem("a_oe")
        st_o = [sem(f"st_o{i}") for i in range(2)]
        st_os = sem("st_os")
        zg_st = [sem(f"zg_st{i}") for i in range(2)]
        b_tr = sem("b_tr")
        b_v = sem("b_v")
        b_a = sem("b_a")
        st_k = sem("st_k")
        ld_t = [sem(f"ld_t{i}") for i in range(2)]
        ld_n = sem("ld_n")
        f_sg = sem("f_sg")
        f_mu = sem("f_mu")
        f_tr = sem("f_tr")
        f_hi = sem("f_hi")
        f_lo = sem("f_lo")
        ld_q = [sem(f"ld_q{i}") for i in range(2)]
        q_sg = sem("q_sg")
        q_mm = sem("q_mm")
        q_ev = sem("q_ev")
        mx_hi = sem("mx_hi")
        mx_lo = sem("mx_lo")
        ld_x2 = sem("ld_x2")
        ld_r = sem("ld_r")
        o_mm = sem("o_mm")
        o_ev = sem("o_ev")
        n_sq = sem("n_sq")
        n_ms = sem("n_ms")
        n_rs = sem("n_rs")
        n_h = sem("n_h")
        st_h = [sem(f"st_h{i}") for i in range(2)]
        n_tr = sem("n_tr")
        n_tc = sem("n_tc")
        n_lg = sem("n_lg")
        n_lc = sem("n_lc")
        init_r = sem("init_r")
        r_v = sem("r_v")
        r_a = sem("r_a")
        r_p = sem("r_p")
        st_x = sem("st_x")
        ld_f = [sem(f"ld_f{i}") for i in range(2)]
        m_end = sem("m_end")
        ld_e = sem("ld_e")
        e_ix = sem("e_ix")
        e_x = [sem(f"e_x{i}") for i in range(2)]
        e_xt = sem("e_xt")
        e_xh = sem("e_xh")
        e_xl = sem("e_xl")
        e_gu = sem("e_gu")
        e_sg = sem("e_sg")
        e_hh = sem("e_hh")
        e_ht = sem("e_ht")
        e_hi = sem("e_hi")
        e_lo = sem("e_lo")
        e_y = sem("e_y")
        e_yc = sem("e_yc")
        e_yd = sem("e_yd")
        st_y = [sem(f"st_y{i}") for i in range(2)]
        v_ld = sem("v_ld")
        v_dn = sem("v_dn")
        f_y = [sem(f"f_y{i}") for i in range(2)]
        f_a = sem("f_a")
        f_sq = sem("f_sq")
        f_ms = sem("f_ms")
        f_rs = sem("f_rs")
        f_o = sem("f_o")
        st_f = sem("st_f")

        block = ctx.enter_context(nc.Block())

        def stat(eng, *steps):
            for s in steps[:-1]:
                s()
                eng.drain()
            return steps[-1]()

        AHEAD = 2

        def M(h, c):
            return h * NT + (c + 1 + AHEAD)

        def K(h, c):
            return h * NPT + (c + 1 + AHEAD)

        def W(n):
            return n + (1 + AHEAD)

        def prev(c):
            return c - 2 if c >= 2 else -1

        def AP_(i, b, u):
            return i * 16 + (8 * b + u + 1 + AHEAD)

        def OE(i, b, g):
            return i * 8 + (4 * b + g + 1 + AG)

        def BL(i, b):
            return i * 2 + (b + 1 + AHEAD)

        def tok(t):
            return slice(t * 128, t * 128 + rows(t))

        Z0_D, Z1_D = 16 * (5 * MH + 1), 16 * (4 * MH + 1)
        Z_END = [Z0_D + 16 * 27, Z1_D + 16 * 27]

        def zst_h(h, j):
            return h * (16 * (5 if j % 2 == 0 else 4)) + 16 * (j // 2 + 1)


        def LDT(n):
            if n < NT:
                return 32 * (n // 2 + 1)
            first = NT + (n - NT) % 2
            return 32 * ((NT + 1 - n % 2) // 2) + 16 * ((n - first) // 2 + 1)

        def E(e):
            return e + (1 + AHEAD)

        R_END = 4

        def LW(par, k, m):
            return k * 16 + (16 + (16 * (N_MOE // 2) if 3 * par + m < 2 else 0))
        @block.sync
        def _(sp):
            def weights(base, src, i=None, per=0):
                n = base if i is None else i * per + base
                sp.wait_ge(w_lo, W(n - 2))
                sp.dma_start(stage[base % 2][:, :].rearrange("p (k n) -> p k n", n=CW),
                             src).then_inc(ld_w[base % 2], 16)

            def cols(w, c):
                return w[:, :, c:c + CW] if isinstance(c, int) else w[:, :, bass.ds(c, CW)]

            sp.dma_start(cst[:, :], cst_d).then_inc(ld_c, 16)
            sp.dma_start(gB[:, :], norm_mix.to_broadcast([128, D])).then_inc(ld_c, 16)
            for t in range(NT):
                if t >= 2:
                    sp.wait_ge(x_n, t - 1)
                sp.dma_start(xt[t % 2][0:rows(t), :], xrows(t)).then_inc(ld_x[t % 2], 16)
                if t == 1:
                    sp.wait_ge(init_v, 1)
                    with nc.allow_non_contiguous_dma(reason="eight columns"):
                        sp.dma_start(wif[:, :, 0:4], wi[:, :, C_IF:C_IF + 4]).then_inc(ld_g, 16)
                        sp.dma_start(wif[:, :, 32:36], wi[:, :, C_IF + 4:C_IF + 8]).then_inc(ld_g, 16)
                        for g in range(2):
                            sp.dma_start(bif[:, g:g + 1], b_if[:, g * MH:(g + 1) * MH].rearrange(
                                "o h -> h o")).then_inc(ld_g, 16)
            with sp.Fori(0, MH) as h:
                weights(0, cols(wi, h * CW + C_MQ), h, 4)
                weights(1, cols(wi, h * CW + C_MK), h, 4)
                weights(2, cols(wi, h * CW + C_MV), h, 4)
                sp.wait_ge(gq_c, NT)
                sp.wait_ge(st_s, h * (10 * 16) + 16)
                for b in range(NB):
                    sp.dma_start(sC[:, b, :, 0:MD], state_C[0, b, bass.ds(h, 1)].rearrange(
                        "o (c p) e -> p (o c) e", p=128)).then_inc(ld_s, 16)
                with nc.allow_non_contiguous_dma(reason="a column of the state"):
                    for c in range(2):
                        sp.dma_start(sC[:, :, c, MD:MD + 1],
                                     state_n[0, :, bass.ds(h, 1), c * 128:(c + 1) * 128].rearrange(
                                         "b o p -> p b o")).then_inc(ld_s, 16)
                weights(3, cols(wi, h * CW + C_AQ), h, 4)
            for j in range(2):
                weights(N_D + j, cols(wi, C_AK + j * CW))
            for j in range(4):
                weights(N_D + 2 + j, cols(wi, C_MO + j * CW))
            weights(N_G, cols(wi, C_GA))
            weights(N_G + 1, cols(wi, C_GB))
            sp.wait_ge(st_hm, MH * 32 + 16)
            sp.wait_ge(st_pc, MH * 32 + 16)
            sp.wait_ge(st_s, MH * 160 + 16)
            sp.wait_ge(st_m, 32)
            sp.wait_ge(z_mm, G_G)
            for i in range(2):
                sp.wait_ge(z_st[i], Z_END[i])
            for a, o in ((cache_k, s_k), (cache_v, s_v)):
                sp.dma_start(o[0, :, 0:WIN - DS], a[0, :, DS:WIN]).then_inc(o_cp, 16)
            sp.dma_start(sinks[:, :], attn_sinks.to_broadcast([128, AH])).then_inc(ld_a, 16)
            sp.dma_start(sinkc[:, :],
                         attn_sinks[0].unsqueeze(1).to_broadcast([AH, 8]).unsqueeze(2)).then_inc(ld_a, 16)
            sp.dma_start(smask[:, :, :], smask_d).then_inc(ld_a, 16)
            sp.dma_start(kc[:, :, :], cache_k[0].rearrange("b w g d -> w b (g d)")).then_inc(ld_a, 16)
            sp.dma_start(vc[:, :, :], cache_v[0].rearrange("b w g d -> w b (g d)")).then_inc(ld_a, 16)

            def qkv(dst, src, sem_):
                for g in range(AG):
                    sp.dma_start(dst[:, g // 2 * 512:(g // 2 + 1) * 512].rearrange(
                        "p (j a d) -> p a j d", j=4, a=2)[:, g % 2], src[:, g * 256:(g + 1) * 256].rearrange(
                        "p (j d) -> p j d", j=4)).then_inc(sem_, 16)
                sp.dma_start(dst[:, ZK:ZO], src[:, ZK:ZO]).then_inc(sem_, 16)

            qkv(Xs, zt_d[TP:T, :], ld_a)
            for i in range(4):
                for b in range(2):
                    sp.wait_ge(X_tr, BL(i, b - 2))
                    qkv(X[b], zt_d[tok(2 * i + b), :], ld_X[b])
                    if i == 1:
                        u0 = (NE + b * NPT) * 128
                        sp.dma_start(ys_d[u0:u0 + TP, :], xp).then_inc(o_cp, 16)
                    nxt = cols(wi, (C_GA, C_GB)[b] + (i + 1) * CW) if i < 3 else cols(proj[0], b * CW)
                    weights(N_G + 2 * (i + 1) + b, nxt)
            sp.wait_ge(st_k, 16 * 4)
            for b in range(2):
                sp.wait_ge(st_o[b], 16 * 5)
                sp.wait_ge(zg_st[b], 16 * 25)
            sp.wait_ge(st_os, 16 * 4)
            sp.wait_ge(o_cp, 64)
            sp.dma_start(tng[:, :], mlstm_norm.to_broadcast([128, D])).then_inc(ld_n, 16)
            for n in range(2 * NT):
                p, t = divmod(n, NT)
                if n >= 2:
                    sp.wait_ge(f_tr, n - 1)
                sp.dma_start(tin[n % 2][0:rows(t), :], (hm_d, o_d)[p][tok(t), :]).then_inc(ld_t[n % 2], 16)
                if p == 0:
                    sp.dma_start(tmo[n % 2][0:rows(t), :], zt_d[tok(t), ZO:ZO + D]
                                 ).then_inc(ld_t[n % 2], 16)
                if t == NT - 1:
                    for k in range(KT):
                        r = KT * p + k
                        if r >= 2:
                            sp.wait_ge(q_ev, 3 * (r - 1))
                        sp.dma_start(sgt[r % 2][:, :], zg_d[r * 128:(r + 1) * 128, :]).then_inc(ld_q[r % 2], 16)
                        if k % 2 == 1:
                            c = k // 2 + 2
                            weights(N_PA + 4 * p + c, cols(proj[p + c // 4], (c % 4) * CW))
            sp.wait_ge(mx_lo, KT)
            for t in range(NT):
                sp.dma_start(x2[0:rows(t), t, :], xrows(t)).then_inc(ld_x2, 16)
            sp.dma_start(gF[:, :], norm_ffn.to_broadcast([128, D])).then_inc(ld_r, 16)
            sp.wait_ge(init_r, 1)
            with nc.allow_non_contiguous_dma(reason="36 columns"):
                sp.dma_start(wr[:, :, 0:NGRP], w_group[0].rearrange("(k p) n -> p k n", p=128)).then_inc(ld_r, 16)
                sp.dma_start(wr[:, :, NGRP:NGRP + NE], w_router[0].rearrange("(k p) n -> p k n", p=128)).then_inc(ld_r, 16)
            sp.dma_start(rb[:, 0:NGRP], b_group.to_broadcast([128, NGRP])).then_inc(ld_r, 16)
            sp.dma_start(rb[:, NGRP:NGRP + NE], b_router.to_broadcast([128, NE])).then_inc(ld_r, 16)
            for c in range(2, 4):
                weights(N_WO + c, cols(proj[2], c * CW))
            for t in range(NT):
                sp.wait_ge(o_ev, 3 * NT + t + 1)
                sp.dma_start(x2_d[tok(t), :], x2[0:rows(t), t, :]).then_inc(st_x, 16)
            def expert_weights(e, par, n, back):
                for m in range(3):
                    s = 3 * par + m
                    w = (wg, wu, wd)[m]
                    src = w[e] if isinstance(e, int) else w[bass.ds(e, 1)].rearrange("o p k n -> p (o k) n")
                    sp.wait_ge(w_lo, W(n + (m - back)))
                    sp.dma_start(stg[s][:, :].rearrange("p (k n) -> p k n", k=KT if m < 2 else 2), src
                                 ).then_inc(ld_w[s], 16)

            sp.wait_ge(r_v, R_END)
            sp.wait_ge(st_x, 16 * NT)
            for i in range(2):
                sp.wait_ge(st_h[i], 16 * ((NT + 1 - i) // 2))
            sp.wait_ge(w_lo, W(N_MOE - 1))
            expert_weights(0, 0, N_MOE, 3)
            with sp.Fori(0, NE // 2 - 1) as i:
                expert_weights(2 * i + 1, 1, i * 6 + (N_MOE + 3), 6)
                expert_weights(2 * i + 2, 0, i * 6 + (N_MOE + 6), 6)
            expert_weights(NE - 1, 1, N_MOE + 3 * (NE - 1), 6)
            with sp.Fori(0, NOVER) as j:
                used_ = sp.value_load(ovt[0:1, 0, bass.ds(j, 1)], min_val=0, max_val=1)
                e_ = sp.value_load(ovt[0:1, 1, bass.ds(j, 1)], min_val=0, max_val=NE - 1)
                with sp.If(used_ > 0):
                    expert_weights(e_, 0, j * 3 + (N_MOE + 3 * NE), 3)
                with sp.Else():
                    sp.nop()
                sp.nop()
            sp.wait_ge(m_end, 1)
            sp.dma_start(gE[:, :], norm_final.unsqueeze(0).to_broadcast([128, D])).then_inc(ld_e, 16)
            for t in range(NT + 1):
                if t < NT:
                    if t >= 2:
                        sp.wait_ge(st_f, 16 * (t - 1))
                    sp.dma_start(xr[t % 2][0:rows(t), :], x2_d[tok(t), :]).then_inc(ld_f[t % 2], 16)
                if t >= 1:
                    sp.wait_ge(f_o, t)
                    dst = yp[tok(t - 1), :] if t - 1 < NPT else ys_out
                    sp.dma_start(dst, xr[(t - 1) % 2][0:rows(t - 1), :]).then_inc(st_f, 16)
            sp.wait_ge(st_f, 16 * NT)

        @block.tensor
        def _(pe):
            for s in (m_s1, m_qc, m_nu, m_cu, u_cu, w_use, X_tr, a_s, a_pt, a_pv,
                      e_xt, e_gu, e_ht, e_y):
                pe.sem_inc(s, AHEAD)
            ident = C("ident")

            def three(out, lh, ll, rh, rl, first, last):
                pe.matmul(out, ll, rh, start=first, stop=False)
                pe.matmul(out, lh, rl, start=False, stop=False)
                return pe.matmul(out, lh, rh, start=False, stop=last)

            def transpose_tile(src, n, banks, width=D):
                for k in range(width // 128):
                    mm = pe.transpose(banks[k // 4][:, (k % 4) * 128:(k % 4) * 128 + n],
                                      src[0:n, k * 128:(k + 1) * 128], ident[0:n, 0:n])
                return mm

            def feature_group(slot, m, ft, nc_, bank, M_=128):
                for k in range(KT):
                    wsl = slice(k * CW + ft * 128, k * CW + ft * 128 + M_)
                    mm = three(bank[0:M_, 0:NC], whi[slot][:, wsl], wlo[slot][:, wsl],
                               aTh[:, k, nc_ * NC:(nc_ + 1) * NC], aTl[:, k, nc_ * NC:(nc_ + 1) * NC],
                               k == 0, k == KT - 1)
                return mm

            def token_group(slot, t, bank):
                n = rows(t)
                for k in range(KT):
                    wsl = slice(k * CW, (k + 1) * CW)
                    mm = three(bank[0:n, 0:CW], aTh[:, k, tok(t)], aTl[:, k, tok(t)],
                               whi[slot][:, wsl], wlo[slot][:, wsl], k == 0, k == KT - 1)
                return mm

            pe.wait_ge(ld_c, 32)
            for t in range(NT):
                pe.wait_ge(x_n, t + 1)
                if t >= 2:
                    pe.wait_ge(x_lo, t - 1)
                banks = [pb[2], pb[3]] if t % 2 else [pb[0], pb[1]]
                transpose_tile(xn[t % 2], rows(t), banks).then_inc(x_t, 1)
            pe.wait_ge(x_lo, NT)
            pe.wait_ge(gw_l, 1)
            for g in range(NG):
                if g >= 2:
                    pe.wait_ge(z_ev, g - 1)
                for k in range(KT):
                    mm = three(ZB[(g + 1) % 2][0:36, 0:NC], wifh[:, k, :], wifl[:, k, :],
                               aTh[:, k, g * NC:(g + 1) * NC], aTl[:, k, g * NC:(g + 1) * NC],
                               k == 0, k == KT - 1)
                mm.then_inc(z_mm, 1)

            def s1(h, c):
                n, b = rows(c), AB[c % 2]
                pe.wait_ge(m_ex, M(h, prev(c)))
                pe.wait_ge(m_st, M(h, prev(c)))
                if c < 2:
                    pe.wait_ge(m_kb, h + 1)
                pe.wait_ge(m_kw, K(h, prev(c) if c < NT - 1 else c - 2))
                for d in range(2):
                    pe.matmul(b[0:n, 0:n], kT[:, d, tok(c)], qT[:, d, tok(c)], start=(d == 0), stop=(d == 1))
                pe.matmul(b[0:n, 128:128 + n], ones4[:, 0:n], nmh[:, tok(c)], start=True, stop=False)
                mk = mcausb if c < NT - 1 else msampb
                pe.matmul(b[0:n, 128:128 + n], identb[0:n, 0:n], mk[:, :], start=False, stop=True)
                for d in range(2):
                    mm = pe.transpose(b[0:n, 256 + d * 128:384 + d * 128], kT[:, d, tok(c)], ident)
                mm.then_inc(m_s1, 1)

            def s2(h, c):
                n = rows(c)
                pe.wait_ge(m_t1, M(h, c - 1))
                qc = pq[0:n, 1, 0:MD + 1]
                if c < NT - 1:
                    pe.wait_ge(m_ce, K(h, c - 1))
                    for d in range(2):
                        mm = pe.matmul(qc, qT[:, d, tok(c)], Ce[:, d, :], start=(d == 0), stop=(d == 1))
                else:
                    pe.wait_ge(m_qm, h + 1)
                    pe.wait_ge(ld_s, h * 160 + 160)
                    for b in range(NB):
                        for d in range(2):
                            mm = pe.matmul(qc, qTm[:, d, b, :], sC[:, b, d, :],
                                           start=(b == 0 and d == 0), stop=(b == NB - 1 and d == 1))
                mm.then_inc(m_qc, 1)
                pe.wait_ge(m_nd, M(h, c - 1))
                pe.wait_ge(m_st, M(h, c))
                if c == NT - 1:
                    pe.sem_inc(carry[0], 1)
                pe.matmul(pq[0:n, 0, 0:MD + 1], stm[c % 2][0:n, 0:n], v1[0:n, c, :],
                          start=True, stop=True).then_inc(m_nu, 1)
                if c == NT - 1:
                    return
                pe.wait_ge(m_kw, K(h, c))
                pe.wait_ge(m_ce, K(h, c - 1))
                if c == 0:
                    pe.wait_ge(u_sc, K(h, -1))
                for d in range(2):
                    mm = pe.matmul(pw[:, d, 0:MD + 1], kw[c % 2][:, d * 128:(d + 1) * 128], v1[:, c, :],
                                   start=True, stop=True)
                mm.then_inc(m_cu, 1)

            def s3(h, b):
                if b == 0:
                    pe.wait_ge(m_kb, h + 2)
                    pe.wait_ge(m_ce, K(h, NPT - 1))
                pe.wait_ge(u_sc, K(h, b - 1))
                for d in range(2):
                    mm = pe.matmul(pw[:, d, 0:MD + 1], kwb[:, b, d * 128:(d + 1) * 128], v1[0:TS, NT - 1, :],
                                   start=True, stop=True)
                mm.then_inc(u_cu, 1)

            def gate_columns():
                pe.wait_ge(gv_r, 1)
                for t in range(NT):
                    if t >= 2:
                        pe.wait_ge(gq_c, t - 1)
                    pe.transpose(AB[t % 2][0:rows(t), 0:128], gq[:, tok(t)], ident).then_inc(gq_t, 1)
                pe.wait_ge(gq_c, NT)

            def head_sets(h):
                pe.wait_ge(h_set, h * 2 + 1)
                pe.wait_ge(m_t1, M(h, -1))
                pe.matmul(pq[:, 1, 0:2 * NB], ones4[:, :], nmh[:, T:T + 2 * NB], start=True, stop=True
                          ).then_inc(h_wc, 1)

            def z_wait(g0, i, per, j):
                pe.wait_ge(z_ev, i * per + (g0 + j - 1))

            def used(g, i, per):
                pe.wait_ge(z_mm, i * per + (g + 1))
                pe.sem_inc(w_use, 1)

            with pe.Fori(0, MH) as h:
                for j in range(12):
                    m, ft, n_ = j // 6, j % 6 // 3, j % 3
                    z_wait(G_M, h, 30, j)
                    if j % 6 == 0:
                        pe.wait_ge(w_lo, W(h * 4 + m))
                    mm = feature_group(m, m, ft, n_, ZB[j % 2]).then_inc(z_mm, 1)
                    if j % 6 == 5:
                        used(G_M + j, h, 30)
                with pe.If(h < 1):
                    gate_columns()
                with pe.Else():
                    pe.nop()
                head_sets(h)
                for j in range(18):
                    z_wait(G_M, h, 30, 12 + j)
                    if j % 9 == 0:
                        pe.wait_ge(w_lo, W(h * 4 + 2 + j // 9))
                    token_group(j // 9, j % 9, ZB[j % 2]).then_inc(z_mm, 1)
                    if j % 9 == 8:
                        used(G_M + 12 + j, h, 30)
                    if j <= 8:
                        s1(h, j)
                    if 1 <= j <= 8:
                        pe.wait_ge(h_set, h * 2 + 2)
                        pe.wait_ge(z_ev, h * 30 + (G_M + 12 + j))
                        s2(h, j - 1)
                    if j == 9:
                        s2(h, 8)
                    if j >= 10:
                        s3(h, j - 10)
            with pe.Fori(0, 3) as i:
                for j in range(18):
                    z_wait(G_D, i, 18, j)
                    if j % 9 == 0:
                        pe.wait_ge(w_lo, W(i * 2 + N_D + j // 9))
                    token_group(j // 9, j % 9, ZB[j % 2]).then_inc(z_mm, 1)
                    if j % 9 == 8:
                        used(G_D + j, i, 18)

            def filler(i, b, f):
                z_wait(G_G + 6 * b, i, 12, f)
                if f == 0:
                    pe.wait_ge(w_lo, W(i * 2 + (N_G + b)))
                feature_group(b, b, f // 3, f % 3, ZB[f % 2]).then_inc(z_mm, 1)
                if f == 5:
                    used(G_G + 6 * b + f, i, 12)

            def scores(i, b, u):
                g, gp, lo = u // 2, u // 4, (u // 2 % 2) * AD
                pe.wait_ge(a_m, AP_(i, b, u - 2))
                for e in range(2):
                    q = qTs[lo:lo + AD, gp * 4 + 2 * (u % 2) + e, :]
                    for half, kk in enumerate((kTs[1 - b], kTs[b])):
                        c0 = e * 256 + half * 128
                        mm = pe.matmul(pw[:, u % 2, c0:c0 + 128], q, kk[lo:lo + AD, gp, :], start=True, stop=True)
                mm.then_inc(a_s, 1)

            def probs_t(i, b, u):
                pe.wait_ge(a_e, AP_(i, b, u))
                pe.wait_ge(a_pc, AP_(i, b, u - 2))
                for e in range(2):
                    for half in range(2):
                        mm = pe.transpose(AB[u % 2][:, (2 * e + half) * 128:(2 * e + half + 1) * 128],
                                          Pm[u % 2][:, e, half * 128:(half + 1) * 128], ident)
                mm.then_inc(a_pt, 1)

            def against_v(i, b, u):
                g, gp = u // 2, u // 4
                if u % 2 == 0:
                    pe.wait_ge(a_oe, OE(i, b, g - 2))
                pe.wait_ge(a_pc, AP_(i, b, u))
                for e in range(2):
                    jj = 2 * (u % 2) + e
                    for half, vv in enumerate((Vw[1 - b], Vw[b])):
                        mm = pe.matmul(pq[:, g % 2, jj * 128:(jj + 1) * 128], PTs[u % 2][:, 2 * e + half, :],
                                       vv[:, gp * 128:(gp + 1) * 128], start=(half == 0), stop=(half == 1))
                mm.then_inc(a_pv, 1)

            with pe.Fori(0, NPT // 2) as i:
                for b in range(2):
                    filler(i, b, 0)
                    pe.wait_ge(X_ro, i * 2 + (b + 1))
                    pe.wait_ge(a_pc, AP_(i, b, -1))
                    pe.wait_ge(a_m, AP_(i, b, -1))
                    for j in range(8):
                        pe.transpose(AB[j // 4][:, (j % 4) * 128:(j % 4 + 1) * 128],
                                     X[b][:, j * 128:(j + 1) * 128], ident)
                    for j in range(2):
                        mm = pe.transpose(pw[:, 0, j * 128:(j + 1) * 128],
                                          X[b][:, ZK + j * 128:ZK + (j + 1) * 128], ident)
                    mm.then_inc(X_tr, 1)
                    filler(i, b, 1)
                    pe.wait_ge(X_ev, i * 2 + (b + 1))
                    for u in range(10):
                        if u < 8:
                            scores(i, b, u)
                        if 1 <= u <= 8:
                            probs_t(i, b, u - 1)
                        if u >= 2:
                            against_v(i, b, u - 2)
                        if u in (1, 3, 5, 7):
                            filler(i, b, 2 + u // 2)

            pe.wait_ge(ld_a, 160)
            pe.wait_ge(z_ev, G_END)
            pe.wait_ge(a_pc, AP_(3, 1, 7))
            for b in range(NB):
                for gp in range(2):
                    j = 2 * b + gp
                    mm = pe.transpose(pb[j // 4][:, (j % 4) * 128:(j % 4 + 1) * 128],
                                      kc[:, b, gp * 128:(gp + 1) * 128], ident)
            mm.then_inc(b_tr, 1)
            pe.wait_ge(b_v, 1)
            for j in range(8):
                pe.transpose(pw[:, 0, j * TS:(j + 1) * TS], Xs[:, j * 128:(j + 1) * 128], ident[0:TS, 0:TS])
            for j in range(2):
                mm = pe.transpose(pw[:, 0, (8 + j) * TS:(9 + j) * TS], Xs[:, ZK + j * 128:ZK + (j + 1) * 128],
                                  ident[0:TS, 0:TS])
            mm.then_inc(b_tr, 1)
            pe.wait_ge(b_a, 2)
            for p in range(4):
                for g in range(AG):
                    gp, lo = g // 2, (g % 2) * AD
                    q = qsT[lo:lo + AD, gp, p, :, :].rearrange("d j t -> d (j t)")
                    out = pb[p][g * 32:(g + 1) * 32, :]
                    pe.matmul(out[:, 0:2 * WIN], q, kTc[lo:lo + AD, gp, 2 * p:2 * p + 2, :].rearrange(
                        "d b w -> d (b w)"), start=True, stop=True)
                    mm = pe.matmul(out[:, 2 * WIN:SMW], q, kTn[lo:lo + AD, gp, :], start=True, stop=True)
            mm.then_inc(b_tr, 1)
            pe.wait_ge(b_a, 3)
            for p in range(4):
                for k in range(3):
                    w = (128, 128, TS)[k]
                    mm = pe.transpose(pb[p][0:w, k * 128:(k + 1) * 128], sP[:, p, k * 128:k * 128 + w], ident)
            mm.then_inc(b_tr, 1)
            pe.wait_ge(b_v, 3)
            for p in range(4):
                for g in range(AG):
                    out = pq[g * 32:(g + 1) * 32, 0, p * AD:(p + 1) * AD]
                    for k in range(3):
                        w = (128, 128, TS)[k]
                        vv = vc[:, 2 * p + k, g * AD:(g + 1) * AD] if k < 2 else Xs[:, ZV + g * AD:ZV + (g + 1) * AD]
                        mm = pe.matmul(out, sPT[0:w, p, k, g * 32:(g + 1) * 32], vv, start=(k == 0), stop=(k == 2))
            mm.then_inc(b_tr, 1)

            TB = [[pb[2], pb[3]], [pw[:, 0, :], pw[:, 1, :]]]
            pe.wait_ge(b_v, 2)
            for p in range(2):
                for t in range(NT):
                    n = NT * p + t
                    if p == 0:
                        pe.wait_ge(f_mu, n + 1)
                    else:
                        pe.wait_ge(ld_t[n % 2], LDT(n))
                    if n >= 2:
                        pe.wait_ge(f_lo, n - 1)
                    transpose_tile(tin[n % 2], rows(t), TB[n % 2]).then_inc(f_tr, 1)
                pe.wait_ge(f_lo, NT * (p + 1))
                for c in range(4):
                    for f in range(6):
                        q = 24 * p + 6 * c + f
                        if q >= 2:
                            pe.wait_ge(q_ev, q - 1)
                        if f == 0:
                            pe.wait_ge(w_lo, W(N_PA + 4 * p + c))
                        feature_group(c % 2, c % 2, f // 3, f % 3, ZB[q % 2]).then_inc(q_mm, 1)
                    pe.wait_ge(q_mm, 24 * p + 6 * c + 6)
                    pe.sem_inc(w_use, 1)

            pe.wait_ge(mx_lo, KT)
            pe.wait_ge(q_ev, 48)
            for c in range(4):
                for t in range(NT + 3 if c == 3 else NT):
                    q = NT * c + t
                    if t < NT:
                        if q >= 2:
                            pe.wait_ge(o_ev, q - 1)
                        if t == 0:
                            pe.wait_ge(w_lo, W(N_WO + c))
                        token_group(c % 2, t, ZB[q % 2]).then_inc(o_mm, 1)
                        if t == NT - 1:
                            pe.wait_ge(o_mm, q + 1)
                            pe.sem_inc(w_use, 1)
                    if c == 3 and 2 <= t < NT + 2:
                        u = t - 2
                        pe.wait_ge(n_h, u + 1)
                        if u >= 2:
                            pe.wait_ge(n_tc, u - 1)
                        transpose_tile(h2[u % 2], rows(u), TB[u % 2]).then_inc(n_tr, 1)
                    if c == 3 and t >= 3:
                        u = t - 3
                        if u == 0:
                            pe.wait_ge(ld_r, 80)
                        pe.wait_ge(n_tc, u + 1)
                        if u >= 2:
                            pe.wait_ge(n_lc, u - 1)
                        for k in range(KT):
                            mm = pe.matmul(pq[0:rows(u), u % 2, 0:128], h2T[:, k, 0:rows(u)], wr[:, k, :],
                                           start=(k == 0), stop=(k == KT - 1))
                        mm.then_inc(n_lg, 1)
            pe.wait_ge(r_v, 2)
            pe.wait_ge(n_lc, NT)
            pe.matmul(pq[:, 0, 0:NT * NE], C("ustrict"), A[:, :, :].rearrange("p t e -> p (t e)"),
                      start=True, stop=False)
            pe.matmul(pq[:, 0, 0:NT * NE], onesf[:, :], Ac[:, 0:NT, :].rearrange("p t e -> p (t e)"),
                      start=False, stop=True)
            pe.matmul(pq[:, 1, 0:NE], onesf[:, :], Ac[:, NT, :], start=True, stop=True).then_inc(r_p, 1)
            pe.wait_ge(r_v, 3)
            for a in range(2 * NT):
                mm = pe.matmul(pw[:, 0, 0:NBLK], OR[:, a, :], OB[:, a, :], start=(a == 0), stop=(a == 2 * NT - 1))
            mm.then_inc(r_p, 1)

            pe.wait_ge(r_v, R_END)
            def transposes_x(e, par, k):
                pe.wait_ge(e_x[par], k * 16 + 16)
                pe.wait_ge(e_xl, E(e - 1))
                transpose_tile(xg[par], 128, TB[0]).then_inc(e_xt, 1)

            def transposes_h(e):
                pe.wait_ge(e_hh, E(e))
                pe.wait_ge(e_lo, E(e - 1))
                for k in range(2):
                    mm = pe.transpose(pb[0][:, k * 128:(k + 1) * 128], hh[:, k * 128:(k + 1) * 128], ident)
                mm.then_inc(e_ht, 1)

            def gate_or_up(e, par, m, n):
                if m == 0:
                    pe.wait_ge(e_xl, E(e))
                    pe.wait_ge(e_hh, E(e - 1))
                pe.wait_ge(w_lo, W(n + m))
                s = 3 * par + m
                for k in range(KT):
                    wsl = slice(k * CW, (k + 1) * CW)
                    mm = three(pw[:, m, 0:FF], xh[par][:, k, :], xl[par][:, k, :], WH[s][:, wsl], WL[s][:, wsl],
                               k == 0, k == KT - 1)
                if m == 1:
                    mm.then_inc(e_gu, 1)
                    pe.wait_ge(e_gu, E(e))
                    pe.sem_inc(w_use, 2)

            def down(e, par, n):
                pe.wait_ge(e_lo, E(e))
                pe.wait_ge(w_lo, W(n + 2))
                pe.wait_ge(e_yc, E(e - 1))
                pe.wait_ge(e_yd, E(e - 1))
                s = 3 * par + 2
                for k in range(2):
                    for half in range(2):
                        wsl = slice(k * D + half * 512, k * D + (half + 1) * 512)
                        mm = three(pq[:, half, :], hTh[:, k, :], hTl[:, k, :], WH[s][:, wsl], WL[s][:, wsl],
                                   k == 0, k == 1)
                mm.then_inc(e_y, 1)
                pe.wait_ge(e_y, E(e))
                pe.sem_inc(w_use, 1)

            def both(e, par, k, n):
                transposes_x(e, par, k)
                transposes_h(e - 1)
                gate_or_up(e, par, 0, n)
                down(e - 1, 1 - par, n - 3)
                gate_or_up(e, par, 1, n)

            transposes_x(0, 0, 0)
            gate_or_up(0, 0, 0, N_MOE)
            gate_or_up(0, 0, 1, N_MOE)
            with pe.Fori(0, NE // 2 - 1) as i:
                both(2 * i + 1, 1, i, i * 6 + (N_MOE + 3))
                both(2 * i + 2, 0, i + 1, i * 6 + (N_MOE + 6))
            both(NE - 1, 1, NE // 2 - 1, N_MOE + 3 * (NE - 1))
            transposes_h(NE - 1)
            down(NE - 1, 1, N_MOE + 3 * (NE - 1))
            with pe.Fori(0, NOVER) as j:
                used_ = pe.value_load(ovt[0:1, 0, bass.ds(j, 1)], min_val=0, max_val=1)
                with pe.If(used_ > 0):
                    n = j * 3 + (N_MOE + 3 * NE)
                    transposes_x(j + NE, 0, j + NE // 2)
                    gate_or_up(j + NE, 0, 0, n)
                    gate_or_up(j + NE, 0, 1, n)
                    transposes_h(j + NE)
                    down(j + NE, 0, n)
                with pe.Else():
                    pe.nop()
                pe.nop()

        @block.scalar
        def _(act):
            for s in (m_ex, m_kw, m_t1, a_e, e_sg, e_xh, e_hi, e_yc):
                act.sem_inc(s, AHEAD)
            act.sem_inc(hp_a, 1)

            def copy(out, in_, scale=1.0):
                return act.activation(out, in_, ACT.Copy, scale=scale)

            def split_hi(n, st, sl, lds, back=2):
                act.wait_ge(ld_w[st], lds)
                act.wait_ge(w_use, W(n - back))
                copy(WH[sl], stg[st][:, :]).then_inc(w_hi, 1)

            def lds(n, i=0, per=0):
                return i * (8 * per) + 16 * (n // 2 + 1)

            act.wait_ge(init_v, 1)
            for t in range(NT + 1):
                if t < NT:
                    act.wait_ge(ld_x[t % 2], 16 * (t // 2 + 1))
                    n = rows(t)
                    if t >= 1:
                        act.wait_ge(x_sq, t)
                    act.activation(xj[0:n, :], xt[t % 2][0:n, :], ACT.Square,
                                   accum_out=ssum[0:n, t:t + 1]).then_inc(x_sq, 1)
                if t >= 1:
                    u = t - 1
                    act.wait_ge(x_t, t)
                    banks = [pb[2], pb[3]] if u % 2 else [pb[0], pb[1]]
                    for g in range(2):
                        i_ = copy(aTh[:, 4 * g:4 * g + 4, tok(u)],
                                  banks[g][:, :].rearrange("p (a b) -> p a b", a=4)[:, :, 0:rows(u)])
                    i_.then_inc(x_hi, 1)
                if t == 2:
                    act.wait_ge(ld_g, 64)
                    copy(wifh[:, :, :], wif[:, :, :]).then_inc(gw_h, 1)
            split_hi(0, 0, 0, lds(0))
            for g in range(NG):
                act.wait_ge(z_mm, g + 1)
                gsl = slice(g * NC, (g + 1) * NC)
                act.activation(gi[:, gsl], ZB[(g + 1) % 2][0:4, 0:NC], ACT.Identity, bias=bif[:, 0:1])
                copy(gf[:, gsl], ZB[(g + 1) % 2][32:36, 0:NC]).then_inc(z_ev, 1)

            def gates():
                act.wait_ge(gv_s, 1)
                act.activation(g2[:, :], g1[:, :], ACT.Exp, scale=-1.0)
                act.drain()
                act.activation(g2[:, :], g2[:, :], ACT.Ln, bias=1.0).then_inc(gi_r, 1)
                act.wait_ge(gv_s, 2)
                act.activation(gq[32:36, :], g2[:, :], ACT.Exp)
                act.activation(gq[64:68, :], g1[:, :], ACT.Exp, scale=-1.0)
                act.activation(nmrow[:, T:T + 2 * NB], nmrow[:, T:T + 2 * NB], ACT.Exp).then_inc(gi_r, 1)
                act.wait_ge(gv_s, 3)
                act.activation(gq[96:100, :], gf[:, :], ACT.Exp).then_inc(gi_r, 1)

            def m_step(h, c):
                n, b = rows(c), AB[c % 2]
                act.wait_ge(m_s1, M(h, c))
                act.wait_ge(m_st, M(h, prev(c)))
                act.activation(ex[c % 2][0:n, 0:n], b[0:n, 128:128 + n], ACT.Exp,
                               bias=hcol[0:n, c, 0:1]).then_inc(m_ex, 1)
                if c < NT - 1:
                    act.wait_ge(m_cu, K(h, prev(c)))
                    copy(kw[c % 2][:, :], b[:, 256:512], scale=hcol[:, c, 3:4]).then_inc(m_kw, 1)

            def t1_step(h, c):
                n = rows(c)
                act.wait_ge(m_qc, M(h, c))
                act.wait_ge(m_nd, M(h, c - 1))
                copy(t1[0:n, :], pq[0:n, 1, 0:MD + 1], scale=hcol[0:n, c, 1:2]).then_inc(m_t1, 1)

            def square(h, c):
                n = rows(c)
                act.wait_ge(m_nd, M(h, c))
                act.wait_ge(hp_a, h * NT + (c + 1))
                act.activation(zo_j[0:n, 0:MD], nd[0:n, c, 0:MD], ACT.Square,
                               accum_out=pst[0:n, 0, c:c + 1]).then_inc(hp_a, 1)

            with act.Fori(0, MH) as h:
                split_hi(h * 4 + 1, 1, 1, lds(1, h, 4))
                with act.If(h < 1):
                    gates()
                with act.Else():
                    act.nop()
                for j in range(12):
                    m, ft, n_ = j // 6, j % 6 // 3, j % 3
                    act.wait_ge(z_mm, h * 30 + (G_M + 1 + j))
                    dst = (qT, kT)[m][:, ft, n_ * NC:(n_ + 1) * NC]
                    copy(dst, ZB[j % 2][:, 0:NC], scale=(1.0, MD ** -0.5)[m]).then_inc(z_ev, 1)
                    if j == 5:
                        split_hi(h * 4 + 2, 0, 0, lds(2, h, 4))
                split_hi(h * 4 + 3, 1, 1, lds(3, h, 4))
                for j in range(18):
                    t, n = j % 9, rows(j % 9)
                    act.wait_ge(z_mm, h * 30 + (G_M + 13 + j))
                    if j < 9:
                        copy(v1[0:n, t, 0:MD], ZB[j % 2][0:n, 0:CW]).then_inc(z_ev, 1)
                    else:
                        act.wait_ge(z_st[t % 2], zst_h(h, t))
                        copy(zo[t % 2][0:n, :], ZB[j % 2][0:n, 0:CW]).then_inc(z_ev, 1)
                    if j == 0:
                        act.wait_ge(h_set, h * 2 + 1)
                    if j <= 8:
                        m_step(h, j)
                    if 1 <= j <= 9:
                        t1_step(h, j - 1)
                    if j == 8:
                        split_hi(h * 4 + 4, 0, 0, lds(4, h, 4))
                    if j >= 9:
                        square(h, j - 9)
            with act.Fori(0, 3) as i:
                split_hi(i * 2 + (N_D + 1), 1, 1, lds(N_D + 1, i, 2))
                for j in range(18):
                    t, n = j % 9, rows(j % 9)
                    act.wait_ge(z_mm, i * 18 + (G_D + 1 + j))
                    act.wait_ge(z_st[j % 2], i * 144 + ((Z0_D, Z1_D)[j % 2] + 16 * (j // 2)))
                    copy(zo[j % 2][0:n, :], ZB[j % 2][0:n, 0:CW]).then_inc(z_ev, 1)
                    if j == 8:
                        split_hi(i * 2 + (N_D + 2), 0, 0, lds(N_D + 2, i, 2))

            def filler_out(i, b, f):
                act.wait_ge(z_mm, i * 12 + (G_G + 6 * b + f + 1))
                act.wait_ge(zg_st[f % 2], i * 96 + 16 * (3 * b + f // 2 + 1))
                copy(go[f % 2][:, :], ZB[f % 2][:, 0:NC]).then_inc(z_ev, 1)

            def exps(i, b, u):
                if u == 0:
                    act.wait_ge(a_oe, OE(i, b, -1))
                act.wait_ge(a_m, AP_(i, b, u))
                act.wait_ge(a_pt, AP_(i, b, u - 2))
                for e in range(2):
                    h = 2 * u + e
                    i_ = act.activation(Pm[u % 2][:, e, :], Sm[u % 2][:, e, :], ACT.Exp, bias=nmx[:, h:h + 1],
                                        accum_out=den[:, h:h + 1])
                i_.then_inc(a_e, 1)
                if u % 2 == 1:
                    g = u // 2
                    act.activation(es[:, 4 * g:4 * g + 4], sdf[:, 4 * g:4 * g + 4], ACT.Exp).then_inc(a_es, 1)

            with act.Fori(0, NPT // 2) as i:
                for b in range(2):
                    filler_out(i, b, 0)
                    act.wait_ge(X_tr, BL(i, b))
                    for gp in range(2):
                        copy(qTs[:, 4 * gp:4 * gp + 4, :], AB[gp][:, :].rearrange("p (j t) -> p j t", j=4),
                             scale=AD ** -0.5)
                    copy(kTs[b][:, :, :], pw[:, 0, 0:256].rearrange("p (j t) -> p j t", j=2)).then_inc(X_ev, 1)
                    filler_out(i, b, 1)
                    for u in range(8):
                        exps(i, b, u)
                        if u in (2, 4, 6):
                            filler_out(i, b, 1 + u // 2)
                        if u == 3:
                            split_hi(i * 2 + (N_G + b + 1), 1 - b, 1 - b, lds(N_G + b + 1, i, 2))
                    filler_out(i, b, 5)

            act.wait_ge(b_tr, 1)
            for k in range(4):
                i_ = copy(kTc[:, :, 2 * k:2 * k + 2, :].rearrange("p g b w -> p b g w"),
                          pb[k][:, :].rearrange("p (b g w) -> p b g w", b=2, g=2))
            i_.then_inc(b_a, 1)
            act.wait_ge(b_tr, 2)
            for gp in range(2):
                copy(qsT[:, gp, :, :, :].rearrange("d p j t -> d j p t"),
                     pw[:, 0, gp * 128:(gp + 1) * 128].rearrange("d (j p t) -> d j p t", j=4, p=4), scale=AD ** -0.5)
            copy(kTn[:, :, :], pw[:, 0, 256:320].rearrange("p (g t) -> p g t", g=2)).then_inc(b_a, 1)
            act.wait_ge(b_v, 2)
            for p in range(4):
                act.activation(sP[:, p, :], sSm[:, p, :], ACT.Exp, bias=nmx[:, p:p + 1], accum_out=den[:, p:p + 1])
            act.activation(es[:, 0:4], sdf[:, 0:4], ACT.Exp).then_inc(b_a, 1)

            TB = [[pb[2], pb[3]], [pw[:, 0, :], pw[:, 1, :]]]
            for p in range(2):
                split_hi(N_PA + 4 * p + 1, 1, 1, lds(N_PA + 4 * p + 1))
                for t in range(NT + 1):
                    n = NT * p + t
                    if t < NT and p == 0:
                        act.wait_ge(ld_t[n % 2], LDT(n))
                        act.activation(tmo[n % 2][0:rows(t), :], tmo[n % 2][0:rows(t), :], ACT.Sigmoid
                                       ).then_inc(f_sg, 1)
                    if t >= 1:
                        u, k = n - 1, rows(t - 1)
                        act.wait_ge(f_tr, u + 1)
                        if u == NT:
                            act.wait_ge(q_mm, 24)
                        for g in range(2):
                            i_ = copy(aTh[:, 4 * g:4 * g + 4, tok(t - 1)],
                                      TB[u % 2][g].rearrange("p (a b) -> p a b", a=4)[:, :, 0:k]
                                      if u % 2 else TB[0][g][:, :].rearrange("p (a b) -> p a b", a=4)[:, :, 0:k])
                        i_.then_inc(f_hi, 1)
                for r in range(KT * p, KT * (p + 1)):
                    act.wait_ge(ld_q[r % 2], 16 * (r // 2 + 1))
                    act.activation(sgt[r % 2][:, :], sgt[r % 2][:, :], ACT.Sigmoid).then_inc(q_sg, 1)
                    c = r % KT // 2
                    if r % 2 == 0 and c > 0:
                        n = N_PA + 4 * p + c + 1
                        split_hi(n, n % 2, n % 2, lds(n))
            act.wait_ge(q_mm, 48)
            act.wait_ge(q_ev, 48)
            for k in range(KT):
                copy(aTh[:, k, :], mixT[:, k, :]).then_inc(mx_hi, 1)

            for c in range(3):
                split_hi(N_WO + c + 1, (c + 1) % 2, (c + 1) % 2, lds(N_WO + c + 1))
            for t in range(NT + 1):
                if t < NT:
                    n = rows(t)
                    act.wait_ge(o_ev, 3 * NT + t + 1)
                    if t >= 2:
                        act.wait_ge(n_h, t - 1)
                        act.wait_ge(n_tr, t - 1)
                        act.wait_ge(st_h[t % 2], 16 * (t // 2))
                    act.activation(h2[t % 2][0:n, :], x2[0:n, t, :], ACT.Square,
                                   accum_out=ssum[0:n, t:t + 1]).then_inc(n_sq, 1)
                if t >= 1:
                    u = t - 1
                    act.wait_ge(n_tr, u + 1)
                    if u >= 1:
                        act.wait_ge(n_lg, u)
                    for g in range(2):
                        bank = TB[u % 2][g] if u % 2 else TB[0][g][:, :]
                        i_ = copy(h2T[:, 4 * g:4 * g + 4, 0:rows(u)],
                                  bank.rearrange("p (a b) -> p a b", a=4)[:, :, 0:rows(u)])
                    i_.then_inc(n_tc, 1)
            act.wait_ge(r_v, 1)
            act.activation(ge[:, :, :], ge[:, :, :], ACT.Exp)
            act.activation(r1[:, 3, :], r1[:, 2, :], ACT.Exp).then_inc(r_a, 1)

            def splits_hi(par, k, n, back):
                for m in range(3):
                    s = 3 * par + m
                    act.wait_ge(ld_w[s], LW(par, k, m))
                    act.wait_ge(w_use, W(n + (m - back)) if back else W(N_MOE - 1))
                    copy(WH[s], stg[s][:, :]).then_inc(w_hi, 1)

            def silu(e):
                act.wait_ge(e_gu, E(e))
                act.activation(sg_[:, :], pw[:, 0, 0:FF], ACT.Sigmoid).then_inc(e_sg, 1)

            def x_high(e, par):
                act.wait_ge(e_xt, E(e))
                for g in range(2):
                    i_ = copy(xh[par][:, 4 * g:4 * g + 4, :], TB[0][g][:, :].rearrange("p (a b) -> p a b", a=4))
                i_.then_inc(e_xh, 1)

            def h_high(e):
                act.wait_ge(e_ht, E(e))
                copy(hTh[:, :, :], pb[0][:, 0:256].rearrange("p (a b) -> p a b", a=2)).then_inc(e_hi, 1)

            def y_half(e, par, k):
                act.wait_ge(e_y, E(e))
                act.wait_ge(st_y[par], k * 16 + 16)
                copy(yo[par][:, 0:512], pq[:, 0, :]).then_inc(e_yc, 1)

            def both(e, par, k, n, last=False):
                silu(e - 1)
                x_high(e, par)
                h_high(e - 1)
                if not last:
                    splits_hi(1 - par, k + par, n + 3, 6)
                y_half(e - 1, 1 - par, k + (par - 1))

            act.wait_ge(r_v, R_END)
            splits_hi(0, 0, N_MOE, 0)
            x_high(0, 0)
            splits_hi(1, 0, N_MOE + 3, 6)
            with act.Fori(0, NE // 2 - 1) as i:
                both(2 * i + 1, 1, i, i * 6 + (N_MOE + 3))
                both(2 * i + 2, 0, i + 1, i * 6 + (N_MOE + 6))
            both(NE - 1, 1, NE // 2 - 1, N_MOE + 3 * (NE - 1), last=True)
            silu(NE - 1)
            h_high(NE - 1)
            y_half(NE - 1, 1, NE // 2 - 1)
            with act.Fori(0, NOVER) as j:
                used_ = act.value_load(ovt[0:1, 0, bass.ds(j, 1)], min_val=0, max_val=1)
                with act.If(used_ > 0):
                    e, k = j + NE, j + NE // 2
                    splits_hi(0, k, j * 3 + (N_MOE + 3 * NE), 3)
                    x_high(e, 0)
                    silu(e)
                    h_high(e)
                    y_half(e, 0, k)
                with act.Else():
                    act.nop()
                act.nop()
            for t in range(NT):
                act.wait_ge(f_a, t + 1)
                if t >= 1:
                    act.wait_ge(f_sq, t)
                act.activation(jk[0:rows(t), :], xr[t % 2][0:rows(t), :], ACT.Square,
                               accum_out=ssum[0:rows(t), t:t + 1]).then_inc(f_sq, 1)

        @block.vector
        def _(ve):
            for s in (m_st, m_nd, m_ce, u_sc, w_lo, a_m, a_pc,
                      e_xl, e_hh, e_lo, e_yd):
                ve.sem_inc(s, AHEAD)
            ve.sem_inc(a_oe, AG)
            ve.sem_inc(m_kb, 1)

            def split_lo(n, st, sl):
                ve.wait_ge(w_hi, n + 1)
                ve.tensor_tensor(WL[sl], stg[st][:, :], WH[sl].bitcast(F32), ALU.subtract).then_inc(w_lo, 1)

            ve.memset(wif[:, :, :], 0.0)
            ve.memset(ssum[:, :], 1.0)
            ve.memset(mhalf[:, :], -0.5).then_inc(init_v, 1)
            ve.memset(ones4[:, :], 1.0)
            ve.memset(v1[:, :, MD:MD + 1], 1.0)
            ve.memset(gcol[:, :, :], 1.0)
            ve.memset(hcol[:, :, :], 1.0)
            ve.memset(pst[:, :, :], 0.0)
            ve.wait_ge(ld_c, 32)
            ve.tensor_copy(identb[:, :], C("ident"))
            ve.tensor_copy(mcausb[:, :], C("mcaus"))
            ve.tensor_copy(msampb[:, :], C("msamp", TS))

            def x_scale(t):
                n = rows(t)
                ve.wait_ge(x_rs, t + 1)
                if t >= 2:
                    ve.wait_ge(x_t, t - 1)
                ve.scalar_tensor_tensor(out=xn[t % 2][0:n, :], in0=xt[t % 2][0:n, :],
                                        scalar=rstd[0:n, t:t + 1], in1=gB[0:n, :],
                                        op0=ALU.mult, op1=ALU.mult).then_inc(x_n, 1)

            for t in range(NT + 2):
                if t < NT:
                    ve.wait_ge(x_sq, t + 1)
                    ve.tensor_scalar(msq[0:rows(t), t:t + 1], ssum[0:rows(t), t:t + 1], 1.0 / D, EPS,
                                     ALU.mult, ALU.add).then_inc(x_ms, 1)
                if 1 <= t <= NT:
                    x_scale(t - 1)
                if t >= 2:
                    u = t - 2
                    ve.wait_ge(x_hi, u + 1)
                    banks = [pb[2], pb[3]] if u % 2 else [pb[0], pb[1]]
                    for g in range(2):
                        i_ = ve.tensor_tensor(aTl[:, 4 * g:4 * g + 4, tok(u)],
                                              banks[g][:, :].rearrange("p (a b) -> p a b", a=4)[:, :, 0:rows(u)],
                                              aTh[:, 4 * g:4 * g + 4, tok(u)].bitcast(F32), ALU.subtract)
                    i_.then_inc(x_lo, 1)
                if t == 4:
                    ve.wait_ge(gw_h, 1)
                    ve.tensor_tensor(wifl[:, :, :], wif[:, :, :], wifh[:, :, :].bitcast(F32),
                                     ALU.subtract).then_inc(gw_l, 1)
            split_lo(0, 0, 0)

            def gates():
                seq = lambda a: a[:, TP:T].rearrange("h (b s) -> h b s", s=DS)
                chk = lambda a: a[:, 0:TP].rearrange("h (c l) -> h c l", l=128)
                ve.wait_ge(z_ev, NG)
                ve.wait_ge(ld_g, 64)
                ve.wait_ge(ld_k, 32)
                ve.tensor_scalar(gf[:, :], gf[:, :], bif[:, 1:2], None, ALU.add)
                ve.drain()
                ve.scalar_tensor_tensor(out=g1[:, :], in0=gf[:, :], scalar=-1.0, in1=gf[:, :],
                                        op0=ALU.mult, op1=ALU.max).then_inc(gv_s, 1)
                ve.memset(gq[:, :], 0.0)
                ve.wait_ge(gi_r, 1)
                ve.scalar_tensor_tensor(out=g1[:, :], in0=gf[:, :], scalar=0.0, in1=g2[:, :],
                                        op0=ALU.min, op1=ALU.subtract)
                ve.drain()
                ve.tensor_tensor_scan(gf[:, :], rowc[:, 0, :], g1[:, :], 0.0, ALU.mult, ALU.add)
                ve.drain()
                ve.tensor_tensor(gi[:, :], gi[:, :], gf[:, :], ALU.subtract)
                ve.tensor_copy(g2[:, :], rowc[:, 1, :])
                ve.drain()
                ve.tensor_copy(g1[:, :], gi[:, :])
                ve.tensor_copy(chk(g2)[:, 1:NPT, 0], chk(gf)[:, 0:NPT - 1, 127])
                ve.tensor_copy(gq[0:MH, :], gi[:, :])
                ve.drain()
                ve.tensor_tensor(seq(g1)[:, :, 0], seq(gi)[:, :, 0], mpre[:, 1, :], ALU.max)
                ve.drain()
                ve.tensor_tensor_scan(gM[:, :], g2[:, :], g1[:, :], 0.0, ALU.add, ALU.max)
                ve.drain()
                ve.tensor_tensor(g1[:, :], gf[:, :], gM[:, :], ALU.add)
                ve.tensor_scalar(nmrow[:, 0:T], gM[:, :], -1.0, None, ALU.mult)
                ve.memset(mpre[:, 0, 0:1], 0.0)
                ve.drain()
                ve.tensor_copy(mpre[:, 0, 1:NPT], chk(g1)[:, 0:NPT - 1, 127])
                ve.tensor_copy(mout[:, 0:1], g1[:, TP - 1:TP])
                ve.tensor_copy(mout[:, 1:1 + NB], seq(g1)[:, :, DS - 1])
                ve.drain()
                wc = nmrow[:, T:T + 2 * NB]
                ve.tensor_tensor(wc[:, 0:NB], mpre[:, 0, :], chk(gM)[:, :, 127], ALU.subtract)
                ve.tensor_tensor(wc[:, NB:2 * NB], mpre[:, 1, :], seq(gM)[:, :, DS - 1], ALU.subtract)
                ve.tensor_tensor(chk(g2), mpre[:, 0, :].unsqueeze(2).to_broadcast([MH, NPT, 128]),
                                 chk(gM), ALU.subtract)
                ve.tensor_tensor(seq(g2), mpre[:, 1, :].unsqueeze(2).to_broadcast([MH, NB, DS]),
                                 seq(gM), ALU.subtract).then_inc(gv_s, 1)
                ve.tensor_tensor(chk(gf), chk(gi), chk(gM)[:, :, 127:128].to_broadcast([MH, NPT, 128]),
                                 ALU.subtract)
                ve.tensor_tensor(seq(gf), seq(gi), seq(gM)[:, :, DS - 1:DS].to_broadcast([MH, NB, DS]),
                                 ALU.subtract).then_inc(gv_s, 1)
                ve.wait_ge(gi_r, 3)
                ve.nop().then_inc(gv_r, 1)
                for t in range(NT):
                    ve.wait_ge(gq_t, t + 1)
                    ve.tensor_copy(gcol[0:rows(t), t, :], AB[t % 2][0:rows(t), 0:128]).then_inc(gq_c, 1)
                ve.drain()
                ve.memset(nd[:, :, :], 0.0)
                ve.drain()

            def head_set(h):
                ve.wait_ge(m_t1, M(h, -1))
                ve.wait_ge(hp_o, h + 1)
                ve.wait_ge(st_pc, h * 32 + 16)
                ve.tensor_scalar(nmh[:, :], nmrow[:, :], cst[0:MH, bass.ds(h + OFF["ident"][0], 1)], None,
                                 ALU.mult)
                for q in range(4):
                    i_ = ve.tensor_copy(hcol[:, :, q:q + 1], gcol[:, :, bass.ds(h + 32 * q, 1)])
                ve.drain()
                ve.tensor_scalar(wsb[:, :], C("bmk", TS), hcol[0:TS, NT - 1, 3:4], None, ALU.mult)
                ve.memset(Ce[:, :, :], 0.0).then_inc(h_set, 1)
                ve.wait_ge(h_wc, h + 1)
                ve.tensor_copy(wcb[:, :], pq[:, 1, 0:2 * NB])
                ve.drain()
                ve.nop().then_inc(h_set, 1)

            def weigh(h, c):
                n, b = rows(c), AB[c % 2]
                ve.wait_ge(m_ex, M(h, c))
                if c < NT - 1:
                    ve.wait_ge(m_kw, K(h, c))
                ve.wait_ge(m_nu, M(h, prev(c)))
                ve.tensor_tensor(stm[c % 2][0:n, 0:n], b[0:n, 0:n], ex[c % 2][0:n, 0:n], ALU.mult
                                 ).then_inc(m_st, 1)

            def numer(h, c):
                n = rows(c)
                ve.wait_ge(m_nu, M(h, c))
                ve.wait_ge(m_t1, M(h, c))
                if c == 0:
                    ve.wait_ge(st_hm, h * 32 + 16)
                ve.tensor_tensor(nd[0:n, c, :], pq[0:n, 0, 0:MD + 1], t1[0:n, :], ALU.add).then_inc(m_nd, 1)

            def state(h, c):
                ve.wait_ge(m_qc, M(h, c))
                ve.wait_ge(m_cu, K(h, c))
                ve.scalar_tensor_tensor(out=Ce[:, :, :], in0=Ce[:, :, :], scalar=wcb[:, c:c + 1],
                                        in1=pw[:, :, 0:MD + 1], op0=ALU.mult, op1=ALU.add).then_inc(m_ce, 1)

            def sample_state(h, b):
                ve.wait_ge(u_cu, K(h, b))
                ve.scalar_tensor_tensor(out=sC[:, b, :, :], in0=sC[:, b, :, :], scalar=wcb[:, NB + b:NB + b + 1],
                                        in1=pw[:, :, 0:MD + 1], op0=ALU.mult, op1=ALU.add).then_inc(u_sc, 1)

            def head_end(h):
                den, rec, ms, sc = (pst[:, k, :] for k in range(1, 5))
                ve.scalar_tensor_tensor(out=ms, in0=nd[:, :, MD], scalar=-1.0, in1=nd[:, :, MD],
                                        op0=ALU.mult, op1=ALU.max)
                ve.drain()
                ve.tensor_tensor(den, ms, hcol[:, :, 2], ALU.max)
                ve.drain()
                ve.reciprocal(rec, den)
                ve.drain()
                ve.tensor_tensor(den, rec, rec, ALU.mult)
                ve.drain()
                ve.wait_ge(hp_a, h * NT + (NT + 1))
                ve.tensor_tensor(ms, pst[:, 0, :], den, ALU.mult)
                ve.drain()
                ve.tensor_scalar(ms, ms, 1.0 / MD, EPS, ALU.mult, ALU.add).then_inc(hp_m, 1)
                ve.wait_ge(hp_r, h + 1)
                ve.tensor_tensor(sc, rec, pst[:, 5, :], ALU.mult)
                ve.drain()
                ve.tensor_tensor(nd[:, :, 0:MD], nd[:, :, 0:MD], sc.unsqueeze(2).to_broadcast([128, NT, MD]),
                                 ALU.mult).then_inc(hp_o, 1)

            ve.sem_inc(hp_o, 1)
            with ve.Fori(0, MH) as h:
                split_lo(h * 4 + 1, 1, 1)
                with ve.If(h < 1):
                    gates()
                with ve.Else():
                    ve.nop()
                head_set(h)
                split_lo(h * 4 + 2, 0, 0)
                ve.wait_ge(z_ev, h * 30 + (G_M + 12))
                for d in range(2):
                    i_ = ve.tensor_tensor(qTm[:, d, :, :], qT[:, d, TP:T].unsqueeze(1).to_broadcast([128, NB, TS]),
                                          C("bmq").rearrange("p (b t) -> p b t", b=NB), ALU.mult)
                i_.then_inc(m_qm, 1)
                split_lo(h * 4 + 3, 1, 1)
                for j in range(18):
                    if j <= 8:
                        weigh(h, j)
                    if j == 8:
                        ve.wait_ge(u_cu, K(h, -1))
                        ve.tensor_tensor(kwb[:, :, :], AB[0][0:TS, 256:512].unsqueeze(1).to_broadcast([TS, NB, MD]),
                                         wsb[:, :].unsqueeze(2).to_broadcast([TS, NB, MD]), ALU.mult
                                         ).then_inc(m_kb, 1)
                    if 1 <= j <= 9:
                        if j <= 8:
                            state(h, j - 1)
                        numer(h, j - 1)
                    if j == 8:
                        split_lo(h * 4 + 4, 0, 0)
                    if j >= 10:
                        sample_state(h, j - 10)
                head_end(h)
            with ve.Fori(0, 3) as i:
                split_lo(i * 2 + (N_D + 1), 1, 1)
                split_lo(i * 2 + (N_D + 2), 0, 0)

            def rope(x, n, cs, sn):
                xv = x[0:n, 0:1280].rearrange("p (h d) -> p h d", d=AD)
                x1, x2_ = xv[:, :, 0:8], xv[:, :, 8:16]
                cb = cs.unsqueeze(1).to_broadcast([n, 20, 8])
                sb_ = sn.unsqueeze(1).to_broadcast([n, 20, 8])
                r_ = [rp[0:n, k, :, :] for k in range(4)]
                ve.tensor_tensor(r_[0], x1, cb, ALU.mult)
                ve.tensor_tensor(r_[1], x2_, sb_, ALU.mult)
                ve.tensor_tensor(r_[2], x2_, cb, ALU.mult)
                ve.tensor_tensor(r_[3], x1, sb_, ALU.mult)
                ve.drain()
                ve.tensor_tensor(x1, r_[0], r_[1], ALU.subtract)
                return ve.tensor_tensor(x2_, r_[2], r_[3], ALU.add)

            def masked_max(i, b, u):
                ve.wait_ge(a_s, AP_(i, b, u))
                ve.wait_ge(a_e, AP_(i, b, u - 2))
                ve.sem_inc(carry[1], 1)
                for e in range(2):
                    h = 2 * u + e
                    ve.tensor_tensor_reduce(out=Sm[u % 2][:, e, :], in0=pw[:, u % 2, e * 256:(e + 1) * 256],
                                            in1=mcur[:, :] if b == 0 else C("amask"), scale=1.0,
                                            scalar=sinks[:, h:h + 1], op0=ALU.add, op1=ALU.max,
                                            accum_out=mx[:, h:h + 1])
                ve.drain()
                if u % 2 == 1:
                    hs = slice(2 * u - 2, 2 * u + 2)
                    ve.tensor_tensor(sdf[:, hs], sinks[:, hs], mx[:, hs], ALU.subtract)
                ve.tensor_scalar(nmx[:, 2 * u:2 * u + 2], mx[:, 2 * u:2 * u + 2], -1.0, None, ALU.mult
                                 ).then_inc(a_m, 1)

            def probs_copy(i, b, u):
                ve.wait_ge(a_pt, AP_(i, b, u))
                ve.wait_ge(a_pv, AP_(i, b, u - 2))
                ve.tensor_copy(PTs[u % 2][:, :, :], AB[u % 2][:, :].rearrange("p (k t) -> p k t", k=4)
                               ).then_inc(a_pc, 1)

            def outputs(i, b, g):
                ve.wait_ge(a_pv, AP_(i, b, 2 * g + 1))
                ve.wait_ge(a_es, i * 8 + (4 * b + g + 1))
                if g == 0:
                    ve.wait_ge(st_o[b], i * 16 + 16)
                hs = slice(4 * g, 4 * g + 4)
                ve.tensor_tensor(rden[:, hs], den[:, hs], es[:, hs], ALU.add)
                ve.drain()
                ve.reciprocal(rden[:, hs], rden[:, hs])
                ve.drain()
                lo = (g % 2) * AD
                ve.tensor_tensor(ot[b][:, g * 256:(g + 1) * 256].rearrange("p (j d) -> p j d", j=4),
                                 pq[:, g % 2, :].rearrange("p (j d) -> p j d", j=4)[:, :, lo:lo + AD],
                                 rden[:, hs].unsqueeze(2).to_broadcast([128, 4, AD]), ALU.mult).then_inc(a_oe, 1)

            def rotate_block(i, b):
                ve.wait_ge(ld_X[b], i * 80 + 80)
                ve.wait_ge(a_pv, AP_(i, b, -1))
                ve.tensor_copy(Vw[b][:, :], X[b][:, ZV:ZV + 256])
                tab = lambda name: cst[:, bass.ds(i * 16 + (OFF[name][0] + 8 * b), 8)]
                rope(X[b], 128, tab("cos"), tab("sin")).then_inc(X_ro, 1)

            ve.wait_ge(ld_a, 160)
            ve.tensor_copy(mcur[:, :], C("amask0"))
            ve.memset(kTs[1][:, :, :], 0.0)
            ve.memset(Vw[1][:, :], 0.0)
            ve.drain()
            with ve.Fori(0, NPT // 2) as i:
                for b in range(2):
                    rotate_block(i, b)
                    for u in range(10):
                        if u < 8:
                            masked_max(i, b, u)
                        if 1 <= u <= 8:
                            probs_copy(i, b, u - 1)
                        if u >= 2 and u % 2 == 1:
                            outputs(i, b, (u - 2) // 2)
                        if u == 4:
                            split_lo(i * 2 + (N_G + b + 1), 1 - b, 1 - b)
                    if b == 0:
                        ve.drain()
                        ve.tensor_copy(mcur[:, :], C("amask"))

            co = OFF["cos"][0] + 8 * NPT
            sn_ = OFF["sin"][0] + 8 * NPT
            rope(Xs, TS, cst[0:TS, co:co + 8], cst[0:TS, sn_:sn_ + 8]).then_inc(b_v, 1)
            for i in range(2):
                ve.wait_ge(st_o[i], 16 * 5)
            ve.wait_ge(b_tr, 3)
            for p in range(4):
                ve.tensor_tensor_reduce(out=sSm[:, p, :], in0=pb[p][:, 0:SMW], in1=smask[:, p, :], scale=1.0,
                                        scalar=sinkc[:, 0:1], op0=ALU.add, op1=ALU.max, accum_out=mx[:, p:p + 1])
            ve.drain()
            ve.tensor_scalar(sdf[:, 0:4], mx[:, 0:4], -1.0, sinkc[:, 0:1], ALU.mult, ALU.add)
            ve.tensor_scalar(nmx[:, 0:4], mx[:, 0:4], -1.0, None, ALU.mult).then_inc(b_v, 1)
            ve.wait_ge(b_tr, 4)
            for p in range(4):
                ve.tensor_copy(sPT[:, p, 0:2, :], pb[p][:, 0:256].rearrange("p (k t) -> p k t", k=2))
                i_ = ve.tensor_copy(sPT[0:TS, p, 2, :], pb[p][0:TS, 256:384])
            i_.then_inc(b_v, 1)
            ve.wait_ge(b_a, 3)
            ve.tensor_tensor(rden[:, 0:4], den[:, 0:4], es[:, 0:4], ALU.add)
            ve.drain()
            ve.reciprocal(rden[:, 0:4], rden[:, 0:4])
            ve.wait_ge(b_tr, 5)
            ve.drain()
            ve.tensor_tensor(so[:, :, :], pq[:, 0, 0:256].rearrange("p (k d) -> p k d", k=4),
                             rden[:, 0:4].unsqueeze(2).to_broadcast([128, 4, AD]), ALU.mult).then_inc(b_v, 1)

            TB = [[pb[2], pb[3]], [pw[:, 0, :], pw[:, 1, :]]]

            def gated(t):
                k, x = rows(t), tin[t % 2]
                ve.wait_ge(ld_t[t % 2], LDT(t))
                ve.tensor_tensor(x[0:k, :], x[0:k, :], tng[0:k, :], ALU.mult)
                ve.wait_ge(f_sg, t + 1)
                ve.drain()
                ve.tensor_tensor(x[0:k, :], x[0:k, :], tmo[t % 2][0:k, :], ALU.mult).then_inc(f_mu, 1)

            ve.wait_ge(ld_n, 16)
            for p in range(2):
                split_lo(N_PA + 4 * p + 1, 1, 1)
                for t in range(NT + 1):
                    n = NT * p + t
                    if t < NT and p == 0:
                        gated(t)
                    if t >= 1:
                        u, k = n - 1, rows(t - 1)
                        ve.wait_ge(f_hi, u + 1)
                        for g in range(2):
                            bank = TB[u % 2][g] if u % 2 else TB[0][g][:, :]
                            i_ = ve.tensor_tensor(aTl[:, 4 * g:4 * g + 4, tok(t - 1)],
                                                  bank.rearrange("p (a b) -> p a b", a=4)[:, :, 0:k],
                                                  aTh[:, 4 * g:4 * g + 4, tok(t - 1)].bitcast(F32), ALU.subtract)
                        i_.then_inc(f_lo, 1)
                for c in range(4):
                    for f in range(6):
                        q, r = 24 * p + 6 * c + f, KT * p + 2 * c + f // 3
                        cols_ = slice((f % 3) * NC, (f % 3 + 1) * NC)
                        m_, s_ = mixT[:, 2 * c + f // 3, cols_], sgt[r % 2][:, cols_]
                        ve.wait_ge(q_sg, r + 1)
                        ve.wait_ge(q_mm, q + 1)
                        if p == 0:
                            ve.tensor_tensor(m_, ZB[q % 2][:, 0:NC], s_, ALU.mult).then_inc(q_ev, 1)
                        else:
                            ve.wait_ge(q_ev, q)
                            ve.tensor_tensor(tmp3[:, :], ZB[q % 2][:, 0:NC], s_, ALU.mult)
                            ve.drain()
                            ve.tensor_tensor(m_, m_, tmp3[:, :], ALU.add).then_inc(q_ev, 1)
                        if f == 1 and c > 0:
                            n = N_PA + 4 * p + c + 1
                            split_lo(n, n % 2, n % 2)
            for k in range(KT):
                ve.wait_ge(mx_hi, k + 1)
                ve.tensor_tensor(aTl[:, k, :], mixT[:, k, :], aTh[:, k, :].bitcast(F32), ALU.subtract
                                 ).then_inc(mx_lo, 1)

            ve.wait_ge(ld_x2, 16 * NT)
            ve.memset(wr[:, :, :], 0.0).then_inc(init_r, 1)
            ve.memset(LG[:, :, :], -3e38)
            ve.memset(LE[:, :, :], 0.0)
            ve.memset(onesf[:, :], 1.0)

            def logits(t):
                n = rows(t)
                ve.wait_ge(n_lg, t + 1)
                ve.tensor_tensor(LG[0:n, t, 0:NGRP], pq[0:n, t % 2, 0:NGRP], rb[0:n, 0:NGRP], ALU.add)
                ve.tensor_tensor(LE[0:n, t, :], pq[0:n, t % 2, NGRP:NGRP + NE], rb[0:n, NGRP:NGRP + NE], ALU.add
                                 ).then_inc(n_lc, 1)

            for c in range(4):
                for t in range(NT + 3 if c == 3 else NT):
                    q, n = NT * c + t, rows(t)
                    if t < NT:
                        ve.wait_ge(o_mm, q + 1)
                        xc = x2[0:n, t, c * CW:(c + 1) * CW]
                        ve.tensor_tensor(xc, xc, ZB[q % 2][0:n, 0:CW], ALU.add).then_inc(o_ev, 1)
                    if t == 1 and c < 3:
                        n_ = N_WO + c + 1
                        split_lo(n_, n_ % 2, n_ % 2)
                    if c == 3 and t < NT:
                        ve.wait_ge(n_sq, t + 1)
                        ve.tensor_scalar(msq[0:n, t:t + 1], ssum[0:n, t:t + 1], 1.0 / D, EPS, ALU.mult, ALU.add
                                         ).then_inc(n_ms, 1)
                    if c == 3 and 1 <= t <= NT:
                        u, k = t - 1, rows(t - 1)
                        if u == 0:
                            ve.wait_ge(ld_r, 80)
                        ve.wait_ge(n_rs, u + 1)
                        ve.scalar_tensor_tensor(out=h2[u % 2][0:k, :], in0=x2[0:k, u, :], scalar=rstd[0:k, u:u + 1],
                                                in1=gF[0:k, :], op0=ALU.mult, op1=ALU.mult).then_inc(n_h, 1)
                    if c == 3 and t >= 3:
                        logits(t - 3)

            def bc(a, shape, *at):
                for k in at:
                    a = a.unsqueeze(k)
                return a.to_broadcast(shape)

            gidx, w2, dv, xv_, pg, nm = (r1[:, k, :] for k in range(6))
            io = C("iota")
            ve.drain()
            for t in range(NT):
                ve.max(m8[:, t, :], LG[:, t, :])
            ve.drain()
            for t in range(NT):
                ve.max_index(i8[:, t, :], m8[:, t, :], LG[:, t, :])
            ve.tensor_tensor(ge[:, :, :], LG[:, :, 0:NGRP], m8[:, :, 0:1].to_broadcast([128, NT, NGRP]), ALU.subtract)
            ve.drain()
            ve.tensor_copy(gidx, i8[:, :, 0])
            ve.drain()
            ve.tensor_tensor(gmk[:, :, :], bc(io[:, 0:NGRP], [128, NT, NGRP], 1), bc(gidx, [128, NT, NGRP], 2),
                             ALU.is_equal)
            ve.drain()
            ve.tensor_scalar(gmk[:, :, :], gmk[:, :, :], 1.0, -BIG, ALU.subtract, ALU.mult)
            ve.drain()
            le4 = LE[:, :, :].rearrange("p t (g e) -> p (t g) e", g=NGRP)
            ve.tensor_tensor(le4, le4, bc(gmk[:, :, :].rearrange("p t g -> p (t g)"), [128, NT * NGRP, EPG], 2),
                             ALU.add)
            ve.drain()
            for t in range(NT):
                ve.max(v8[:, t, :], LE[:, t, :])
            ve.drain()
            for t in range(NT):
                ve.max_index(j8[:, t, :], v8[:, t, :], LE[:, t, :])
            ve.tensor_tensor(dv, v8[:, :, 1], v8[:, :, 0], ALU.subtract).then_inc(r_v, 1)
            ve.drain()
            for k in range(2):
                ve.tensor_copy(ee[:, k, :], j8[:, :, k])
            ve.drain()
            for k in range(2):
                ve.tensor_tensor(O[:, k, :, :], bc(io[:, 0:NE], [128, NT, NE], 1), bc(ee[:, k, :], [128, NT, NE], 2),
                                 ALU.is_equal)
            ve.drain()
            for k in range(2):
                ve.tensor_tensor(O[:, k, :, :], O[:, k, :, :], bc(C("valid"), [128, NT, NE], 2), ALU.mult)
            ve.memset(Ac[:, 0, :], 0.0)
            ve.drain()
            ve.tensor_tensor(A[:, :, :], O[:, 0, :, :], O[:, 1, :, :], ALU.add)
            ve.drain()
            for t in range(NT):
                i_ = ve.tensor_tensor(Ac[:, t + 1, :], Ac[:, t, :], A[:, t, :], ALU.add)
                if t < NT - 1:
                    ve.drain()
            i_.then_inc(r_v, 1)
            ve.tensor_scalar(thr[:, :], io[:, 0:8], 128.0, 128.0, ALU.mult, ALU.add)
            ve.wait_ge(r_a, 1)
            ve.tensor_reduce(pg, ge[:, :, :], AX.X, ALU.add)
            ve.tensor_scalar(w2, xv_, 1.0, None, ALU.add)
            ve.drain()
            ve.tensor_tensor(nm, pg, w2, ALU.mult)
            ve.drain()
            ve.reciprocal(wgt[:, 0, :], nm)
            ve.drain()
            ve.tensor_tensor(wgt[:, 1, :], wgt[:, 0, :], xv_, ALU.mult)
            ve.wait_ge(r_p, 1)
            ve.tensor_copy(R[:, 0:NT, :], pq[:, 0, 0:NT * NE].rearrange("p (t e) -> p t e", t=NT))
            ve.tensor_copy(R[:, NT, :], pq[:, 1, 0:NE])
            ve.drain()
            ve.tensor_tensor(cmp8[:, :, :], bc(R[:, NT, :], [128, NE, 8], 2), bc(thr[:, :], [128, NE, 8], 1), ALU.is_gt)
            ve.tensor_tensor(RO[:, :, :, :], O[:, :, :, :], bc(R[:, 0:NT, :], [128, 2, NT, NE], 1), ALU.mult)
            ve.drain()
            ov, incl, base = cnt[:, 0, :], cnt[:, 1, :], cnt[:, 2, :]
            ve.tensor_reduce(ov, cmp8[:, :, :], AX.X, ALU.add)
            slv = lambda k: sl[:, k, :]
            r_, b_, q_, rr, blk, t0, mq = (slv(k) for k in range(7))
            ro = RO[:, :, :, :].rearrange("p k t e -> p (k t) e")
            ve.tensor_reduce(r_, ro, AX.X, ALU.add)
            ve.drain()
            ve.tensor_tensor_scan(incl, onesf[:, 0:NE], ov, 0.0, ALU.mult, ALU.add)
            ve.tensor_tensor(cmpq[:, :, :], bc(r_, [128, 2 * NT, 8], 2), bc(thr[:, :], [128, 2 * NT, 8], 1), ALU.is_ge)
            ve.drain()
            ve.tensor_tensor(base, incl, ov, ALU.subtract)
            ve.tensor_reduce(q_, cmpq[:, :, :], AX.X, ALU.add)
            ve.drain()
            ve.tensor_tensor(RO[:, :, :, :], O[:, :, :, :], base.unsqueeze(1).unsqueeze(1).to_broadcast(
                [128, 2, NT, NE]), ALU.mult)
            ve.scalar_tensor_tensor(out=rr, in0=q_, scalar=-128.0, in1=r_, op0=ALU.mult, op1=ALU.add)
            ve.drain()
            ve.tensor_reduce(b_, ro, AX.X, ALU.add)
            ve.drain()
            e_ = ee[:, :, :].rearrange("p k t -> p (k t)")
            ve.scalar_tensor_tensor(out=t0, in0=b_, scalar=float(NE - 1), in1=q_, op0=ALU.add, op1=ALU.add)
            ve.tensor_scalar(mq, q_, 1.0, None, ALU.min)
            ve.drain()
            ve.tensor_tensor(t0, t0, e_, ALU.subtract)
            ve.drain()
            ve.tensor_tensor(t0, t0, mq, ALU.mult)
            ve.drain()
            ve.tensor_tensor(blk, t0, e_, ALU.add)
            ve.drain()
            ve.scalar_tensor_tensor(out=t0, in0=blk, scalar=128.0, in1=rr, op0=ALU.mult, op1=ALU.add)
            ve.tensor_tensor(OR[:, :, :], bc(io, [128, 2 * NT, 128], 1), bc(rr, [128, 2 * NT, 128], 2), ALU.is_equal)
            ve.tensor_tensor(OB[:, :, :], bc(io[:, 0:NBLK], [128, 2 * NT, NBLK], 1), bc(blk, [128, 2 * NT, NBLK], 2),
                             ALU.is_equal)
            ve.drain()
            ob = OB[:, :, :].rearrange("p (k t) b -> p k t b", k=2)
            for k in range(2):
                i_ = ve.tensor_tensor(ob[:, k], ob[:, k], bc(C("tokid"), [128, NT, NBLK], 2), ALU.mult)
            i_.then_inc(r_v, 1)
            ve.tensor_copy(slot[:, :, :].rearrange("p k t -> p (k t)"), t0)
            ve.tensor_tensor(cmp[:, :, :], bc(incl[0:1], [1, NOVER, NE], 1), bc(io[0:1, 0:NOVER], [1, NOVER, NE], 2),
                             ALU.is_le)
            ve.tensor_scalar(ovf[:, 0, :], io[0:1, 0:NOVER], incl[0:1, NE - 1:NE], None, ALU.is_lt)
            ve.drain()
            ve.tensor_reduce(ovf[:, 1, :], cmp[:, :, :], AX.X, ALU.add)
            ve.drain()
            ve.tensor_scalar(ovf[:, 1, :], ovf[:, 1, :], float(NE - 1), None, ALU.min)
            ve.drain()
            ve.tensor_copy(ovt[:, :, :], ovf[:, 0:2, :])
            ve.wait_ge(r_p, 2)
            ve.tensor_copy(idx[:, :], pw[:, 0, 0:NBLK])
            ve.drain()
            ve.nop().then_inc(r_v, 1)

            def splits_lo(par, n):
                for m in range(3):
                    split_lo(n + m if isinstance(n, int) else n + m, 3 * par + m, 3 * par + m)

            def hidden(e):
                ve.wait_ge(e_sg, E(e))
                ve.wait_ge(e_ht, E(e - 1))
                ve.tensor_tensor(hh[:, :], pw[:, 0, 0:FF], sg_[:, :], ALU.mult)
                ve.drain()
                ve.tensor_tensor(hh[:, :], hh[:, :], pw[:, 1, 0:FF], ALU.mult).then_inc(e_hh, 1)

            def x_low(e, par):
                ve.wait_ge(e_xh, E(e))
                for g in range(2):
                    i_ = ve.tensor_tensor(xl[par][:, 4 * g:4 * g + 4, :],
                                          TB[0][g][:, :].rearrange("p (a b) -> p a b", a=4),
                                          xh[par][:, 4 * g:4 * g + 4, :].bitcast(F32), ALU.subtract)
                i_.then_inc(e_xl, 1)

            def h_low(e):
                ve.wait_ge(e_hi, E(e))
                ve.tensor_tensor(hTl[:, :, :], pb[0][:, 0:256].rearrange("p (a b) -> p a b", a=2),
                                 hTh[:, :, :].bitcast(F32), ALU.subtract).then_inc(e_lo, 1)

            def y_half(e, par, k):
                ve.wait_ge(e_y, E(e))
                ve.wait_ge(st_y[par], k * 16 + 16)
                ve.tensor_copy(yo[par][:, 512:D], pq[:, 1, :]).then_inc(e_yd, 1)

            def both(e, par, k, n, last=False):
                hidden(e - 1)
                x_low(e, par)
                h_low(e - 1)
                if not last:
                    splits_lo(1 - par, n + 3)
                y_half(e - 1, 1 - par, k + (par - 1))

            splits_lo(0, N_MOE)
            x_low(0, 0)
            splits_lo(1, N_MOE + 3)
            with ve.Fori(0, NE // 2 - 1) as i:
                both(2 * i + 1, 1, i, i * 6 + (N_MOE + 3))
                both(2 * i + 2, 0, i + 1, i * 6 + (N_MOE + 6))
            both(NE - 1, 1, NE // 2 - 1, N_MOE + 3 * (NE - 1), last=True)
            hidden(NE - 1)
            h_low(NE - 1)
            y_half(NE - 1, 1, NE // 2 - 1)
            with ve.Fori(0, NOVER) as j:
                used_ = ve.value_load(ovt[0:1, 0, bass.ds(j, 1)], min_val=0, max_val=1)
                with ve.If(used_ > 0):
                    e, k = j + NE, j + NE // 2
                    splits_lo(0, j * 3 + (N_MOE + 3 * NE))
                    x_low(e, 0)
                    hidden(e)
                    h_low(e)
                    y_half(e, 0, k)
                with ve.Else():
                    ve.nop()
                ve.nop()
            ve.wait_ge(ld_e, 16)
            for t in range(NT):
                n, x = rows(t), xr[t % 2]
                ve.wait_ge(ld_f[t % 2], 16 * (t // 2 + 1))
                ve.wait_ge(f_y[t % 2], 32 * (t // 2 + 1))
                for k, y in enumerate((y1, y2)):
                    i_ = ve.scalar_tensor_tensor(out=x[0:n, :], in0=y[t % 2][0:n, :], scalar=wgt[0:n, k, t:t + 1],
                                                 in1=x[0:n, :], op0=ALU.mult, op1=ALU.add)
                    if k == 0:
                        ve.drain()
                i_.then_inc(f_a, 1)
                ve.wait_ge(f_sq, t + 1)
                ve.tensor_scalar(msq[0:n, t:t + 1], ssum[0:n, t:t + 1], 1.0 / D, EPS, ALU.mult, ALU.add
                                 ).then_inc(f_ms, 1)
                ve.wait_ge(f_rs, t + 1)
                ve.scalar_tensor_tensor(out=x[0:n, :], in0=x[0:n, :], scalar=rstd[0:n, t:t + 1], in1=gE[0:n, :],
                                        op0=ALU.mult, op1=ALU.mult).then_inc(f_o, 1)

        @block.gpsimd
        def _(gp):
            gp.wait_ge(init_v, 1)
            for k, s in enumerate([st_s, st_pc, st_hm] + z_st + zg_st + st_o + st_y):
                gp.dma_start(pad_d[:, k:k + 1], mhalf[0:1, k:k + 1]).then_inc(s, 16)
            for t in range(NT):
                n = rows(t)
                gp.wait_ge(x_ms, t + 1)
                gp.tensor_tensor(rstd[0:n, t:t + 1], msq[0:n, t:t + 1], mhalf[0:n, 0:1], ALU.pow).then_inc(x_rs, 1)
            gp.wait_ge(gw_l, 1)
            gp.wait_ge(z_mm, NG)
            gp.dma_start(rowc[:, :, :], rowc_d).then_inc(ld_k, 16)
            with nc.allow_non_contiguous_dma(reason="32 floats"):
                gp.dma_start(mpre[:, 1, :], state_m[0].rearrange("b h -> h b")).then_inc(ld_k, 16)
            gp.wait_ge(gv_s, 2)
            with nc.allow_non_contiguous_dma(reason="36 floats"):
                gp.dma_start(p_m[0].rearrange("b h -> h b"), mout[:, 0:1]).then_inc(st_m, 16)
                gp.dma_start(s_m[0].rearrange("b h -> h b"), mout[:, 1:1 + NB]).then_inc(st_m, 16)
            with gp.Fori(0, MH) as h:
                for t in range(NT):
                    if t == 1:
                        gp.wait_ge(m_ce, K(h, NPT - 1))
                        gp.sem_inc(carry[2], 1)
                        gp.dma_start(p_C[0, 0, bass.ds(h, 1)].rearrange("o (c p) e -> p (o c) e", p=128),
                                     Ce[:, :, 0:MD]).then_inc(st_pc, 16)
                        with nc.allow_non_contiguous_dma(reason="a column of the state"):
                            gp.dma_start(p_n[0, 0, bass.ds(h, 1)].rearrange("o (c p) -> p (o c)", p=128),
                                         Ce[:, :, MD]).then_inc(st_pc, 16)
                    gp.wait_ge(z_ev, h * 30 + (G_M + 22 + t))
                    gp.sem_inc(carry[2], 1)
                    gp.dma_start(zt_d[tok(t), bass.ds(h * CW, CW)], zo[t % 2][0:rows(t), :]).then_inc(z_st[t % 2], 16)
                for b in range(NB):
                    gp.wait_ge(u_sc, K(h, b))
                    gp.sem_inc(carry[2], 1)
                    gp.dma_start(s_C[0, b, bass.ds(h, 1)].rearrange("o (c p) e -> p (o c) e", p=128),
                                 sC[:, b, :, 0:MD]).then_inc(st_s, 16)
                with nc.allow_non_contiguous_dma(reason="a column of the state"):
                    for c in range(2):
                        gp.dma_start(s_n[0, :, bass.ds(h, 1), c * 128:(c + 1) * 128].rearrange("b o p -> p b o"),
                                     sC[:, :, c, MD:MD + 1]).then_inc(st_s, 16)
                gp.wait_ge(hp_m, h + 1)
                gp.tensor_tensor(pst[:, 5, :], pst[:, 3, :], mhalf[:, 0:NT], ALU.pow).then_inc(hp_r, 1)
                gp.wait_ge(hp_o, h + 2)
                gp.sem_inc(carry[2], 1)
                gp.dma_start(hm_d[0:TP, bass.ds(h * MD, MD)].rearrange("(t p) e -> p t e", p=128),
                             nd[:, 0:NPT, 0:MD]).then_inc(st_hm, 16)
                gp.dma_start(hm_d[TP:T, bass.ds(h * MD, MD)], nd[0:TS, NPT, 0:MD]).then_inc(st_hm, 16)
            with gp.Fori(0, 3) as i:
                for j in range(18):
                    t = j % 9
                    gp.wait_ge(z_ev, i * 18 + (G_D + 1 + j))
                    gp.sem_inc(carry[2], 1)
                    gp.dma_start(zt_d[tok(t), bass.ds(i * 512 + (ZK + (j // 9) * CW), CW)],
                                 zo[j % 2][0:rows(t), :]).then_inc(z_st[j % 2], 16)

            with gp.Fori(0, NPT // 2) as i:
                for b in range(2):
                    for f in range(6):
                        ft, n_ = f // 3, f % 3
                        gp.wait_ge(z_ev, i * 12 + (G_G + 6 * b + f + 1))
                        gp.sem_inc(carry[2], 1)
                        gp.dma_start(zg_d[bass.ds(i * CW + (b * D + ft * 128), 128), n_ * NC:(n_ + 1) * NC],
                                     go[f % 2][:, :]).then_inc(zg_st[f % 2], 16)
                    gp.wait_ge(a_oe, OE(i, b, 3))
                    gp.sem_inc(carry[2], 1)
                    gp.dma_start(o_d[bass.ds(i * 256 + b * 128, 128), :], ot[b][:, :]).then_inc(st_o[b], 16)
            gp.dma_start(p_k[0, 0].rearrange("w g d -> w (g d)"), X[1][:, ZK:ZK + 256]).then_inc(st_k, 16)
            gp.dma_start(p_v[0, 0].rearrange("w g d -> w (g d)"), X[1][:, ZV:ZV + 256]).then_inc(st_k, 16)
            gp.wait_ge(b_v, 1)
            for o, c in ((s_k, ZK), (s_v, ZV)):
                gp.dma_start(o[0, :, WIN - DS:WIN].rearrange("b t g d -> b t (g d)"),
                             Xs[:, c:c + 256]).then_inc(st_k, 16)
            gp.wait_ge(b_v, 4)
            for p in range(4):
                gp.dma_start(o_d[TP + 8 * p:TP + 8 * p + 8, :].rearrange("t (g d) -> g t d", d=AD),
                             so[:, p, :]).then_inc(st_os, 16)

            for t in range(NT + 1):
                if t < NT:
                    n = rows(t)
                    gp.wait_ge(n_ms, t + 1)
                    gp.tensor_tensor(rstd[0:n, t:t + 1], msq[0:n, t:t + 1], mhalf[0:n, 0:1], ALU.pow
                                     ).then_inc(n_rs, 1)
                if t >= 1:
                    u = t - 1
                    gp.wait_ge(n_h, u + 1)
                    gp.dma_start(h2_d[tok(u), :], h2[u % 2][0:rows(u), :]).then_inc(st_h[u % 2], 16)

            def gather(e, par):
                gp.wait_ge(e_xt, E(e - 2))
                gp.tensor_copy(ixs[par][:, :], idx[:, e:e + 1] if isinstance(e, int) else idx[:, bass.ds(e, 1)])
                gp.drain()
                gp.indirect_dma_start(out=xg[par][:, :], out_offset=None, in_=h2_d,
                                      in_offset=bass.IndirectOffsetOnAxis(ap=ixs[par][:, 0:1], axis=0),
                                      bounds_check=T - 1).then_inc(e_x[par], 16)

            def store_y(e, par):
                gp.wait_ge(e_yc, E(e))
                gp.wait_ge(e_yd, E(e))
                gp.sem_inc(carry[2], 1)
                dst = ys_d[e * 128:(e + 1) * 128, :] if isinstance(e, int) else ys_d[bass.ds(e * 128, 128), :]
                gp.dma_start(dst, yo[par][:, :]).then_inc(st_y[par], 16)

            gp.wait_ge(r_v, R_END)
            gp.wait_ge(st_x, 16 * NT)
            for i in range(2):
                gp.wait_ge(st_h[i], 16 * ((NT + 1 - i) // 2))
            gather(0, 0)
            gather(1, 1)
            with gp.Fori(0, NE // 2 - 1) as i:
                gather(2 * i + 2, 0)
                store_y(2 * i, 0)
                gather(2 * i + 3, 1)
                store_y(2 * i + 1, 1)
            store_y(NE - 2, 0)
            store_y(NE - 1, 1)
            with gp.Fori(0, NOVER) as j:
                used_ = gp.value_load(ovt[0:1, 0, bass.ds(j, 1)], min_val=0, max_val=1)
                with gp.If(used_ > 0):
                    gather(j + NE, 0)
                    store_y(j + NE, 0)
                    gp.wait_ge(st_y[0], j * 16 + 16 * (NE // 2 + 2))
                with gp.Else():
                    gp.nop()
                gp.nop()
            for i in range(2):
                gp.wait_ge(st_y[i], 16 * (NE // 2 + 1))
            gp.sem_inc(m_end, 1)
            for t in range(NT + 1):
                if t < NT:
                    n = rows(t)
                    if t >= 2:
                        gp.wait_ge(f_a, t - 1)
                    for k, y in enumerate((y1, y2)):
                        gp.indirect_dma_start(out=y[t % 2][0:n, :], out_offset=None, in_=ys_d,
                                              in_offset=bass.IndirectOffsetOnAxis(ap=slot[0:n, k, t:t + 1], axis=0),
                                              bounds_check=NBLK * 128 - 1).then_inc(f_y[t % 2], 16)
                if t >= 1:
                    u, n = t - 1, rows(t - 1)
                    gp.wait_ge(f_ms, t)
                    gp.tensor_tensor(rstd[0:n, u:u + 1], msq[0:n, u:u + 1], mhalf[0:n, 0:1], ALU.pow
                                     ).then_inc(f_rs, 1)


def constants():
    cst = np.zeros((128, CSTW), np.float32)

    def put(name, a):
        o, w = OFF[name]
        cst[0:a.shape[0], o:o + w] = a.reshape(a.shape[0], w)

    i, j = np.arange(128)[:, None], np.arange(128)[None, :]
    put("ident", (i == j).astype(np.float32))
    put("ustrict", (i < j).astype(np.float32))
    put("mcaus", np.where(i <= j, 0.0, BIG))
    s, t = np.arange(TS)[:, None], np.arange(TS)[None, :]
    put("msamp", np.where((s <= t) & (s // DS == t // DS), 0.0, BIG))
    cur = np.where(j <= i, 0.0, BIG)
    put("amask", np.concatenate([np.where(j > i, 0.0, BIG), cur], 1))
    put("amask0", np.concatenate([np.full((128, 128), BIG), cur], 1))
    half = AD // 8
    freq = np.power(np.float32(500000.0), -np.arange(0, 2 * half, 2, dtype=np.float32) / np.float32(2 * half))
    pos = np.zeros((128, NT), np.float32)
    pos[:, :NPT] = np.arange(128)[:, None] + 128 * np.arange(NPT)[None, :]
    pos[:TS, NPT] = 4096 + np.arange(TS) % DS
    ang = (pos[:, :, None] * freq.astype(np.float32)).astype(np.float32)
    put("cos", np.cos(ang))
    put("sin", np.sin(ang))
    put("iota", np.broadcast_to(j, (128, 128)).astype(np.float32))
    tid = np.arange(128)[:, None] + 128 * np.arange(NT)[None, :]
    put("valid", (tid < T).astype(np.float32))
    put("tokid", np.where(tid < T, tid, 0).astype(np.float32))
    put("bmq", np.broadcast_to((t // DS == np.arange(NB)[:, None])[None], (128, NB, TS)).astype(np.float32))
    put("bmk", (i // DS == np.arange(NB)[None, :]).astype(np.float32))
    sm = np.full((AG, 4, 2, DS, NB // 2, SMW), BIG, np.float32)
    for b2 in range(2):
        for t_ in range(DS):
            for p in range(NB // 2):
                sm[:, :, b2, t_, p, b2 * WIN + t_ + 1:(b2 + 1) * WIN] = 0.0
                n0 = 2 * WIN + DS * (2 * p + b2)
                sm[:, :, b2, t_, p, n0:n0 + t_ + 1] = 0.0
    rowc = np.zeros((MH, 2, T), np.float32)
    rowc[:, 0] = 1.0
    rowc[:, 0, 0:TP:128] = 0.0
    rowc[:, 0, TP::DS] = 0.0
    rowc[:, 1, TP::DS] = BIG
    return cst, sm.reshape(128, NB // 2, SMW), rowc


_INS = ["x_prompt", "x_sample", "state_C", "state_n", "state_m", "cache_k", "cache_v", "w_in", "b_if",
        "norm_mix", "mlstm_norm", "attn_sinks", "w_proj_a", "w_proj_b", "w_out", "norm_ffn", "w_group",
        "b_group", "w_router", "b_router", "w_gate_e", "w_up_e", "w_down_e", "norm_final"]
_OUTS = [(1, TP, D), (NB, DS, D),
         (1, 1, MH, MD, MD), (1, 1, MH, MD), (1, 1, MH), (1, 1, WIN, AG, AD), (1, 1, WIN, AG, AD),
         (1, NB, MH, MD, MD), (1, NB, MH, MD), (1, NB, MH), (1, NB, WIN, AG, AD), (1, NB, WIN, AG, AD)]


def kernel(**inputs):
    import concourse.bacc as _bacc
    from concourse.bass_utils import run_bass_kernel_spmd as _run

    nc = _bacc.Bacc("TRN2", target_bir_lowering=False, num_devices=1)
    arrays = {f"in_{name}": np.ascontiguousarray(inputs[name]) for name in _INS}
    arrays.update(zip(("in_cst", "in_smask", "in_rowc"), constants()))
    args = [nc.dram_tensor(name, a.shape, mybir.dt.from_np(a.dtype), kind="ExternalInput").ap()
            for name, a in arrays.items()]
    for i, shape in enumerate(_OUTS):
        args.append(nc.dram_tensor(f"out_{i}", shape, F32, kind="ExternalOutput").ap())
    build(nc, *args)
    r = _run(nc, [arrays], core_ids=[0])
    return tuple(r.results[0][f"out_{i}"] for i in range(len(_OUTS)))
```

```python
from contextlib import ExitStack

import numpy as np

import concourse.bass as bass
from concourse import mybir

F32 = mybir.dt.float32
F32R = mybir.dt.float32r
BF16 = mybir.dt.bfloat16
I32 = mybir.dt.int32
U32 = mybir.dt.uint32
ALU = mybir.AluOpType
ACT = mybir.ActivationFunctionType
AX = mybir.AxisListType

D = 1024
KT = D // 128
TP = 1024
NPT = TP // 128
NB, DS = 8, 4
TS = NB * DS
T = TP + TS
NT = NPT + 1
NC = 352
NG = T // NC
MH, MD = 4, 256
AH, AG, AD = 16, 4, 64
WIN = 128
NX = 4
NGRP, EPG, NE, FF = 4, 8, 32, 256
CW = 256
CHUNK = KT * CW
NOVER = (2 * T) // 128
NBLK = NE + NOVER
EPS = 1e-6
BIG = -1e30
C_MQ, C_MK, C_MV, C_MO, C_IF = 0, 1024, 2048, 3072, 4096
C_AQ, C_AK, C_AV, C_GA, C_GB = 4104, 5128, 5384, 5640, 6664
ZQ, ZK, ZV, ZO, ZW = 0, 1024, 1280, 1536, 2560
_c = 0
OFF = {}
for _n, _w in (("ident", 128), ("ustrict", 128), ("mcaus", 128), ("msamp", TS), ("amask", 256),
               ("amask0", 256), ("cos", NT * 8), ("sin", NT * 8), ("iota", 128), ("valid", NT),
               ("tokid", NT), ("bmq", NB * TS), ("bmk", NB)):
    OFF[_n] = (_c, _w)
    _c += _w
CSTW = _c
SMW = 2 * WIN + TS

N_D, N_G, N_PA, N_PB, N_WO, N_MOE = 16, 22, 30, 34, 38, 42
G_M, G_D, G_G, G_END = 3, 3 + 4 * 30, 3 + 120 + 54, 3 + 120 + 54 + 48


def rows(t):
    return 128 if t < NPT else TS


def build(nc, x_prompt, x_sample, state_C, state_n, state_m, cache_k, cache_v, w_in, b_if, norm_mix,
          mlstm_norm, attn_sinks, w_proj_a, w_proj_b, w_out, norm_ffn, w_group, b_group, w_router,
          b_router, w_gate_e, w_up_e, w_down_e, norm_final, cst_d, smask_d, rowc_d,
          y_prompt, y_sample, p_C, p_n, p_m, p_k, p_v, s_C, s_n, s_m, s_k, s_v):
    zt_d = nc.dram_tensor("zt_scratch", (T, ZW), F32, kind="Internal").ap()
    zg_d = nc.dram_tensor("zg_scratch", (2 * D, T), F32, kind="Internal").ap()
    hm_d = nc.dram_tensor("hm_scratch", (T, D), F32, kind="Internal").ap()
    o_d = nc.dram_tensor("o_scratch", (T, D), F32, kind="Internal").ap()
    h2_d = nc.dram_tensor("h2_scratch", (T, D), F32, kind="Internal").ap()
    pad_d = nc.dram_tensor("pad_scratch", (1, 16), F32, kind="Internal").ap()
    x2_d = nc.dram_tensor("x2_scratch", (T, D), F32, kind="Internal").ap()
    ys_d = nc.dram_tensor("ys_scratch", (2 * T, D), F32, kind="Internal").ap()

    xp = x_prompt[0]
    xs_ = x_sample.rearrange("b t d -> (b t) d")
    yp = y_prompt[0]
    ys_out = y_sample.rearrange("b t d -> (b t) d")

    def xrows(t):
        return xp[t * 128:(t + 1) * 128, :] if t < NPT else xs_[:, :]

    wi = w_in[0].rearrange("(k p) n -> p k n", p=128)
    proj = [w[0].rearrange("(k p) n -> p k n", p=128) for w in (w_proj_a, w_proj_b, w_out)]
    wg = w_gate_e[0].rearrange("e (p k) n -> e p k n", p=128)
    wu = w_up_e[0].rearrange("e (p k) n -> e p k n", p=128)
    wd = w_down_e[0].rearrange("e (p k) n -> e p k n", p=128)

    ctx = ExitStack()
    with ctx:
        def sem(name):
            return ctx.enter_context(nc.semaphore(name))

        def alloc(stack, name, shape, dt=F32):
            return stack.enter_context(nc.sbuf_tensor(name, shape, dt))

        def sb(name, shape, dt=F32):
            return alloc(ctx, name, shape, dt)

        cst = sb("cst", [128, CSTW])
        rstd = sb("rstd", [128, NT])
        ssum = sb("ssum", [128, NT])
        msq = sb("msq", [128, NT])
        mhalf = sb("mhalf", [128, 16])
        stage = [sb(f"stage{i}", [128, CHUNK]) for i in range(2)]
        whi = [sb(f"whi{i}", [128, CHUNK], F32R) for i in range(2)]
        wlo = [sb(f"wlo{i}", [128, CHUNK], F32R) for i in range(2)]
        aTh = sb("aTh", [128, KT, T], F32R)
        aTl = sb("aTl", [128, KT, T], F32R)

        def C(name, p=128):
            o, w = OFF[name]
            return cst[0:p, o:o + w]

        s1 = ExitStack()
        with s1:
            a1 = lambda n, s, dt=F32: alloc(s1, n, s, dt)
            qT = a1("qT", [128, 2, T])
            kT = a1("kT", [128, 2, T])
            v1 = a1("v1", [128, NT, MD + 1])
            identb = a1("identb", [128, 128], BF16)
            mcausb = a1("mcausb", [128, 128], BF16)
            msampb = a1("msampb", [TS, TS], BF16)
            ones4 = a1("ones4", [MH, 128])
            gcol = a1("gcol", [128, NT, 128])
            hcol = a1("hcol", [128, NT, 4])
            wcb = a1("wcb", [128, 2 * NB])
            nmrow = a1("nmrow", [MH, T + 2 * NB])
            nmh = a1("nmh", [MH, T + 2 * NB])
            Ce = a1("Ce", [128, 2, MD + 1])
            ex = [a1(f"ex{i}", [128, 128]) for i in range(2)]
            stm = [a1(f"stm{i}", [128, 128]) for i in range(2)]
            kw = [a1(f"kw{i}", [128, MD]) for i in range(2)]
            t1 = a1("t1", [128, MD + 1])
            qTm = a1("qTm", [128, 2, NB, TS])
            wsb = a1("wsb", [TS, NB])
            pst = a1("pst", [128, 8, NT])
            zo = [a1(f"zo{i}", [128, CW]) for i in range(2)]
            zo_j = a1("zo_j", [128, MD])
            mout = a1("mout", [MH, 1 + NB])
            bif = a1("bif", [MH, 2])
            sa = ExitStack()
            with sa:
                xt = [alloc(sa, f"xt{i}", [128, D]) for i in range(NX)]
                xn = [alloc(sa, f"xn{i}", [128, D]) for i in range(2)]
                gB = alloc(sa, "gB", [128, D])
                wif = alloc(sa, "wif", [128, KT, 36])
                wifh = alloc(sa, "wifh", [128, KT, 36], F32R)
                wifl = alloc(sa, "wifl", [128, KT, 36], F32R)
            sg = ExitStack()
            with sg:
                gi = alloc(sg, "gi", [MH, T])
                gf = alloc(sg, "gf", [MH, T])
                g1 = alloc(sg, "g1", [MH, T])
                g2 = alloc(sg, "g2", [MH, T])
                gM = alloc(sg, "gM", [MH, T])
                rowc = alloc(sg, "rowc", [MH, 2, T])
                mpre = alloc(sg, "mpre", [MH, 2, NB])
                gq = alloc(sg, "gq", [128, T])
            sc_ = ExitStack()
            with sc_:
                nd = alloc(sc_, "nd", [128, NT, MD + 1])
                sC = alloc(sc_, "sC", [128, NB, 2, MD + 1])
                kwb = alloc(sc_, "kwb", [TS, NB, MD])
        s2 = ExitStack()
        with s2:
            a2 = lambda n, s, dt=F32: alloc(s2, n, s, dt)
            X = [a2(f"X{i}", [128, 1536]) for i in range(2)]
            Vw = [a2(f"Vw{i}", [128, 256]) for i in range(2)]
            qTs = a2("qTs", [128, 8, 128])
            kTs = [a2(f"kTs{i}", [128, 2, 128]) for i in range(2)]
            mcur = a2("mcur", [128, 256])
            go = [a2(f"go{i}", [128, NC]) for i in range(2)]
            a2("pad2", [128, 6 * D - 2 * 1536 - 2 * 256 - 1024 - 512 - 256 - 2 * NC])
            mx = a2("mx", [128, 16])
            nmx = a2("nmx", [128, 16])
            sdf = a2("sdf", [128, 16])
            es = a2("es", [128, 16])
            den = a2("den", [128, 16])
            rden = a2("rden", [128, 16])
            sinks = a2("sinks", [128, 16])
            sinkc = a2("sinkc", [128, 1])
            rp = a2("rp", [128, 4, 20, 8])
            Xs = a2("Xs", [TS, 1536])
            smask = a2("smask", [128, 4, SMW])
            kc = a2("kc", [128, NB, 256])
            vc = a2("vc", [128, NB, 256])
            kTc = a2("kTc", [128, 2, NB, 128])
            qsT = a2("qsT", [128, 2, 4, 4, 8])
            kTn = a2("kTn", [128, 2, TS])
            s2a = ExitStack()
            with s2a:
                Sm = [alloc(s2a, f"Sm{i}", [128, 2, 256]) for i in range(2)]
                Pm = [alloc(s2a, f"Pm{i}", [128, 2, 256]) for i in range(2)]
                PTs = [alloc(s2a, f"PTs{i}", [128, 4, 128]) for i in range(2)]
                ot = [alloc(s2a, f"ot{i}", [128, D]) for i in range(2)]
            s2b = ExitStack()
            with s2b:
                sSm = alloc(s2b, "sSm", [128, 4, SMW])
                sP = alloc(s2b, "sP", [128, 4, SMW])
                sPT = alloc(s2b, "sPT", [128, 4, 3, 128])
                so = alloc(s2b, "so", [128, 4, AD])
        s3 = ExitStack()
        with s3:
            a3 = lambda n, s, dt=F32: alloc(s3, n, s, dt)
            s3b = ExitStack()
            with s3b:
                b3 = lambda n, s, dt=F32: alloc(s3b, n, s, dt)
                b3("pad3", [128, 2 * NBLK + 4 * NT + 2 * NOVER + 32])
                tng = b3("tng", [128, D])
                tt = [b3(f"tt{i}", [128, D]) for i in range(2 * NX)]
                tin, tmo = tt[0::2], tt[1::2]
                mixT = b3("mixT", [128, KT, T])
                sgt = [b3(f"sgt{i}", [128, T]) for i in range(2)]
                tmp3 = b3("tmp3", [128, NC])
        s4 = ExitStack()
        with s4:
            a4 = lambda n, s, dt=F32: alloc(s4, n, s, dt)
            idx = a4("idx", [128, 2, NBLK], I32)
            slot = a4("slot", [128, 2, NT], I32)
            wgt = a4("wgt", [128, 2, NT])
            ovt = a4("ovt", [1, 2, NOVER], I32)
            s4a = ExitStack()
            with s4a:
                b4 = lambda n, s, dt=F32: alloc(s4a, n, s, dt)
                x2 = b4("x2", [128, NT, D])
                s4n = ExitStack()
                with s4n:
                    gF = alloc(s4n, "gF", [128, D])
                    h2 = [alloc(s4n, f"h2{i}", [128, D]) for i in range(2)]
                OR = b4("OR", [128, 2 * NT, 128])
                emp = b4("emp", [128, 2, NBLK])
                cmp8 = b4("cmp8", [128, NE, 8])
                b4("rest", [128, 3 * D - 2 * NT * 128 - 2 * NBLK - 8 * NE])
                h2T = [b4(f"h2T{i}", [128, KT, 128]) for i in range(2)]
                wr = b4("wr", [128, KT, 128])
                rb = b4("rb", [128, 36])
                LG = b4("LG", [128, NT, 8])
                LE = b4("LE", [128, NT, NE])
                m8 = b4("m8", [128, NT, 8])
                i8 = b4("i8", [128, NT, 8], U32)
                v8 = b4("v8", [128, NT, 8])
                j8 = b4("j8", [128, NT, 8], U32)
                r1 = b4("r1", [128, 16, NT])
                gmk = b4("gmk", [128, NT, NGRP])
                ee = b4("ee", [128, 2, NT])
                smk = b4("smk", [128, NE, NT])
                Ae = b4("Ae", [128, NE, NT])
                cum = b4("cum", [128, NE, NT])
                O = b4("O", [128, 2, NT, NE])
                A = b4("A", [128, NT, NE])
                Ac = b4("Ac", [128, NT + 1, NE])
                R = b4("R", [128, NT + 1, NE])
                RO = b4("RO", [128, 2, NT, NE])
                onesf = b4("onesf", [128, 128])
                cnt = b4("cnt", [128, 4, NE])
                thr = b4("thr", [128, 8])
                cmpq = b4("cmpq", [128, 2 * NT, 8])
                ge = b4("ge", [128, NT, NGRP])
                sl = b4("sl", [128, 8, 2 * NT])
                ovf = b4("ovf", [1, 2, NOVER])
                cmp = b4("cmp", [1, NOVER, NE])
                OB = b4("OB", [128, 2 * NT, 2, NBLK])
                big = b4("big", [128, 1])
            s4b = ExitStack()
            with s4b:
                c4 = lambda n, s, dt=F32: alloc(s4b, n, s, dt)
                stg = stage + [c4(f"stg{i}", [128, CHUNK]) for i in range(4)]
                xg = [c4(f"xg{i}", [128, D]) for i in range(2)]
                xh = [c4(f"xh{i}", [128, KT, 128], F32R) for i in range(2)]
                xl = [c4(f"xl{i}", [128, KT, 128], F32R) for i in range(2)]
                ixs = [c4(f"ixs{i}", [128, 1], I32) for i in range(2)]
                dxs = [c4(f"dxs{i}", [128, 1], I32) for i in range(2)]
                sg_ = c4("sg_", [128, FF])
                hh = c4("hh", [128, FF])
                hTh = c4("hTh", [128, 2, 128], F32R)
                hTl = c4("hTl", [128, 2, 128], F32R)
                yo = [c4(f"yo{i}", [128, D]) for i in range(2)]
                xr = [c4(f"xr{i}", [128, D]) for i in range(NX)]
            s4c = ExitStack()
            with s4c:
                d4 = lambda n, s, dt=F32: alloc(s4c, n, s, dt)
                gE = d4("gE", [128, D])
                y1 = [d4(f"y1{i}", [128, D]) for i in range(NX)]
                y2 = [d4(f"y2{i}", [128, D]) for i in range(NX)]

        fh = aTh[:, :, :].rearrange("p k t -> p (k t)")
        fl = aTl[:, :, :].rearrange("p k t -> p (k t)")
        WH = [w[:, :] for w in whi] + [fh[:, i * CHUNK:(i + 1) * CHUNK] for i in range(4)]
        WL = [w[:, :] for w in wlo] + [fl[:, i * CHUNK:(i + 1) * CHUNK] for i in range(4)]

        pb = [ctx.enter_context(nc.psum_tensor(f"pb{i}", [128, 512], F32)) for i in range(4)]
        pw = ctx.enter_context(nc.psum_tensor("pw", [128, 2, 512], F32))
        pq = ctx.enter_context(nc.psum_tensor("pq", [128, 2, 512], F32))
        ZB = [pb[0], pb[1]]
        AB = [pb[2], pb[3]]
        XB = [[pb[0][:, :], pb[1][:, :]], [pb[2][:, :], pb[3][:, :]], [pw[:, 0, :], pw[:, 1, :]]]
        squares = pq[:, :, :].rearrange("p a n -> p (a n)")
        BK = [pb[0], pb[1], pb[2], pb[3], pw[:, 0, :], pw[:, 1, :], pq[:, 0, :], pq[:, 1, :]]

        ld_c = sem("ld_c")
        ld_g = sem("ld_g")
        ld_k = sem("ld_k")
        ld_x = [sem(f"ld_x{i}") for i in range(NX)]
        ld_w = [sem(f"ld_w{i}") for i in range(6)]
        carry = [sem(f"carry_{e}") for e in ("pe", "dve", "pool")]
        init_v = sem("init_v")
        x_sq = sem("x_sq")
        x_ms = sem("x_ms")
        x_rs = sem("x_rs")
        x_n = sem("x_n")
        x_t = sem("x_t")
        x_hi = sem("x_hi")
        x_lo = sem("x_lo")
        w_hi = sem("w_hi")
        w_lo = sem("w_lo")
        w_use = sem("w_use")
        z_mm = sem("z_mm")
        z_ev = sem("z_ev")
        z_st = [sem(f"z_st{i}") for i in range(2)]
        gw_h = sem("gw_h")
        gw_l = sem("gw_l")
        gv_s = sem("gv_s")
        gi_r = sem("gi_r")
        gv_r = sem("gv_r")
        gq_t = sem("gq_t")
        gq_c = sem("gq_c")
        h_set = sem("h_set")
        h_wc = sem("h_wc")
        m_s1 = sem("m_s1")
        m_ex = sem("m_ex")
        m_kw = sem("m_kw")
        m_st = sem("m_st")
        m_qc = sem("m_qc")
        m_nu = sem("m_nu")
        m_t1 = sem("m_t1")
        m_nd = sem("m_nd")
        m_cu = sem("m_cu")
        m_ce = sem("m_ce")
        m_qm = sem("m_qm")
        m_kb = sem("m_kb")
        ld_s = sem("ld_s")
        u_cu = sem("u_cu")
        u_sc = sem("u_sc")
        st_s = sem("st_s")
        st_pc = sem("st_pc")
        hp_a = sem("hp_a")
        hp_m = sem("hp_m")
        hp_r = sem("hp_r")
        hp_o = sem("hp_o")
        st_hm = sem("st_hm")
        st_m = sem("st_m")
        o_cp = sem("o_cp")
        ld_X = [sem(f"ld_X{i}") for i in range(2)]
        ld_a = sem("ld_a")
        ld_b = sem("ld_b")
        X_ro = sem("X_ro")
        X_tr = sem("X_tr")
        X_ev = sem("X_ev")
        a_s = sem("a_s")
        a_m = sem("a_m")
        a_e = sem("a_e")
        a_pt = sem("a_pt")
        a_pc = sem("a_pc")
        a_pv = sem("a_pv")
        a_es = sem("a_es")
        a_oe = sem("a_oe")
        st_o = [sem(f"st_o{i}") for i in range(2)]
        zg_st = [sem(f"zg_st{i}") for i in range(2)]
        b_tr = sem("b_tr")
        b_v = sem("b_v")
        b_a = sem("b_a")
        st_k = sem("st_k")
        ld_t = [sem(f"ld_t{i}") for i in range(NX)]
        ld_n = sem("ld_n")
        f_sg = sem("f_sg")
        f_gn = sem("f_gn")
        f_mu = sem("f_mu")
        f_tr = sem("f_tr")
        f_hi = sem("f_hi")
        f_lo = sem("f_lo")
        ld_q = [sem(f"ld_q{i}") for i in range(2)]
        q_sg = sem("q_sg")
        q_mm = sem("q_mm")
        q_ev = sem("q_ev")
        mx_hi = sem("mx_hi")
        mx_lo = sem("mx_lo")
        ld_x2 = sem("ld_xs")
        ld_r = sem("ld_r")
        o_mm = sem("o_mm")
        o_ev = sem("o_ev")
        n_sq = sem("n_sq")
        n_ms = sem("n_ms")
        n_rs = sem("n_rs")
        n_h = sem("n_h")
        st_h = [sem(f"st_h{i}") for i in range(2)]
        n_tr = sem("n_tr")
        n_tc = sem("n_tc")
        n_lg = sem("n_lg")
        n_lc = sem("n_lc")
        init_r = sem("init_r")
        r_v = sem("r_v")
        r_a = sem("r_a")
        r_p = sem("r_p")
        st_x = sem("st_x")
        e_ix = sem("e_ix")
        m_end = sem("m_end")
        e_dx = sem("e_dx")
        e_x = [sem(f"e_x{i}") for i in range(2)]
        e_xt = sem("e_xt")
        e_xh = sem("e_xh")
        e_xl = sem("e_xl")
        e_gu = sem("e_gu")
        e_sg = sem("e_sg")
        e_hh = sem("e_hh")
        e_ht = sem("e_ht")
        e_hi = sem("e_hi")
        e_lo = sem("e_lo")
        e_y = sem("e_y")
        e_yc = sem("e_yc")
        st_y = [sem(f"st_y{i}") for i in range(2)]
        f_y = [sem(f"f_y{i}") for i in range(NX)]
        f_a = sem("f_a")
        f_o = sem("f_o")
        st_f = [sem(f"st_f{i}") for i in range(NX)]

        block = ctx.enter_context(nc.Block())

        def stat(eng, *steps):
            for s in steps[:-1]:
                s()
                eng.drain()
            return steps[-1]()

        AHEAD = 2

        def M(h, c):
            return h * NT + (c + 1 + AHEAD)

        def K(h, c):
            return h * NPT + (c + 1 + AHEAD)

        def W(n):
            return n + (1 + AHEAD)

        def prev(c):
            return c - 2 if c >= 2 else -1

        def AP_(i, b, u):
            return i * 16 + (8 * b + u + 1 + AHEAD)

        def OE(i, b, g):
            return i * 8 + (4 * b + g + 1 + AG)

        def BL(i, b):
            return i * 2 + (b + 1 + AHEAD)

        def tok(t):
            return slice(t * 128, t * 128 + rows(t))

        Z0_D, Z1_D = 16 * (5 * MH + 1), 16 * (4 * MH + 1)
        Z_END = [Z0_D + 16 * 27, Z1_D + 16 * 27]

        def zst_h(h, j):
            return h * (16 * (5 if j % 2 == 0 else 4)) + 16 * (j // 2 + 1)


        def LDT(n):
            return sum(32 if m < NT else 16 for m in range(n % NX, n + 1, NX))

        def LXF(t):
            return 16 * ((NT - 1 - t % NX) // NX + 1) + 16 * (t // NX + 1)

        def LX2(t):
            if t < 2:
                return ld_q[0], 16 * KT + 32
            if t < 5:
                return ld_q[1], 16 * KT + 48
            return ld_x2, 16 * (NT - 5)

        def E(e):
            return e + (1 + AHEAD)

        R_END = 4

        def LW(par, k, m):
            return k * 16 + (16 + (16 * (N_MOE // 2) if 3 * par + m < 2 else 0))
        @block.sync
        def _(sp):
            def weights(base, src, i=None, per=0):
                n = base if i is None else i * per + base
                sp.wait_ge(w_lo, W(n - 2))
                sp.dma_start(stage[base % 2][:, :].rearrange("p (k n) -> p k n", n=CW),
                             src).then_inc(ld_w[base % 2], 16)

            def cols(w, c):
                return w[:, :, c:c + CW] if isinstance(c, int) else w[:, :, bass.ds(c, CW)]

            for t in range(NT):
                if t >= NX:
                    sp.wait_ge(x_n, t - NX + 1)
                sp.dma_start(xt[t % NX][0:rows(t), :], xrows(t)).then_inc(ld_x[t % NX], 16)
                if t == 0:
                    sp.dma_start(gB[:, :], norm_mix.to_broadcast([128, D])).then_inc(ld_c, 16)
                    sp.dma_start(cst[:, :], cst_d).then_inc(ld_c, 16)
                if t == 1:
                    sp.wait_ge(init_v, 1)
                    with nc.allow_non_contiguous_dma(reason="eight columns"):
                        sp.dma_start(wif[:, :, 0:4], wi[:, :, C_IF:C_IF + 4]).then_inc(ld_g, 16)
                        sp.dma_start(wif[:, :, 32:36], wi[:, :, C_IF + 4:C_IF + 8]).then_inc(ld_g, 16)
                        for g in range(2):
                            sp.dma_start(bif[:, g:g + 1], b_if[:, g * MH:(g + 1) * MH].rearrange(
                                "o h -> h o")).then_inc(ld_g, 16)
            with sp.Fori(0, MH) as h:
                weights(0, cols(wi, h * CW + C_MQ), h, 4)
                weights(1, cols(wi, h * CW + C_MK), h, 4)
                weights(2, cols(wi, h * CW + C_MV), h, 4)
                sp.wait_ge(gq_c, NT)
                sp.wait_ge(st_s, h * (10 * 16) + 16)
                for b in range(NB):
                    sp.dma_start(sC[:, b, :, 0:MD], state_C[0, b, bass.ds(h, 1)].rearrange(
                        "o (c p) e -> p (o c) e", p=128)).then_inc(ld_s, 16)
                with nc.allow_non_contiguous_dma(reason="a column of the state"):
                    for c in range(2):
                        sp.dma_start(sC[:, :, c, MD:MD + 1],
                                     state_n[0, :, bass.ds(h, 1), c * 128:(c + 1) * 128].rearrange(
                                         "b o p -> p b o")).then_inc(ld_s, 16)
                weights(3, cols(wi, h * CW + C_AQ), h, 4)
            for j in range(2):
                weights(N_D + j, cols(wi, C_AK + j * CW))
            for j in range(4):
                weights(N_D + 2 + j, cols(wi, C_MO + j * CW))
            weights(N_G, cols(wi, C_GA))
            weights(N_G + 1, cols(wi, C_GB))
            sp.wait_ge(st_hm, MH * 32 + 16)
            sp.wait_ge(st_pc, MH * 32 + 16)
            sp.wait_ge(st_s, MH * 160 + 16)
            sp.wait_ge(st_m, 32)
            for i in range(2):
                sp.wait_ge(z_st[i], (Z0_D, Z1_D)[i] + 16 * 9)
            sp.dma_start(sinks[:, :], attn_sinks.to_broadcast([128, AH])).then_inc(ld_a, 16)

            def qkv(dst, src, sem_):
                for g in range(AG):
                    sp.dma_start(dst[:, g // 2 * 512:(g // 2 + 1) * 512].rearrange(
                        "p (j a d) -> p a j d", j=4, a=2)[:, g % 2], src[:, g * 256:(g + 1) * 256].rearrange(
                        "p (j d) -> p j d", j=4)).then_inc(sem_, 16)
                sp.dma_start(dst[:, ZK:ZO], src[:, ZK:ZO]).then_inc(sem_, 16)

            for i in range(4):
                for b in range(2):
                    sp.wait_ge(X_tr, BL(i, b - 2))
                    qkv(X[b], zt_d[tok(2 * i + b), :], ld_X[b])
                    if i == 1 and b == 0:
                        for k in range(2):
                            sp.wait_ge(z_st[k], Z_END[k])
                        sp.dma_start(sinkc[:, :], attn_sinks[0].unsqueeze(1).to_broadcast([AH, 8]).unsqueeze(2)
                                     ).then_inc(ld_b, 16)
                        sp.dma_start(smask[:, :, :], smask_d).then_inc(ld_b, 16)
                        for cache, dst in ((cache_k, kc), (cache_v, vc)):
                            sp.dma_start(dst[:, :, :], cache[0].rearrange("b w g d -> w b (g d)")).then_inc(ld_b, 16)
                        qkv(Xs, zt_d[TP:T, :], ld_b)
                    if i == 1 and b == 1:
                        for a, o in ((cache_k, s_k), (cache_v, s_v)):
                            sp.dma_start(o[0, :, 0:WIN - DS], a[0, :, DS:WIN]).then_inc(o_cp, 16)
                    nxt = cols(wi, (C_GA, C_GB)[b] + (i + 1) * CW) if i < 3 else cols(proj[0], b * CW)
                    weights(N_G + 2 * (i + 1) + b, nxt)
            def attention_over():
                sp.wait_ge(st_k, 16 * 6)
                for b in range(2):
                    sp.wait_ge(st_o[b], 16 * 5)
                sp.wait_ge(o_cp, 32)

            sp.wait_ge(a_pv, AP_(3, 1, 7))
            sp.wait_ge(st_pc, MH * 32 + 48)
            for b in range(2):
                sp.wait_ge(zg_st[b], 16 * 25)
            sp.dma_start(tng[:, :], mlstm_norm.to_broadcast([128, D])).then_inc(ld_n, 16)
            for n in range(2 * NT):
                if n == 2:
                    attention_over()
                p, t = divmod(n, NT)
                if n >= NX:
                    sp.wait_ge(f_tr, n - NX + 1)
                sp.dma_start(tin[n % NX][0:rows(t), :], (hm_d, o_d)[p][tok(t), :]).then_inc(ld_t[n % NX], 16)
                if p == 0:
                    sp.dma_start(tmo[n % NX][0:rows(t), :], zt_d[tok(t), ZO:ZO + D]
                                 ).then_inc(ld_t[n % NX], 16)
                if t == NT - 1:
                    for k in range(KT):
                        r = KT * p + k
                        if r >= 2:
                            sp.wait_ge(q_ev, 3 * (r - 1))
                        sp.dma_start(sgt[r % 2][:, :], zg_d[r * 128:(r + 1) * 128, :]).then_inc(ld_q[r % 2], 16)
                        if k % 2 == 1:
                            c = k // 2 + 2
                            weights(N_PA + 4 * p + c, cols(proj[p + c // 4], (c % 4) * CW))
            sp.wait_ge(f_tr, 2 * NT)
            sp.wait_ge(q_sg, 2 * KT)
            for t in range(NT):
                sp.dma_start(x2[0:rows(t), t, :], xrows(t)).then_inc(LX2(t)[0], 16)
            sp.wait_ge(mx_lo, NT)
            sp.dma_start(gF[:, :], norm_ffn.to_broadcast([128, D])).then_inc(ld_r, 16)
            sp.wait_ge(init_r, 1)
            with nc.allow_non_contiguous_dma(reason="36 columns"):
                sp.dma_start(wr[:, :, 0:NGRP], w_group[0].rearrange("(k p) n -> p k n", p=128)).then_inc(ld_r, 16)
                sp.dma_start(wr[:, :, NGRP:NGRP + NE], w_router[0].rearrange("(k p) n -> p k n", p=128)).then_inc(ld_r, 16)
            sp.dma_start(rb[:, 0:NGRP], b_group.to_broadcast([128, NGRP])).then_inc(ld_r, 16)
            sp.dma_start(rb[:, NGRP:NGRP + NE], b_router.to_broadcast([128, NE])).then_inc(ld_r, 16)
            for c in range(2, 4):
                weights(N_WO + c, cols(proj[2], c * CW))
            weights(N_MOE, wg[0])
            weights(N_MOE + 1, wu[0])
            for t in range(NT):
                sp.wait_ge(o_ev, 3 * NT + t + 1)
                sp.dma_start(x2_d[tok(t), :], x2[0:rows(t), t, :]).then_inc(st_x, 16)
            def expert_weights(e, par, n, back, ms=range(3)):
                for m in ms:
                    s = 3 * par + m
                    w = (wg, wu, wd)[m]
                    src = w[e] if isinstance(e, int) else w[bass.ds(e, 1)].rearrange("o p k n -> p (o k) n")
                    sp.wait_ge(w_lo, W(n + (m - back)))
                    sp.dma_start(stg[s][:, :].rearrange("p (k n) -> p k n", k=KT if m < 2 else 2), src
                                 ).then_inc(ld_w[s], 16)

            sp.wait_ge(r_v, R_END)
            sp.wait_ge(st_x, 16 * NT)
            for i in range(2):
                sp.wait_ge(st_h[i], 16 * ((NT + 1 - i) // 2))
            sp.wait_ge(w_lo, W(N_MOE - 1))
            expert_weights(0, 0, N_MOE, 3, ms=[2])
            sp.wait_ge(e_x[0], 16)
            with sp.Fori(0, NE // 2 - 1) as i:
                expert_weights(2 * i + 1, 1, i * 6 + (N_MOE + 3), 6)
                expert_weights(2 * i + 2, 0, i * 6 + (N_MOE + 6), 6)
            expert_weights(NE - 1, 1, N_MOE + 3 * (NE - 1), 6)
            def x_again(t):
                if t >= NX:
                    sp.wait_ge(st_f[t % NX], 16 * (t // NX))
                sp.dma_start(xr[t % NX][0:rows(t), :], x2_d[tok(t), :]).then_inc(ld_x[t % NX], 16)

            for t in range(NX):
                x_again(t)
            any_ = sp.value_load(ovt[0:1, 0, 0:1], min_val=0, max_val=1)
            with sp.If(any_ > 0):
                with sp.Fori(0, NOVER) as j:
                    used_ = sp.value_load(ovt[0:1, 0, bass.ds(j, 1)], min_val=0, max_val=1)
                    e_ = sp.value_load(ovt[0:1, 1, bass.ds(j, 1)], min_val=0, max_val=NE - 1)
                    with sp.If(used_ > 0):
                        expert_weights(e_, 0, j * 3 + (N_MOE + 3 * NE), 3)
                    with sp.Else():
                        sp.nop()
            with sp.Else():
                sp.nop()
                sp.nop()
            sp.wait_ge(m_end, 1)
            sp.dma_start(gE[:, :], norm_final.unsqueeze(0).to_broadcast([128, D])).then_inc(ld_n, 16)
            for t in range(NT):
                sp.wait_ge(f_o, t + 1)
                dst = yp[tok(t), :] if t < NPT else ys_out
                sp.dma_start(dst, xr[t % NX][0:rows(t), :]).then_inc(st_f[t % NX], 16)
                if 1 <= t <= NT - NX:
                    x_again(t + NX - 1)
            for i in range(NX):
                sp.wait_ge(st_f[i], 16 * ((NT - 1 - i) // NX + 1))

        @block.tensor
        def _(pe):
            for s in (m_s1, m_qc, m_nu, m_cu, u_cu, w_use, X_tr, a_s, a_pt, a_pv,
                      e_xt, e_gu, e_ht, e_y):
                pe.sem_inc(s, AHEAD)
            ident = C("ident")

            def three(out, lh, ll, rh, rl, first, last):
                pe.matmul(out, ll, rh, start=first, stop=False)
                pe.matmul(out, lh, rl, start=False, stop=False)
                return pe.matmul(out, lh, rh, start=False, stop=last)

            def transpose_tile(src, n, banks, width=D):
                for k in range(width // 128):
                    mm = pe.transpose(banks[k // 4][:, (k % 4) * 128:(k % 4) * 128 + n],
                                      src[0:n, k * 128:(k + 1) * 128], ident[0:n, 0:n])
                return mm

            def feature_group(slot, m, ft, nc_, bank, M_=128):
                for k in range(KT):
                    wsl = slice(k * CW + ft * 128, k * CW + ft * 128 + M_)
                    mm = three(bank[0:M_, 0:NC], whi[slot][:, wsl], wlo[slot][:, wsl],
                               aTh[:, k, nc_ * NC:(nc_ + 1) * NC], aTl[:, k, nc_ * NC:(nc_ + 1) * NC],
                               k == 0, k == KT - 1)
                return mm

            def token_group(slot, t, bank):
                n = rows(t)
                for k in range(KT):
                    wsl = slice(k * CW, (k + 1) * CW)
                    mm = three(bank[0:n, 0:CW], aTh[:, k, tok(t)], aTl[:, k, tok(t)],
                               whi[slot][:, wsl], wlo[slot][:, wsl], k == 0, k == KT - 1)
                return mm

            pe.wait_ge(ld_c, 32)
            for t in range(NT):
                pe.wait_ge(x_n, t + 1)
                if t >= 3:
                    pe.wait_ge(x_lo, t - 2)
                transpose_tile(xn[t % 2], rows(t), XB[t % 3]).then_inc(x_t, 1)
            pe.wait_ge(x_lo, NT)
            pe.wait_ge(gw_l, 1)
            for g in range(NG):
                if g >= 2:
                    pe.wait_ge(z_ev, g - 1)
                for k in range(KT):
                    mm = three(ZB[(g + 1) % 2][0:36, 0:NC], wifh[:, k, :], wifl[:, k, :],
                               aTh[:, k, g * NC:(g + 1) * NC], aTl[:, k, g * NC:(g + 1) * NC],
                               k == 0, k == KT - 1)
                mm.then_inc(z_mm, 1)

            def s1(h, c):
                n, b = rows(c), AB[c % 2]
                pe.wait_ge(m_ex, M(h, prev(c)))
                pe.wait_ge(m_st, M(h, prev(c)))
                if c < 2:
                    pe.wait_ge(m_kb, h + 1)
                pe.wait_ge(m_kw, K(h, prev(c) if c < NT - 1 else c - 2))
                for d in range(2):
                    pe.matmul(b[0:n, 0:n], kT[:, d, tok(c)], qT[:, d, tok(c)], start=(d == 0), stop=(d == 1))
                pe.matmul(b[0:n, 128:128 + n], ones4[:, 0:n], nmh[:, tok(c)], start=True, stop=False)
                mk = mcausb if c < NT - 1 else msampb
                pe.matmul(b[0:n, 128:128 + n], identb[0:n, 0:n], mk[:, :], start=False, stop=True)
                for d in range(2):
                    mm = pe.transpose(b[0:n, 256 + d * 128:384 + d * 128], kT[:, d, tok(c)], ident)
                mm.then_inc(m_s1, 1)

            def s2(h, c):
                n = rows(c)
                pe.wait_ge(m_t1, M(h, c - 1))
                qc = pq[0:n, 1, 0:MD + 1]
                if c < NT - 1:
                    pe.wait_ge(m_ce, K(h, c - 1))
                    for d in range(2):
                        mm = pe.matmul(qc, qT[:, d, tok(c)], Ce[:, d, :], start=(d == 0), stop=(d == 1))
                else:
                    pe.wait_ge(m_qm, h + 1)
                    pe.wait_ge(ld_s, h * 160 + 160)
                    for b in range(NB):
                        for d in range(2):
                            mm = pe.matmul(qc, qTm[:, d, b, :], sC[:, b, d, :],
                                           start=(b == 0 and d == 0), stop=(b == NB - 1 and d == 1))
                mm.then_inc(m_qc, 1)
                pe.wait_ge(m_nd, M(h, c - 1))
                pe.wait_ge(m_st, M(h, c))
                if c == NT - 1:
                    pe.sem_inc(carry[0], 1)
                pe.matmul(pq[0:n, 0, 0:MD + 1], stm[c % 2][0:n, 0:n], v1[0:n, c, :],
                          start=True, stop=True).then_inc(m_nu, 1)
                if c == NT - 1:
                    return
                pe.wait_ge(m_kw, K(h, c))
                pe.wait_ge(m_ce, K(h, c - 1))
                if c == 0:
                    pe.wait_ge(u_sc, K(h, -1))
                for d in range(2):
                    mm = pe.matmul(pw[:, d, 0:MD + 1], kw[c % 2][:, d * 128:(d + 1) * 128], v1[:, c, :],
                                   start=True, stop=True)
                mm.then_inc(m_cu, 1)

            def s3(h, b):
                if b == 0:
                    pe.wait_ge(m_kb, h + 2)
                    pe.wait_ge(m_ce, K(h, NPT - 1))
                pe.wait_ge(u_sc, K(h, b - 1))
                for d in range(2):
                    mm = pe.matmul(pw[:, d, 0:MD + 1], kwb[:, b, d * 128:(d + 1) * 128], v1[0:TS, NT - 1, :],
                                   start=True, stop=True)
                mm.then_inc(u_cu, 1)

            def gate_columns():
                pe.wait_ge(gv_r, 1)
                for t in range(NT):
                    if t >= 2:
                        pe.wait_ge(gq_c, t - 1)
                    pe.transpose(AB[t % 2][0:rows(t), 0:128], gq[:, tok(t)], ident).then_inc(gq_t, 1)
                pe.wait_ge(gq_c, NT)

            def head_sets(h):
                pe.wait_ge(h_set, h * 2 + 1)
                pe.wait_ge(m_t1, M(h, -1))
                pe.matmul(pq[:, 1, 0:2 * NB], ones4[:, :], nmh[:, T:T + 2 * NB], start=True, stop=True
                          ).then_inc(h_wc, 1)

            def z_wait(g0, i, per, j):
                pe.wait_ge(z_ev, i * per + (g0 + j - 1))

            def used(g, i, per):
                pe.wait_ge(z_mm, i * per + (g + 1))
                pe.sem_inc(w_use, 1)

            with pe.Fori(0, MH) as h:
                for j in range(12):
                    m, ft, n_ = j // 6, j % 6 // 3, j % 3
                    z_wait(G_M, h, 30, j)
                    if j % 6 == 0:
                        pe.wait_ge(w_lo, W(h * 4 + m))
                    mm = feature_group(m, m, ft, n_, ZB[j % 2]).then_inc(z_mm, 1)
                    if j % 6 == 5:
                        used(G_M + j, h, 30)
                with pe.If(h < 1):
                    gate_columns()
                with pe.Else():
                    pe.nop()
                head_sets(h)
                for j in range(18):
                    z_wait(G_M, h, 30, 12 + j)
                    if j % 9 == 0:
                        pe.wait_ge(w_lo, W(h * 4 + 2 + j // 9))
                    token_group(j // 9, j % 9, ZB[j % 2]).then_inc(z_mm, 1)
                    if j % 9 == 8:
                        used(G_M + 12 + j, h, 30)
                    if j <= 8:
                        s1(h, j)
                    if 1 <= j <= 8:
                        pe.wait_ge(h_set, h * 2 + 2)
                        pe.wait_ge(z_ev, h * 30 + (G_M + 12 + j))
                        s2(h, j - 1)
                    if j == 9:
                        s2(h, 8)
                    if j >= 10:
                        s3(h, j - 10)
            with pe.Fori(0, 3) as i:
                for j in range(18):
                    z_wait(G_D, i, 18, j)
                    if j % 9 == 0:
                        pe.wait_ge(w_lo, W(i * 2 + N_D + j // 9))
                    token_group(j // 9, j % 9, ZB[j % 2]).then_inc(z_mm, 1)
                    if j % 9 == 8:
                        used(G_D + j, i, 18)

            def filler(i, b, f):
                z_wait(G_G + 6 * b, i, 12, f)
                if f == 0:
                    pe.wait_ge(w_lo, W(i * 2 + (N_G + b)))
                feature_group(b, b, f // 3, f % 3, ZB[f % 2]).then_inc(z_mm, 1)
                if f == 5:
                    used(G_G + 6 * b + f, i, 12)

            def scores(i, b, u):
                g, gp, lo = u // 2, u // 4, (u // 2 % 2) * AD
                pe.wait_ge(a_m, AP_(i, b, u - 2))
                for e in range(2):
                    q = qTs[lo:lo + AD, gp * 4 + 2 * (u % 2) + e, :]
                    for half, kk in enumerate((kTs[1 - b], kTs[b])):
                        c0 = e * 256 + half * 128
                        mm = pe.matmul(pw[:, u % 2, c0:c0 + 128], q, kk[lo:lo + AD, gp, :], start=True, stop=True)
                mm.then_inc(a_s, 1)

            def probs_t(i, b, u):
                pe.wait_ge(a_e, AP_(i, b, u))
                pe.wait_ge(a_pc, AP_(i, b, u - 2))
                for e in range(2):
                    for half in range(2):
                        mm = pe.transpose(AB[u % 2][:, (2 * e + half) * 128:(2 * e + half + 1) * 128],
                                          Pm[u % 2][:, e, half * 128:(half + 1) * 128], ident)
                mm.then_inc(a_pt, 1)

            def against_v(i, b, u):
                g, gp = u // 2, u // 4
                if u % 2 == 0:
                    pe.wait_ge(a_oe, OE(i, b, g - 2))
                pe.wait_ge(a_pc, AP_(i, b, u))
                for e in range(2):
                    jj = 2 * (u % 2) + e
                    for half, vv in enumerate((Vw[1 - b], Vw[b])):
                        mm = pe.matmul(pq[:, g % 2, jj * 128:(jj + 1) * 128], PTs[u % 2][:, 2 * e + half, :],
                                       vv[:, gp * 128:(gp + 1) * 128], start=(half == 0), stop=(half == 1))
                mm.then_inc(a_pv, 1)

            with pe.Fori(0, NPT // 2) as i:
                for b in range(2):
                    filler(i, b, 0)
                    pe.wait_ge(X_ro, i * 2 + (b + 1))
                    pe.wait_ge(a_pc, AP_(i, b, -1))
                    pe.wait_ge(a_m, AP_(i, b, -1))
                    for j in range(8):
                        pe.transpose(AB[j // 4][:, (j % 4) * 128:(j % 4 + 1) * 128],
                                     X[b][:, j * 128:(j + 1) * 128], ident)
                    for j in range(2):
                        mm = pe.transpose(pw[:, 0, j * 128:(j + 1) * 128],
                                          X[b][:, ZK + j * 128:ZK + (j + 1) * 128], ident)
                    mm.then_inc(X_tr, 1)
                    filler(i, b, 1)
                    pe.wait_ge(X_ev, i * 2 + (b + 1))
                    for u in range(10):
                        if u < 8:
                            scores(i, b, u)
                        if 1 <= u <= 8:
                            probs_t(i, b, u - 1)
                        if u >= 2:
                            against_v(i, b, u - 2)
                        if u in (1, 3, 5, 7):
                            filler(i, b, 2 + u // 2)

            pe.wait_ge(ld_b, 144)
            pe.wait_ge(z_ev, G_END)
            pe.wait_ge(a_pc, AP_(3, 1, 7))
            for b in range(NB):
                for gp in range(2):
                    j = 2 * b + gp
                    mm = pe.transpose(pb[j // 4][:, (j % 4) * 128:(j % 4 + 1) * 128],
                                      kc[:, b, gp * 128:(gp + 1) * 128], ident)
            mm.then_inc(b_tr, 1)
            pe.wait_ge(b_v, 1)
            for j in range(8):
                pe.transpose(pw[:, 0, j * TS:(j + 1) * TS], Xs[:, j * 128:(j + 1) * 128], ident[0:TS, 0:TS])
            for j in range(2):
                mm = pe.transpose(pw[:, 0, (8 + j) * TS:(9 + j) * TS], Xs[:, ZK + j * 128:ZK + (j + 1) * 128],
                                  ident[0:TS, 0:TS])
            mm.then_inc(b_tr, 1)
            pe.wait_ge(b_a, 2)
            for p in range(4):
                for g in range(AG):
                    gp, lo = g // 2, (g % 2) * AD
                    q = qsT[lo:lo + AD, gp, p, :, :].rearrange("d j t -> d (j t)")
                    out = pb[p][g * 32:(g + 1) * 32, :]
                    pe.matmul(out[:, 0:2 * WIN], q, kTc[lo:lo + AD, gp, 2 * p:2 * p + 2, :].rearrange(
                        "d b w -> d (b w)"), start=True, stop=True)
                    mm = pe.matmul(out[:, 2 * WIN:SMW], q, kTn[lo:lo + AD, gp, :], start=True, stop=True)
            mm.then_inc(b_tr, 1)
            pe.wait_ge(b_a, 3)
            for p in range(4):
                for k in range(3):
                    w = (128, 128, TS)[k]
                    mm = pe.transpose(pb[p][0:w, k * 128:(k + 1) * 128], sP[:, p, k * 128:k * 128 + w], ident)
            mm.then_inc(b_tr, 1)
            pe.wait_ge(b_v, 3)
            for p in range(4):
                for g in range(AG):
                    out = pq[g * 32:(g + 1) * 32, 0, p * AD:(p + 1) * AD]
                    for k in range(3):
                        w = (128, 128, TS)[k]
                        vv = vc[:, 2 * p + k, g * AD:(g + 1) * AD] if k < 2 else Xs[:, ZV + g * AD:ZV + (g + 1) * AD]
                        mm = pe.matmul(out, sPT[0:w, p, k, g * 32:(g + 1) * 32], vv, start=(k == 0), stop=(k == 2))
            mm.then_inc(b_tr, 1)

            TB = [[pb[2], pb[3]], [pw[:, 0, :], pw[:, 1, :]]]
            pe.wait_ge(b_v, 2)
            for p in range(2):
                def transposed(t):
                    n = NT * p + t
                    if p == 0:
                        pe.wait_ge(f_mu, n + 1)
                    else:
                        pe.wait_ge(ld_t[n % NX], LDT(n))
                    if n >= 2:
                        pe.wait_ge(f_lo, n - 1)
                    transpose_tile(tin[n % NX], rows(t), TB[n % 2]).then_inc(f_tr, 1)
                for c in range(4):
                    for f in range(6):
                        q = 24 * p + 6 * c + f
                        if c == 0 and f < 3:
                            for t in (range(5), range(5, 7), range(7, 9))[f]:
                                transposed(t)
                            pe.wait_ge(f_lo, NT * p + 3 * f + 3)
                        if q >= 2:
                            pe.wait_ge(q_ev, q - 1)
                        if f == 0:
                            pe.wait_ge(w_lo, W(N_PA + 4 * p + c))
                        feature_group(c % 2, c % 2, f // 3, f % 3, ZB[q % 2]).then_inc(q_mm, 1)
                    pe.wait_ge(q_mm, 24 * p + 6 * c + 6)
                    pe.sem_inc(w_use, 1)

            pe.wait_ge(q_ev, 48)
            for c in range(4):
                for t in range(NT + 3 if c == 3 else NT):
                    q = NT * c + t
                    if t < NT:
                        if q >= 2:
                            pe.wait_ge(o_ev, q - 1)
                        if t == 0:
                            pe.wait_ge(w_lo, W(N_WO + c))
                        if c == 0:
                            pe.wait_ge(mx_lo, t + 1)
                        token_group(c % 2, t, ZB[q % 2]).then_inc(o_mm, 1)
                        if t == NT - 1:
                            pe.wait_ge(o_mm, q + 1)
                            pe.sem_inc(w_use, 1)
                    if c == 3 and 2 <= t < NT + 2:
                        u = t - 2
                        pe.wait_ge(n_h, u + 1)
                        if u >= 2:
                            pe.wait_ge(n_tc, u - 1)
                        transpose_tile(h2[u % 2], rows(u), TB[u % 2]).then_inc(n_tr, 1)
                    if c == 3 and t >= 3:
                        u = t - 3
                        if u == 0:
                            pe.wait_ge(ld_r, 80)
                        pe.wait_ge(n_tc, u + 1)
                        if u >= 2:
                            pe.wait_ge(n_lc, u - 1)
                        for k in range(KT):
                            mm = pe.matmul(pq[0:rows(u), u % 2, 0:128], h2T[u % 2][:, k, 0:rows(u)], wr[:, k, :],
                                           start=(k == 0), stop=(k == KT - 1))
                        mm.then_inc(n_lg, 1)
            pe.wait_ge(r_v, 2)
            pe.wait_ge(n_lc, NT)
            pe.matmul(pq[:, 0, 0:NT * NE], C("ustrict"), A[:, :, :].rearrange("p t e -> p (t e)"),
                      start=True, stop=False)
            pe.matmul(pq[:, 0, 0:NT * NE], onesf[:, :], Ac[:, 0:NT, :].rearrange("p t e -> p (t e)"),
                      start=False, stop=True)
            pe.matmul(pq[:, 1, 0:NE], onesf[:, :], Ac[:, NT, :], start=True, stop=True).then_inc(r_p, 1)
            pe.wait_ge(r_v, 3)
            for a in range(2 * NT):
                mm = pe.matmul(pw[:, 0, 0:2 * NBLK], OR[:, a, :], OB[:, a, :, :].rearrange("p k b -> p (k b)"), start=(a == 0), stop=(a == 2 * NT - 1))
            mm.then_inc(r_p, 1)

            pe.wait_ge(r_v, R_END)

            def transposes_x(e, par, k):
                pe.wait_ge(e_x[par], k * 16 + 16)
                pe.wait_ge(e_xl, E(e - 1))
                for k in range(KT):
                    mm = pe.transpose(TB[0][k // 4][:, (k % 4) * 128:(k % 4 + 1) * 128], xg[par][:, k:D:KT], ident)
                mm.then_inc(e_xt, 1)

            def transposes_h(e):
                pe.wait_ge(e_hh, E(e))
                pe.wait_ge(e_lo, E(e - 1))
                for k in range(2):
                    mm = pe.transpose(pb[0][:, k * 128:(k + 1) * 128], hh[:, k:FF:2], ident)
                mm.then_inc(e_ht, 1)

            def gate_or_up(e, par, m, n):
                if m == 0:
                    pe.wait_ge(e_xl, E(e))
                    pe.wait_ge(e_hh, E(e - 2))
                pe.wait_ge(w_lo, W(n + m))
                s = 3 * par + m
                for k in range(KT):
                    wsl = slice(k * CW, (k + 1) * CW)
                    mm = three(pw[:, par, m * FF:(m + 1) * FF], xh[par][:, k, :], xl[par][:, k, :],
                               WH[s][:, wsl], WL[s][:, wsl], k == 0, k == KT - 1)
                if m == 1:
                    mm.then_inc(e_gu, 1)

            def gu_used(e):
                pe.wait_ge(e_gu, E(e))
                pe.sem_inc(w_use, 2)

            def down(e, par, n):
                pe.wait_ge(e_lo, E(e))
                pe.wait_ge(w_lo, W(n + 2))
                pe.wait_ge(e_yc, E(e - 1))
                s = 3 * par + 2
                for k in range(2):
                    for half in range(2):
                        wsl = slice(k * D + half * 512, k * D + (half + 1) * 512)
                        mm = three(pq[:, half, :], hTh[:, k, :], hTl[:, k, :], WH[s][:, wsl], WL[s][:, wsl],
                                   k == 0, k == 1)
                mm.then_inc(e_y, 1)

            def down_used(e):
                pe.wait_ge(e_y, E(e))
                pe.sem_inc(w_use, 1)

            def both(e, par, k, n, last=False):
                gate_or_up(e, par, 0, n)
                transposes_h(e - 1)
                gate_or_up(e, par, 1, n)
                if not last:
                    transposes_x(e + 1, 1 - par, k + par)
                down(e - 1, 1 - par, n - 3)
                down_used(e - 1)
                gu_used(e)

            transposes_x(0, 0, 0)
            gate_or_up(0, 0, 0, N_MOE)
            gate_or_up(0, 0, 1, N_MOE)
            transposes_x(1, 1, 0)
            gu_used(0)
            with pe.Fori(0, NE // 2 - 1) as i:
                both(2 * i + 1, 1, i, i * 6 + (N_MOE + 3))
                both(2 * i + 2, 0, i + 1, i * 6 + (N_MOE + 6))
            both(NE - 1, 1, NE // 2 - 1, N_MOE + 3 * (NE - 1), last=True)
            transposes_h(NE - 1)
            down(NE - 1, 1, N_MOE + 3 * (NE - 1))
            down_used(NE - 1)
            any_ = pe.value_load(ovt[0:1, 0, 0:1], min_val=0, max_val=1)
            with pe.If(any_ > 0):
                with pe.Fori(0, NOVER) as j:
                    used_ = pe.value_load(ovt[0:1, 0, bass.ds(j, 1)], min_val=0, max_val=1)
                    with pe.If(used_ > 0):
                        n = j * 3 + (N_MOE + 3 * NE)
                        transposes_x(j + NE, 0, j + NE // 2)
                        gate_or_up(j + NE, 0, 0, n)
                        gate_or_up(j + NE, 0, 1, n)
                        gu_used(j + NE)
                        transposes_h(j + NE)
                        down(j + NE, 0, n)
                        down_used(j + NE)
                    with pe.Else():
                        pe.nop()
            with pe.Else():
                pe.nop()
                pe.nop()

        @block.scalar
        def _(act):
            for s in (m_ex, m_kw, m_t1, a_e, e_sg, e_xh, e_hi, e_yc):
                act.sem_inc(s, AHEAD)
            for s in z_st + zg_st:
                act.sem_inc(s, 16)
            act.sem_inc(hp_a, 1)

            def copy(out, in_, scale=1.0):
                return act.activation(out, in_, ACT.Copy, scale=scale)

            def split_hi(n, st, sl, lds, back=2):
                act.wait_ge(ld_w[st], lds)
                act.wait_ge(w_use, W(n - back))
                copy(WH[sl], stg[st][:, :]).then_inc(w_hi, 1)

            def lds(n, i=0, per=0):
                return i * (8 * per) + 16 * (n // 2 + 1)

            act.wait_ge(init_v, 1)
            for t in range(NT + 2):
                if t < NT:
                    act.wait_ge(ld_x[t % NX], 16 * (t // NX + 1))
                    n = rows(t)
                    if t >= 1:
                        act.wait_ge(x_sq, t)
                    act.activation(squares[0:n, :], xt[t % NX][0:n, :], ACT.Square,
                                   accum_out=ssum[0:n, t:t + 1]).then_inc(x_sq, 1)
                if t >= 2:
                    u = t - 2
                    act.wait_ge(x_t, u + 1)
                    for g in range(2):
                        i_ = copy(aTh[:, 4 * g:4 * g + 4, tok(u)],
                                  XB[u % 3][g].rearrange("p (a b) -> p a b", a=4)[:, :, 0:rows(u)])
                    i_.then_inc(x_hi, 1)
                if t == 2:
                    act.wait_ge(ld_g, 64)
                    copy(wifh[:, :, :], wif[:, :, :]).then_inc(gw_h, 1)
            split_hi(0, 0, 0, lds(0))
            for g in range(NG):
                act.wait_ge(z_mm, g + 1)
                gsl = slice(g * NC, (g + 1) * NC)
                act.activation(gi[:, gsl], ZB[(g + 1) % 2][0:4, 0:NC], ACT.Identity, bias=bif[:, 0:1])
                copy(gf[:, gsl], ZB[(g + 1) % 2][32:36, 0:NC]).then_inc(z_ev, 1)

            def gates_1():
                act.wait_ge(gv_s, 1)
                act.activation(g2[:, :], g1[:, :], ACT.Exp, scale=-1.0)
                act.drain()
                act.activation(g2[:, :], g2[:, :], ACT.Ln, bias=1.0).then_inc(gi_r, 1)

            def gates_2():
                act.wait_ge(gv_s, 2)
                act.activation(gq[32:36, :], g2[:, :], ACT.Exp)
                act.activation(gq[64:68, :], g1[:, :], ACT.Exp, scale=-1.0)
                act.activation(nmrow[:, T:T + 2 * NB], nmrow[:, T:T + 2 * NB], ACT.Exp).then_inc(gi_r, 1)
                act.wait_ge(gv_s, 3)
                act.activation(gq[96:100, :], gf[:, :], ACT.Exp).then_inc(gi_r, 1)

            def m_step(h, c):
                n, b = rows(c), AB[c % 2]
                act.wait_ge(m_s1, M(h, c))
                act.wait_ge(m_st, M(h, prev(c)))
                act.activation(ex[c % 2][0:n, 0:n], b[0:n, 128:128 + n], ACT.Exp,
                               bias=hcol[0:n, c, 0:1]).then_inc(m_ex, 1)
                if c < NT - 1:
                    act.wait_ge(m_cu, K(h, prev(c)))
                    copy(kw[c % 2][:, :], b[:, 256:512], scale=hcol[:, c, 3:4]).then_inc(m_kw, 1)

            def t1_step(h, c):
                n = rows(c)
                act.wait_ge(m_qc, M(h, c))
                act.wait_ge(m_nd, M(h, c - 1))
                copy(t1[0:n, :], pq[0:n, 1, 0:MD + 1], scale=hcol[0:n, c, 1:2]).then_inc(m_t1, 1)

            def square(h, c):
                n = rows(c)
                act.wait_ge(m_nd, M(h, c))
                act.wait_ge(hp_a, h * NT + (c + 1))
                act.activation(zo_j[0:n, 0:MD], nd[0:n, c, 0:MD], ACT.Square,
                               accum_out=pst[0:n, 0, c:c + 1]).then_inc(hp_a, 1)

            with act.Fori(0, MH) as h:
                split_hi(h * 4 + 1, 1, 1, lds(1, h, 4))
                for j in range(12):
                    m, ft, n_ = j // 6, j % 6 // 3, j % 3
                    act.wait_ge(z_mm, h * 30 + (G_M + 1 + j))
                    dst = (qT, kT)[m][:, ft, n_ * NC:(n_ + 1) * NC]
                    copy(dst, ZB[j % 2][:, 0:NC], scale=(1.0, MD ** -0.5)[m]).then_inc(z_ev, 1)
                    if j in (1, 7):
                        with act.If(h < 1):
                            (gates_1 if j == 1 else gates_2)()
                        with act.Else():
                            act.nop()
                    if j == 5:
                        split_hi(h * 4 + 2, 0, 0, lds(2, h, 4))
                split_hi(h * 4 + 3, 1, 1, lds(3, h, 4))
                for j in range(18):
                    t, n = j % 9, rows(j % 9)
                    act.wait_ge(z_mm, h * 30 + (G_M + 13 + j))
                    if j < 9:
                        copy(v1[0:n, t, 0:MD], ZB[j % 2][0:n, 0:CW]).then_inc(z_ev, 1)
                    else:
                        act.wait_ge(z_st[t % 2], zst_h(h, t))
                        copy(zo[t % 2][0:n, :], ZB[j % 2][0:n, 0:CW]).then_inc(z_ev, 1)
                    if j == 0:
                        act.wait_ge(h_set, h * 2 + 1)
                    if j <= 8:
                        m_step(h, j)
                    if 1 <= j <= 9:
                        t1_step(h, j - 1)
                    if j == 8:
                        split_hi(h * 4 + 4, 0, 0, lds(4, h, 4))
                    if j >= 9:
                        square(h, j - 9)
                        act.wait_ge(z_ev, h * 30 + (G_M + 13 + j))
                        act.dma_start(zt_d[tok(t), bass.ds(h * CW, CW)], zo[t % 2][0:n, :]).then_inc(z_st[t % 2], 16)
            with act.Fori(0, 3) as i:
                split_hi(i * 2 + (N_D + 1), 1, 1, lds(N_D + 1, i, 2))
                for j in range(18):
                    t, n = j % 9, rows(j % 9)
                    act.wait_ge(z_mm, i * 18 + (G_D + 1 + j))
                    act.wait_ge(z_st[j % 2], i * 144 + ((Z0_D, Z1_D)[j % 2] + 16 * (j // 2)))
                    copy(zo[j % 2][0:n, :], ZB[j % 2][0:n, 0:CW]).then_inc(z_ev, 1)
                    act.wait_ge(z_ev, i * 18 + (G_D + 1 + j))
                    act.dma_start(zt_d[tok(t), bass.ds(i * 512 + (ZK + (j // 9) * CW), CW)],
                                  zo[j % 2][0:n, :]).then_inc(z_st[j % 2], 16)
                    if j == 8:
                        split_hi(i * 2 + (N_D + 2), 0, 0, lds(N_D + 2, i, 2))

            def filler_out(i, b, f):
                act.wait_ge(z_mm, i * 12 + (G_G + 6 * b + f + 1))
                act.wait_ge(zg_st[f % 2], i * 96 + 16 * (3 * b + f // 2 + 1))
                copy(go[f % 2][:, :], ZB[f % 2][:, 0:NC]).then_inc(z_ev, 1)
                act.wait_ge(z_ev, i * 12 + (G_G + 6 * b + f + 1))
                act.dma_start(zg_d[bass.ds(i * CW + (b * D + (f // 3) * 128), 128),
                                   (f % 3) * NC:(f % 3 + 1) * NC], go[f % 2][:, :]).then_inc(zg_st[f % 2], 16)

            def exps(i, b, u):
                if u == 0:
                    act.wait_ge(a_oe, OE(i, b, -1))
                act.wait_ge(a_m, AP_(i, b, u))
                act.wait_ge(a_pt, AP_(i, b, u - 2))
                for e in range(2):
                    h = 2 * u + e
                    i_ = act.activation(Pm[u % 2][:, e, :], Sm[u % 2][:, e, :], ACT.Exp, bias=nmx[:, h:h + 1],
                                        accum_out=den[:, h:h + 1])
                i_.then_inc(a_e, 1)
                if u % 2 == 1:
                    g = u // 2
                    act.activation(es[:, 4 * g:4 * g + 4], sdf[:, 4 * g:4 * g + 4], ACT.Exp).then_inc(a_es, 1)

            with act.Fori(0, NPT // 2) as i:
                for b in range(2):
                    filler_out(i, b, 0)
                    act.wait_ge(X_tr, BL(i, b))
                    for gp in range(2):
                        copy(qTs[:, 4 * gp:4 * gp + 4, :], AB[gp][:, :].rearrange("p (j t) -> p j t", j=4),
                             scale=AD ** -0.5)
                    copy(kTs[b][:, :, :], pw[:, 0, 0:256].rearrange("p (j t) -> p j t", j=2)).then_inc(X_ev, 1)
                    filler_out(i, b, 1)
                    for u in range(8):
                        exps(i, b, u)
                        if u in (2, 4, 6):
                            filler_out(i, b, 1 + u // 2)
                        if u == 3:
                            split_hi(i * 2 + (N_G + b + 1), 1 - b, 1 - b, lds(N_G + b + 1, i, 2))
                    filler_out(i, b, 5)

            act.wait_ge(b_tr, 1)
            for k in range(4):
                i_ = copy(kTc[:, :, 2 * k:2 * k + 2, :].rearrange("p g b w -> p b g w"),
                          pb[k][:, :].rearrange("p (b g w) -> p b g w", b=2, g=2))
            i_.then_inc(b_a, 1)
            act.wait_ge(b_tr, 2)
            for gp in range(2):
                copy(qsT[:, gp, :, :, :].rearrange("d p j t -> d j p t"),
                     pw[:, 0, gp * 128:(gp + 1) * 128].rearrange("d (j p t) -> d j p t", j=4, p=4), scale=AD ** -0.5)
            copy(kTn[:, :, :], pw[:, 0, 256:320].rearrange("p (g t) -> p g t", g=2)).then_inc(b_a, 1)
            act.wait_ge(b_v, 2)
            for p in range(4):
                act.activation(sP[:, p, :], sSm[:, p, :], ACT.Exp, bias=nmx[:, p:p + 1], accum_out=den[:, p:p + 1])
            act.activation(es[:, 0:4], sdf[:, 0:4], ACT.Exp).then_inc(b_a, 1)

            TB = [[pb[2], pb[3]], [pw[:, 0, :], pw[:, 1, :]]]
            for p in range(2):
                split_hi(N_PA + 4 * p + 1, 1, 1, lds(N_PA + 4 * p + 1))
                for t in range(NT + 1):
                    n = NT * p + t
                    if t < NT and p == 0:
                        act.wait_ge(ld_t[n % NX], LDT(n))
                        act.activation(tmo[n % NX][0:rows(t), :], tmo[n % NX][0:rows(t), :], ACT.Sigmoid
                                       ).then_inc(f_sg, 1)
                    if t >= 1:
                        u, k = n - 1, rows(t - 1)
                        act.wait_ge(f_tr, u + 1)
                        if u == NT:
                            act.wait_ge(q_mm, 24)
                        for g in range(2):
                            i_ = copy(aTh[:, 4 * g:4 * g + 4, tok(t - 1)],
                                      TB[u % 2][g].rearrange("p (a b) -> p a b", a=4)[:, :, 0:k]
                                      if u % 2 else TB[0][g][:, :].rearrange("p (a b) -> p a b", a=4)[:, :, 0:k])
                        i_.then_inc(f_hi, 1)
                for r in range(KT * p, KT * (p + 1)):
                    act.wait_ge(ld_q[r % 2], 16 * (r // 2 + 1))
                    act.activation(sgt[r % 2][:, :], sgt[r % 2][:, :], ACT.Sigmoid).then_inc(q_sg, 1)
                    c = r % KT // 2
                    if r % 2 == 0 and c > 0:
                        n = N_PA + 4 * p + c + 1
                        split_hi(n, n % 2, n % 2, lds(n))
            act.wait_ge(q_mm, 48)
            act.wait_ge(q_ev, 48)
            for t in range(NT):
                copy(aTh[:, :, tok(t)], mixT[:, :, tok(t)]).then_inc(mx_hi, 1)

            for c in range(3):
                split_hi(N_WO + c + 1, (c + 1) % 2, (c + 1) % 2, lds(N_WO + c + 1))
            for t in range(NT + 1):
                if t < NT:
                    n = rows(t)
                    act.wait_ge(o_ev, 3 * NT + t + 1)
                    if t >= 1:
                        act.wait_ge(n_sq, t)
                    act.activation(OB[0:n, :, :, :].rearrange("p a k b -> p (a k b)")[:, 0:D], x2[0:n, t, :], ACT.Square,
                                   accum_out=ssum[0:n, t:t + 1]).then_inc(n_sq, 1)
                if t >= 1:
                    u = t - 1
                    act.wait_ge(n_tr, u + 1)
                    if u >= 2:
                        act.wait_ge(n_lg, u - 1)
                    for g in range(2):
                        bank = TB[u % 2][g] if u % 2 else TB[0][g][:, :]
                        i_ = copy(h2T[u % 2][:, 4 * g:4 * g + 4, 0:rows(u)],
                                  bank.rearrange("p (a b) -> p a b", a=4)[:, :, 0:rows(u)])
                    i_.then_inc(n_tc, 1)
            for m in range(2):
                split_hi(N_MOE + m, m, m, lds(N_MOE + m))
            act.wait_ge(r_v, 1)
            act.activation(ge[:, :, :], ge[:, :, :], ACT.Exp)
            act.activation(r1[:, 3, :], r1[:, 2, :], ACT.Exp).then_inc(r_a, 1)

            def splits_hi(par, k, n, back):
                for m in range(3):
                    split_one(par, k, n, m, back)

            def split_one(par, k, n, m, back):
                s = 3 * par + m
                act.wait_ge(ld_w[s], LW(par, k, m))
                act.wait_ge(w_use, W(n + (m - back)) if back else W(N_MOE - 1))
                copy(WH[s], stg[s][:, :]).then_inc(w_hi, 1)

            def silu(e, par):
                act.wait_ge(e_gu, E(e))
                act.activation(sg_[:, :], pw[:, par, 0:FF], ACT.Sigmoid).then_inc(e_sg, 1)

            def x_high(e, par):
                act.wait_ge(e_xt, E(e))
                for g in range(2):
                    i_ = copy(xh[par][:, 4 * g:4 * g + 4, :], TB[0][g][:, :].rearrange("p (a b) -> p a b", a=4))
                i_.then_inc(e_xh, 1)

            def h_high(e):
                act.wait_ge(e_ht, E(e))
                copy(hTh[:, :, :], pb[0][:, 0:256].rearrange("p (a b) -> p a b", a=2)).then_inc(e_hi, 1)

            def y_out(e, par, k):
                act.wait_ge(e_y, E(e))
                act.wait_ge(st_y[par], k * 16 + 16)
                copy(yo[par][:, :].rearrange("p (a n) -> p a n", a=2), pq[:, :, :]).then_inc(e_yc, 1)

            def both(e, par, k, n, last=False):
                silu(e - 1, 1 - par)
                if not last:
                    split_one(1 - par, k + par, n + 3, 0, 6)
                h_high(e - 1)
                if not last:
                    split_one(1 - par, k + par, n + 3, 1, 6)
                    x_high(e + 1, 1 - par)
                    split_one(1 - par, k + par, n + 3, 2, 6)
                y_out(e - 1, 1 - par, k + (par - 1))

            act.wait_ge(r_v, R_END)
            split_one(0, 0, N_MOE, 2, 0)
            x_high(0, 0)
            splits_hi(1, 0, N_MOE + 3, 6)
            x_high(1, 1)
            with act.Fori(0, NE // 2 - 1) as i:
                both(2 * i + 1, 1, i, i * 6 + (N_MOE + 3))
                both(2 * i + 2, 0, i + 1, i * 6 + (N_MOE + 6))
            both(NE - 1, 1, NE // 2 - 1, N_MOE + 3 * (NE - 1), last=True)
            silu(NE - 1, 1)
            h_high(NE - 1)
            y_out(NE - 1, 1, NE // 2 - 1)
            any_ = act.value_load(ovt[0:1, 0, 0:1], min_val=0, max_val=1)
            with act.If(any_ > 0):
                with act.Fori(0, NOVER) as j:
                    used_ = act.value_load(ovt[0:1, 0, bass.ds(j, 1)], min_val=0, max_val=1)
                    with act.If(used_ > 0):
                        e, k = j + NE, j + NE // 2
                        splits_hi(0, k, j * 3 + (N_MOE + 3 * NE), 3)
                        x_high(e, 0)
                        silu(e, 0)
                        h_high(e)
                        y_out(e, 0, k)
                    with act.Else():
                        act.nop()
            with act.Else():
                act.nop()
                act.nop()
            for t in range(NT):
                act.wait_ge(f_a, t + 1)
                if t >= 1:
                    act.wait_ge(n_sq, NT + t)
                act.activation(squares[0:rows(t), :], xr[t % NX][0:rows(t), :], ACT.Square,
                               accum_out=ssum[0:rows(t), t:t + 1]).then_inc(n_sq, 1)

        @block.vector
        def _(ve):
            for s in (m_st, m_nd, m_ce, u_sc, w_lo, a_m, a_pc,
                      e_xl, e_hh, e_lo):
                ve.sem_inc(s, AHEAD)
            ve.sem_inc(a_oe, AG)
            ve.sem_inc(m_kb, 1)

            def split_lo(n, st, sl):
                ve.wait_ge(w_hi, n + 1)
                ve.tensor_tensor(WL[sl], stg[st][:, :], WH[sl].bitcast(F32), ALU.subtract).then_inc(w_lo, 1)

            ve.memset(wif[:, :, :], 0.0)
            ve.memset(ssum[:, :], 1.0)
            ve.memset(mhalf[:, :], -0.5).then_inc(init_v, 1)
            ve.memset(ones4[:, :], 1.0)
            ve.memset(v1[:, :, MD:MD + 1], 1.0)
            ve.memset(gcol[:, :, :], 1.0)
            ve.memset(hcol[:, :, :], 1.0)
            ve.memset(pst[:, :, :], 0.0)
            ve.wait_ge(ld_c, 32)
            ve.tensor_copy(identb[:, :], C("ident"))
            ve.tensor_copy(mcausb[:, :], C("mcaus"))
            ve.tensor_copy(msampb[:, :], C("msamp", TS))

            def x_scale(t):
                n = rows(t)
                ve.wait_ge(x_rs, t + 1)
                if t >= 2:
                    ve.wait_ge(x_t, t - 1)
                ve.scalar_tensor_tensor(out=xn[t % 2][0:n, :], in0=xt[t % NX][0:n, :],
                                        scalar=rstd[0:n, t:t + 1], in1=gB[0:n, :],
                                        op0=ALU.mult, op1=ALU.mult).then_inc(x_n, 1)

            for t in range(NT + 3):
                if t < NT:
                    ve.wait_ge(x_sq, t + 1)
                    ve.tensor_scalar(msq[0:rows(t), t:t + 1], ssum[0:rows(t), t:t + 1], 1.0 / D, EPS,
                                     ALU.mult, ALU.add).then_inc(x_ms, 1)
                if 1 <= t <= NT:
                    x_scale(t - 1)
                if t >= 3:
                    u = t - 3
                    ve.wait_ge(x_hi, u + 1)
                    for g in range(2):
                        i_ = ve.tensor_tensor(aTl[:, 4 * g:4 * g + 4, tok(u)],
                                              XB[u % 3][g].rearrange("p (a b) -> p a b", a=4)[:, :, 0:rows(u)],
                                              aTh[:, 4 * g:4 * g + 4, tok(u)].bitcast(F32), ALU.subtract)
                    i_.then_inc(x_lo, 1)
                if t == 4:
                    ve.wait_ge(gw_h, 1)
                    ve.tensor_tensor(wifl[:, :, :], wif[:, :, :], wifh[:, :, :].bitcast(F32),
                                     ALU.subtract).then_inc(gw_l, 1)
            split_lo(0, 0, 0)

            def gates():
                seq = lambda a: a[:, TP:T].rearrange("h (b s) -> h b s", s=DS)
                chk = lambda a: a[:, 0:TP].rearrange("h (c l) -> h c l", l=128)
                ve.wait_ge(z_ev, NG)
                ve.wait_ge(ld_g, 64)
                ve.wait_ge(ld_k, 32)
                ve.tensor_scalar(gf[:, :], gf[:, :], bif[:, 1:2], None, ALU.add)
                ve.drain()
                ve.scalar_tensor_tensor(out=g1[:, :], in0=gf[:, :], scalar=-1.0, in1=gf[:, :],
                                        op0=ALU.mult, op1=ALU.max).then_inc(gv_s, 1)
                ve.memset(gq[:, :], 0.0)
                ve.wait_ge(gi_r, 1)
                ve.scalar_tensor_tensor(out=g1[:, :], in0=gf[:, :], scalar=0.0, in1=g2[:, :],
                                        op0=ALU.min, op1=ALU.subtract)
                ve.drain()
                ve.tensor_tensor_scan(gf[:, :], rowc[:, 0, :], g1[:, :], 0.0, ALU.mult, ALU.add)
                ve.drain()
                ve.tensor_tensor(gi[:, :], gi[:, :], gf[:, :], ALU.subtract)
                ve.tensor_copy(g2[:, :], rowc[:, 1, :])
                ve.drain()
                ve.tensor_copy(g1[:, :], gi[:, :])
                ve.tensor_copy(chk(g2)[:, 1:NPT, 0], chk(gf)[:, 0:NPT - 1, 127])
                ve.tensor_copy(gq[0:MH, :], gi[:, :])
                ve.drain()
                ve.tensor_tensor(seq(g1)[:, :, 0], seq(gi)[:, :, 0], mpre[:, 1, :], ALU.max)
                ve.drain()
                ve.tensor_tensor_scan(gM[:, :], g2[:, :], g1[:, :], 0.0, ALU.add, ALU.max)
                ve.drain()
                ve.tensor_tensor(g1[:, :], gf[:, :], gM[:, :], ALU.add)
                ve.tensor_scalar(nmrow[:, 0:T], gM[:, :], -1.0, None, ALU.mult)
                ve.memset(mpre[:, 0, 0:1], 0.0)
                ve.drain()
                ve.tensor_copy(mpre[:, 0, 1:NPT], chk(g1)[:, 0:NPT - 1, 127])
                ve.tensor_copy(mout[:, 0:1], g1[:, TP - 1:TP])
                ve.tensor_copy(mout[:, 1:1 + NB], seq(g1)[:, :, DS - 1])
                ve.drain()
                wc = nmrow[:, T:T + 2 * NB]
                ve.tensor_tensor(wc[:, 0:NB], mpre[:, 0, :], chk(gM)[:, :, 127], ALU.subtract)
                ve.tensor_tensor(wc[:, NB:2 * NB], mpre[:, 1, :], seq(gM)[:, :, DS - 1], ALU.subtract)
                ve.tensor_tensor(chk(g2), mpre[:, 0, :].unsqueeze(2).to_broadcast([MH, NPT, 128]),
                                 chk(gM), ALU.subtract)
                ve.tensor_tensor(seq(g2), mpre[:, 1, :].unsqueeze(2).to_broadcast([MH, NB, DS]),
                                 seq(gM), ALU.subtract).then_inc(gv_s, 1)
                ve.tensor_tensor(chk(gf), chk(gi), chk(gM)[:, :, 127:128].to_broadcast([MH, NPT, 128]),
                                 ALU.subtract)
                ve.tensor_tensor(seq(gf), seq(gi), seq(gM)[:, :, DS - 1:DS].to_broadcast([MH, NB, DS]),
                                 ALU.subtract).then_inc(gv_s, 1)

            def gate_columns():
                ve.wait_ge(gi_r, 3)
                ve.nop().then_inc(gv_r, 1)
                for t in range(NT):
                    ve.wait_ge(gq_t, t + 1)
                    ve.tensor_copy(gcol[0:rows(t), t, :], AB[t % 2][0:rows(t), 0:128]).then_inc(gq_c, 1)
                ve.drain()
                ve.memset(nd[:, NT - 1, :], 0.0)
                ve.drain()

            def head_set(h):
                ve.wait_ge(m_t1, M(h, -1))
                ve.wait_ge(hp_o, h + 1)
                ve.wait_ge(st_pc, h * 32 + 16)
                ve.tensor_scalar(nmh[:, :], nmrow[:, :], cst[0:MH, bass.ds(h + OFF["ident"][0], 1)], None,
                                 ALU.mult)
                for q in range(4):
                    i_ = ve.tensor_copy(hcol[:, :, q:q + 1], gcol[:, :, bass.ds(h + 32 * q, 1)])
                ve.drain()
                ve.tensor_scalar(wsb[:, :], C("bmk", TS), hcol[0:TS, NT - 1, 3:4], None, ALU.mult)
                ve.memset(Ce[:, :, :], 0.0).then_inc(h_set, 1)
                ve.wait_ge(h_wc, h + 1)
                ve.tensor_copy(wcb[:, :], pq[:, 1, 0:2 * NB])
                ve.drain()
                ve.nop().then_inc(h_set, 1)

            def weigh(h, c):
                n, b = rows(c), AB[c % 2]
                ve.wait_ge(m_ex, M(h, c))
                if c < NT - 1:
                    ve.wait_ge(m_kw, K(h, c))
                ve.wait_ge(m_nu, M(h, prev(c)))
                ve.tensor_tensor(stm[c % 2][0:n, 0:n], b[0:n, 0:n], ex[c % 2][0:n, 0:n], ALU.mult
                                 ).then_inc(m_st, 1)

            def numer(h, c):
                n = rows(c)
                ve.wait_ge(m_nu, M(h, c))
                ve.wait_ge(m_t1, M(h, c))
                if c == 0:
                    ve.wait_ge(st_hm, h * 32 + 16)
                ve.tensor_tensor(nd[0:n, c, :], pq[0:n, 0, 0:MD + 1], t1[0:n, :], ALU.add).then_inc(m_nd, 1)

            def state(h, c):
                ve.wait_ge(m_qc, M(h, c))
                ve.wait_ge(m_cu, K(h, c))
                ve.scalar_tensor_tensor(out=Ce[:, :, :], in0=Ce[:, :, :], scalar=wcb[:, c:c + 1],
                                        in1=pw[:, :, 0:MD + 1], op0=ALU.mult, op1=ALU.add).then_inc(m_ce, 1)

            def sample_state(h, b):
                ve.wait_ge(u_cu, K(h, b))
                ve.scalar_tensor_tensor(out=sC[:, b, :, :], in0=sC[:, b, :, :], scalar=wcb[:, NB + b:NB + b + 1],
                                        in1=pw[:, :, 0:MD + 1], op0=ALU.mult, op1=ALU.add).then_inc(u_sc, 1)

            def head_end(h):
                den, rec, ms, sc = (pst[:, k, :] for k in range(1, 5))
                ve.scalar_tensor_tensor(out=ms, in0=nd[:, :, MD], scalar=-1.0, in1=nd[:, :, MD],
                                        op0=ALU.mult, op1=ALU.max)
                ve.drain()
                ve.tensor_tensor(den, ms, hcol[:, :, 2], ALU.max)
                ve.drain()
                ve.reciprocal(rec, den)
                ve.drain()
                ve.tensor_tensor(den, rec, rec, ALU.mult)
                ve.drain()
                ve.wait_ge(hp_a, h * NT + (NT + 1))
                ve.tensor_tensor(ms, pst[:, 0, :], den, ALU.mult)
                ve.drain()
                ve.tensor_scalar(ms, ms, 1.0 / MD, EPS, ALU.mult, ALU.add).then_inc(hp_m, 1)
                ve.wait_ge(hp_r, h + 1)
                ve.tensor_tensor(sc, rec, pst[:, 5, :], ALU.mult)
                ve.drain()
                ve.tensor_tensor(nd[:, :, 0:MD], nd[:, :, 0:MD], sc.unsqueeze(2).to_broadcast([128, NT, MD]),
                                 ALU.mult).then_inc(hp_o, 1)

            ve.sem_inc(hp_o, 1)
            with ve.Fori(0, MH) as h:
                split_lo(h * 4 + 1, 1, 1)
                with ve.If(h < 1):
                    gates()
                with ve.Else():
                    ve.nop()
                split_lo(h * 4 + 2, 0, 0)
                with ve.If(h < 1):
                    gate_columns()
                with ve.Else():
                    ve.nop()
                head_set(h)
                ve.wait_ge(z_ev, h * 30 + (G_M + 12))
                for d in range(2):
                    i_ = ve.tensor_tensor(qTm[:, d, :, :], qT[:, d, TP:T].unsqueeze(1).to_broadcast([128, NB, TS]),
                                          C("bmq").rearrange("p (b t) -> p b t", b=NB), ALU.mult)
                i_.then_inc(m_qm, 1)
                split_lo(h * 4 + 3, 1, 1)
                for j in range(18):
                    if j <= 8:
                        weigh(h, j)
                    if j == 8:
                        ve.wait_ge(u_cu, K(h, -1))
                        ve.tensor_tensor(kwb[:, :, :], AB[0][0:TS, 256:512].unsqueeze(1).to_broadcast([TS, NB, MD]),
                                         wsb[:, :].unsqueeze(2).to_broadcast([TS, NB, MD]), ALU.mult
                                         ).then_inc(m_kb, 1)
                    if 1 <= j <= 9:
                        if j <= 8:
                            state(h, j - 1)
                        numer(h, j - 1)
                    if j == 8:
                        split_lo(h * 4 + 4, 0, 0)
                    if j >= 10:
                        sample_state(h, j - 10)
                head_end(h)
            with ve.Fori(0, 3) as i:
                split_lo(i * 2 + (N_D + 1), 1, 1)
                split_lo(i * 2 + (N_D + 2), 0, 0)

            def rope(x, n, cs, sn):
                xv = x[0:n, 0:1280].rearrange("p (h d) -> p h d", d=AD)
                x1, x2_ = xv[:, :, 0:8], xv[:, :, 8:16]
                cb = cs.unsqueeze(1).to_broadcast([n, 20, 8])
                sb_ = sn.unsqueeze(1).to_broadcast([n, 20, 8])
                r_ = [rp[0:n, k, :, :] for k in range(4)]
                ve.tensor_tensor(r_[0], x1, cb, ALU.mult)
                ve.tensor_tensor(r_[1], x2_, sb_, ALU.mult)
                ve.tensor_tensor(r_[2], x2_, cb, ALU.mult)
                ve.tensor_tensor(r_[3], x1, sb_, ALU.mult)
                ve.drain()
                ve.tensor_tensor(x1, r_[0], r_[1], ALU.subtract)
                return ve.tensor_tensor(x2_, r_[2], r_[3], ALU.add)

            def masked_max(i, b, u):
                ve.wait_ge(a_s, AP_(i, b, u))
                ve.wait_ge(a_e, AP_(i, b, u - 2))
                ve.sem_inc(carry[1], 1)
                for e in range(2):
                    h = 2 * u + e
                    ve.tensor_tensor_reduce(out=Sm[u % 2][:, e, :], in0=pw[:, u % 2, e * 256:(e + 1) * 256],
                                            in1=mcur[:, :] if b == 0 else C("amask"), scale=1.0,
                                            scalar=sinks[:, h:h + 1], op0=ALU.add, op1=ALU.max,
                                            accum_out=mx[:, h:h + 1])
                ve.drain()
                if u % 2 == 1:
                    hs = slice(2 * u - 2, 2 * u + 2)
                    ve.tensor_tensor(sdf[:, hs], sinks[:, hs], mx[:, hs], ALU.subtract)
                ve.tensor_scalar(nmx[:, 2 * u:2 * u + 2], mx[:, 2 * u:2 * u + 2], -1.0, None, ALU.mult
                                 ).then_inc(a_m, 1)

            def probs_copy(i, b, u):
                ve.wait_ge(a_pt, AP_(i, b, u))
                ve.wait_ge(a_pv, AP_(i, b, u - 2))
                ve.tensor_copy(PTs[u % 2][:, :, :], AB[u % 2][:, :].rearrange("p (k t) -> p k t", k=4)
                               ).then_inc(a_pc, 1)

            def outputs(i, b, g):
                ve.wait_ge(a_pv, AP_(i, b, 2 * g + 1))
                ve.wait_ge(a_es, i * 8 + (4 * b + g + 1))
                if g == 0:
                    ve.wait_ge(st_o[b], i * 16 + 16)
                hs = slice(4 * g, 4 * g + 4)
                ve.tensor_tensor(rden[:, hs], den[:, hs], es[:, hs], ALU.add)
                ve.drain()
                ve.reciprocal(rden[:, hs], rden[:, hs])
                ve.drain()
                lo = (g % 2) * AD
                ve.tensor_tensor(ot[b][:, g * 256:(g + 1) * 256].rearrange("p (j d) -> p j d", j=4),
                                 pq[:, g % 2, :].rearrange("p (j d) -> p j d", j=4)[:, :, lo:lo + AD],
                                 rden[:, hs].unsqueeze(2).to_broadcast([128, 4, AD]), ALU.mult).then_inc(a_oe, 1)

            def rotate_block(i, b):
                ve.wait_ge(ld_X[b], i * 80 + 80)
                ve.wait_ge(a_pv, AP_(i, b, -1))
                ve.tensor_copy(Vw[b][:, :], X[b][:, ZV:ZV + 256])
                tab = lambda name: cst[:, bass.ds(i * 16 + (OFF[name][0] + 8 * b), 8)]
                rope(X[b], 128, tab("cos"), tab("sin")).then_inc(X_ro, 1)

            ve.wait_ge(ld_a, 16)
            ve.tensor_copy(mcur[:, :], C("amask0"))
            ve.memset(kTs[1][:, :, :], 0.0)
            ve.memset(Vw[1][:, :], 0.0)
            ve.drain()
            with ve.Fori(0, NPT // 2) as i:
                for b in range(2):
                    rotate_block(i, b)
                    for u in range(10):
                        if u < 8:
                            masked_max(i, b, u)
                        if 1 <= u <= 8:
                            probs_copy(i, b, u - 1)
                        if u >= 2 and u % 2 == 1:
                            outputs(i, b, (u - 2) // 2)
                        if u == 4:
                            split_lo(i * 2 + (N_G + b + 1), 1 - b, 1 - b)
                    if b == 0:
                        ve.drain()
                        ve.tensor_copy(mcur[:, :], C("amask"))

            ve.wait_ge(ld_b, 144)
            co = OFF["cos"][0] + 8 * NPT
            sn_ = OFF["sin"][0] + 8 * NPT
            rope(Xs, TS, cst[0:TS, co:co + 8], cst[0:TS, sn_:sn_ + 8]).then_inc(b_v, 1)
            for i in range(2):
                ve.wait_ge(st_o[i], 16 * 5)
            ve.wait_ge(b_tr, 3)
            for p in range(4):
                ve.tensor_tensor_reduce(out=sSm[:, p, :], in0=pb[p][:, 0:SMW], in1=smask[:, p, :], scale=1.0,
                                        scalar=sinkc[:, 0:1], op0=ALU.add, op1=ALU.max, accum_out=mx[:, p:p + 1])
            ve.drain()
            ve.tensor_scalar(sdf[:, 0:4], mx[:, 0:4], -1.0, sinkc[:, 0:1], ALU.mult, ALU.add)
            ve.tensor_scalar(nmx[:, 0:4], mx[:, 0:4], -1.0, None, ALU.mult).then_inc(b_v, 1)
            ve.wait_ge(b_tr, 4)
            for p in range(4):
                ve.tensor_copy(sPT[:, p, 0:2, :], pb[p][:, 0:256].rearrange("p (k t) -> p k t", k=2))
                i_ = ve.tensor_copy(sPT[0:TS, p, 2, :], pb[p][0:TS, 256:384])
            i_.then_inc(b_v, 1)
            ve.wait_ge(b_a, 3)
            ve.tensor_tensor(rden[:, 0:4], den[:, 0:4], es[:, 0:4], ALU.add)
            ve.drain()
            ve.reciprocal(rden[:, 0:4], rden[:, 0:4])
            ve.wait_ge(b_tr, 5)
            ve.drain()
            ve.tensor_tensor(so[:, :, :], pq[:, 0, 0:256].rearrange("p (k d) -> p k d", k=4),
                             rden[:, 0:4].unsqueeze(2).to_broadcast([128, 4, AD]), ALU.mult).then_inc(b_v, 1)

            TB = [[pb[2], pb[3]], [pw[:, 0, :], pw[:, 1, :]]]

            def gated(t):
                k, x = rows(t), tin[t % NX]
                ve.wait_ge(f_gn, t + 1)
                ve.wait_ge(f_sg, t + 1)
                ve.tensor_tensor(x[0:k, :], x[0:k, :], tmo[t % NX][0:k, :], ALU.mult).then_inc(f_mu, 1)

            for p in range(2):
                split_lo(N_PA + 4 * p + 1, 1, 1)
                for t in range(NT + 1):
                    n = NT * p + t
                    if t < NT and p == 0:
                        gated(t)
                    if t >= 1:
                        u, k = n - 1, rows(t - 1)
                        ve.wait_ge(f_hi, u + 1)
                        for g in range(2):
                            bank = TB[u % 2][g] if u % 2 else TB[0][g][:, :]
                            i_ = ve.tensor_tensor(aTl[:, 4 * g:4 * g + 4, tok(t - 1)],
                                                  bank.rearrange("p (a b) -> p a b", a=4)[:, :, 0:k],
                                                  aTh[:, 4 * g:4 * g + 4, tok(t - 1)].bitcast(F32), ALU.subtract)
                        i_.then_inc(f_lo, 1)
                for c in range(4):
                    for f in range(6):
                        q, r = 24 * p + 6 * c + f, KT * p + 2 * c + f // 3
                        cols_ = slice((f % 3) * NC, (f % 3 + 1) * NC)
                        m_, s_ = mixT[:, 2 * c + f // 3, cols_], sgt[r % 2][:, cols_]
                        ve.wait_ge(q_sg, r + 1)
                        ve.wait_ge(q_mm, q + 1)
                        if p == 0:
                            ve.tensor_tensor(m_, ZB[q % 2][:, 0:NC], s_, ALU.mult).then_inc(q_ev, 1)
                        else:
                            ve.wait_ge(q_ev, q)
                            ve.tensor_tensor(tmp3[:, :], ZB[q % 2][:, 0:NC], s_, ALU.mult)
                            ve.drain()
                            ve.tensor_tensor(m_, m_, tmp3[:, :], ALU.add).then_inc(q_ev, 1)
                        if f == 1 and c > 0:
                            n = N_PA + 4 * p + c + 1
                            split_lo(n, n % 2, n % 2)
            for t in range(NT):
                ve.wait_ge(mx_hi, t + 1)
                ve.tensor_tensor(aTl[:, :, tok(t)], mixT[:, :, tok(t)], aTh[:, :, tok(t)].bitcast(F32), ALU.subtract
                                 ).then_inc(mx_lo, 1)

            ve.wait_ge(mx_lo, NT)
            ve.memset(wr[:, :, :], 0.0).then_inc(init_r, 1)
            ve.memset(smk[:, :, 1:NT], 1.0)
            ve.memset(smk[:, :, 0:1], 0.0)
            ve.memset(LG[:, :, :], -3e38)
            ve.memset(LE[:, :, :], 0.0)
            ve.memset(onesf[:, :], 1.0)

            def logits(t):
                n = rows(t)
                ve.wait_ge(n_lg, t + 1)
                ve.tensor_tensor(LG[0:n, t, 0:NGRP], pq[0:n, t % 2, 0:NGRP], rb[0:n, 0:NGRP], ALU.add)
                ve.tensor_tensor(LE[0:n, t, :], pq[0:n, t % 2, NGRP:NGRP + NE], rb[0:n, NGRP:NGRP + NE], ALU.add
                                 ).then_inc(n_lc, 1)

            for c in range(4):
                for t in range(NT + 3 if c == 3 else NT):
                    q, n = NT * c + t, rows(t)
                    if t < NT:
                        ve.wait_ge(*LX2(t))
                        ve.wait_ge(o_mm, q + 1)
                        xc = x2[0:n, t, c * CW:(c + 1) * CW]
                        ve.tensor_tensor(xc, xc, ZB[q % 2][0:n, 0:CW], ALU.add).then_inc(o_ev, 1)
                    if t == 1 and c < 3:
                        n_ = N_WO + c + 1
                        split_lo(n_, n_ % 2, n_ % 2)
                    if c == 3 and t < NT:
                        ve.wait_ge(n_sq, t + 1)
                        ve.tensor_scalar(msq[0:n, t:t + 1], ssum[0:n, t:t + 1], 1.0 / D, EPS, ALU.mult, ALU.add
                                         ).then_inc(n_ms, 1)
                    if c == 3 and 1 <= t <= NT:
                        u, k = t - 1, rows(t - 1)
                        if u == 0:
                            ve.wait_ge(ld_r, 80)
                        ve.wait_ge(n_rs, u + 1)
                        if u >= 2:
                            ve.wait_ge(n_tr, u - 1)
                            ve.wait_ge(st_h[u % 2], 16 * (u // 2))
                        ve.scalar_tensor_tensor(out=h2[u % 2][0:k, :], in0=x2[0:k, u, :], scalar=rstd[0:k, u:u + 1],
                                                in1=gF[0:k, :], op0=ALU.mult, op1=ALU.mult).then_inc(n_h, 1)
                    if c == 3 and t >= 3:
                        logits(t - 3)

            def bc(a, shape, *at):
                for k in at:
                    a = a.unsqueeze(k)
                return a.to_broadcast(shape)

            gidx, w2, dv, xv_, pg, nm = (r1[:, k, :] for k in range(6))
            io = C("iota")
            ve.drain()
            for t in range(NT):
                ve.max(m8[:, t, :], LG[:, t, :])
            ve.drain()
            for t in range(NT):
                ve.max_index(i8[:, t, :], m8[:, t, :], LG[:, t, :])
            ve.tensor_tensor(ge[:, :, :], LG[:, :, 0:NGRP], m8[:, :, 0:1].to_broadcast([128, NT, NGRP]), ALU.subtract)
            ve.drain()
            ve.tensor_copy(gidx, i8[:, :, 0])
            ve.drain()
            ve.tensor_tensor(gmk[:, :, :], bc(io[:, 0:NGRP], [128, NT, NGRP], 1), bc(gidx, [128, NT, NGRP], 2),
                             ALU.is_equal)
            ve.drain()
            ve.tensor_scalar(gmk[:, :, :], gmk[:, :, :], 1.0, -BIG, ALU.subtract, ALU.mult)
            ve.drain()
            le4 = LE[:, :, :].rearrange("p t (g e) -> p (t g) e", g=NGRP)
            ve.tensor_tensor(le4, le4, bc(gmk[:, :, :].rearrange("p t g -> p (t g)"), [128, NT * NGRP, EPG], 2),
                             ALU.add)
            ve.drain()
            for t in range(NT):
                ve.max(v8[:, t, :], LE[:, t, :])
            ve.drain()
            for t in range(NT):
                ve.max_index(j8[:, t, :], v8[:, t, :], LE[:, t, :])
            ve.tensor_tensor(dv, v8[:, :, 1], v8[:, :, 0], ALU.subtract).then_inc(r_v, 1)
            ve.drain()
            for k in range(2):
                ve.tensor_copy(ee[:, k, :], j8[:, :, k])
            ve.drain()
            for k in range(2):
                ve.tensor_tensor(O[:, k, :, :], bc(io[:, 0:NE], [128, NT, NE], 1), bc(ee[:, k, :], [128, NT, NE], 2),
                                 ALU.is_equal)
            ve.drain()
            for k in range(2):
                ve.tensor_tensor(O[:, k, :, :], O[:, k, :, :], bc(C("valid"), [128, NT, NE], 2), ALU.mult)
            ve.memset(Ac[:, 0, :], 0.0)
            ve.drain()
            ve.tensor_tensor(A[:, :, :], O[:, 0, :, :], O[:, 1, :, :], ALU.add)
            ve.tensor_tensor(Ae[:, :, :], O[:, 0, :, :].rearrange("p t e -> p e t"),
                             O[:, 1, :, :].rearrange("p t e -> p e t"), ALU.add)
            ve.drain()
            flat = lambda a: a[:, :, :].rearrange("p e t -> p (e t)")
            ve.tensor_tensor_scan(flat(cum), flat(smk), flat(Ae), 0.0, ALU.mult, ALU.add)
            ve.drain()
            ve.tensor_copy(Ac[:, 1:NT + 1, :], cum[:, :, :].rearrange("p e t -> p t e")).then_inc(r_v, 1)
            ve.tensor_scalar(thr[:, :], io[:, 0:8], 128.0, 128.0, ALU.mult, ALU.add)
            ve.wait_ge(r_a, 1)
            ve.tensor_reduce(pg, ge[:, :, :], AX.X, ALU.add)
            ve.tensor_scalar(w2, xv_, 1.0, None, ALU.add)
            ve.drain()
            ve.tensor_tensor(nm, pg, w2, ALU.mult)
            ve.drain()
            ve.reciprocal(wgt[:, 0, :], nm)
            ve.drain()
            ve.tensor_tensor(wgt[:, 1, :], wgt[:, 0, :], xv_, ALU.mult)
            ve.wait_ge(r_p, 1)
            ve.tensor_copy(R[:, 0:NT, :], pq[:, 0, 0:NT * NE].rearrange("p (t e) -> p t e", t=NT))
            ve.tensor_copy(R[:, NT, :], pq[:, 1, 0:NE])
            ve.drain()
            for k in range(2):
                ve.wait_ge(st_h[k], 16 * ((NT + 1 - k) // 2))
            ve.tensor_tensor(cmp8[:, :, :], bc(R[:, NT, :], [128, NE, 8], 2), bc(thr[:, :], [128, NE, 8], 1), ALU.is_gt)
            ve.tensor_tensor(RO[:, :, :, :], O[:, :, :, :], bc(R[:, 0:NT, :], [128, 2, NT, NE], 1), ALU.mult)
            ve.drain()
            ov, incl, base, seen = (cnt[:, k, :] for k in range(4))
            ve.tensor_reduce(ov, cmp8[:, :, :], AX.X, ALU.add)
            slv = lambda k: sl[:, k, :]
            r_, b_, q_, rr, blk, t0, mq, place = (slv(k) for k in range(8))
            ro = RO[:, :, :, :].rearrange("p k t e -> p (k t) e")
            ve.tensor_reduce(r_, ro, AX.X, ALU.add)
            ve.drain()
            ve.tensor_tensor_scan(incl, onesf[:, 0:NE], ov, 0.0, ALU.mult, ALU.add)
            ve.tensor_tensor_scan(seen, onesf[:, 0:NE], R[:, NT, :], 0.0, ALU.mult, ALU.add)
            ve.tensor_tensor(cmpq[:, :, :], bc(r_, [128, 2 * NT, 8], 2), bc(thr[:, :], [128, 2 * NT, 8], 1), ALU.is_ge)
            ve.drain()
            ve.tensor_tensor(base, incl, ov, ALU.subtract)
            ve.tensor_tensor(seen, seen, R[:, NT, :], ALU.subtract)
            ve.tensor_reduce(q_, cmpq[:, :, :], AX.X, ALU.add)
            ve.drain()
            ve.tensor_tensor(RO[:, :, :, :], O[:, :, :, :], base.unsqueeze(1).unsqueeze(1).to_broadcast(
                [128, 2, NT, NE]), ALU.mult)
            ve.scalar_tensor_tensor(out=rr, in0=q_, scalar=-128.0, in1=r_, op0=ALU.mult, op1=ALU.add)
            ve.drain()
            ve.tensor_reduce(b_, ro, AX.X, ALU.add)
            ve.drain()
            ve.tensor_tensor(RO[:, :, :, :], O[:, :, :, :], seen.unsqueeze(1).unsqueeze(1).to_broadcast(
                [128, 2, NT, NE]), ALU.mult)
            e_ = ee[:, :, :].rearrange("p k t -> p (k t)")
            ve.scalar_tensor_tensor(out=t0, in0=b_, scalar=float(NE - 1), in1=q_, op0=ALU.add, op1=ALU.add)
            ve.tensor_scalar(mq, q_, 1.0, None, ALU.min)
            ve.drain()
            ve.tensor_tensor(t0, t0, e_, ALU.subtract)
            ve.drain()
            ve.tensor_tensor(t0, t0, mq, ALU.mult)
            ve.drain()
            ve.tensor_tensor(blk, t0, e_, ALU.add)
            ve.drain()
            ve.tensor_reduce(place, ro, AX.X, ALU.add)
            ve.tensor_tensor(OR[:, :, :], bc(io, [128, 2 * NT, 128], 1), bc(rr, [128, 2 * NT, 128], 2), ALU.is_equal)
            ve.tensor_tensor(OB[:, :, 0, :], bc(io[:, 0:NBLK], [128, 2 * NT, NBLK], 1),
                             bc(blk, [128, 2 * NT, NBLK], 2), ALU.is_equal)
            ve.drain()
            ve.tensor_tensor(place, place, r_, ALU.add)
            ve.drain()
            ve.scalar_tensor_tensor(out=t0.rearrange("p (k t) -> p k t", k=2), in0=place.rearrange(
                "p (k t) -> p k t", k=2), scalar=1.0, in1=bc(C("valid"), [128, 2, NT], 1), op0=ALU.add, op1=ALU.mult)
            ve.drain()
            ve.tensor_tensor(OB[:, :, 1, :], OB[:, :, 0, :], bc(t0, [128, 2 * NT, NBLK], 2), ALU.mult)
            ve.drain()
            ob = OB[:, :, 0, :].rearrange("p (k t) b -> p k t b", k=2)
            for k in range(2):
                i_ = ve.tensor_tensor(ob[:, k], ob[:, k], bc(C("tokid"), [128, NT, NBLK], 2), ALU.mult)
            i_.then_inc(r_v, 1)
            ve.tensor_copy(slot[:, :, :].rearrange("p k t -> p (k t)"), place)
            ve.tensor_scalar(big[:, :], C("tokid")[:, 0:1], float(2 ** 17), None, ALU.add)
            ve.tensor_tensor(cmp[:, :, :], bc(incl[0:1], [1, NOVER, NE], 1), bc(io[0:1, 0:NOVER], [1, NOVER, NE], 2),
                             ALU.is_le)
            ve.tensor_scalar(ovf[:, 0, :], io[0:1, 0:NOVER], incl[0:1, NE - 1:NE], None, ALU.is_lt)
            ve.drain()
            ve.tensor_reduce(ovf[:, 1, :], cmp[:, :, :], AX.X, ALU.add)
            ve.drain()
            ve.tensor_scalar(ovf[:, 1, :], ovf[:, 1, :], float(NE - 1), None, ALU.min)
            ve.drain()
            ve.tensor_copy(ovt[:, :, :], ovf[:, 0:2, :])
            for m in range(2):
                split_lo(N_MOE + m, m, m)
            ve.wait_ge(r_p, 2)
            found = pw[:, 0, 0:2 * NBLK].rearrange("p (k b) -> p k b", k=2)
            ve.tensor_scalar(emp[:, :, :], found, 0.0, big[:, 0:1], ALU.is_equal, ALU.mult)
            ve.drain()
            ve.scalar_tensor_tensor(out=idx[:, :, :], in0=found, scalar=-1.0, in1=emp[:, :, :],
                                    op0=ALU.add, op1=ALU.add)
            ve.drain()
            ve.nop().then_inc(r_v, 1)

            def splits_lo(par, n):
                for m in range(3):
                    split_lo(n + m, 3 * par + m, 3 * par + m)

            def hidden(e, par):
                ve.wait_ge(e_sg, E(e))
                ve.wait_ge(e_ht, E(e - 1))
                ve.tensor_tensor(hh[:, :], pw[:, par, 0:FF], sg_[:, :], ALU.mult)
                ve.drain()
                ve.tensor_tensor(hh[:, :], hh[:, :], pw[:, par, FF:2 * FF], ALU.mult).then_inc(e_hh, 1)

            def x_low(e, par):
                ve.wait_ge(e_xh, E(e))
                for g in range(2):
                    i_ = ve.tensor_tensor(xl[par][:, 4 * g:4 * g + 4, :],
                                          TB[0][g][:, :].rearrange("p (a b) -> p a b", a=4),
                                          xh[par][:, 4 * g:4 * g + 4, :].bitcast(F32), ALU.subtract)
                i_.then_inc(e_xl, 1)

            def h_low(e):
                ve.wait_ge(e_hi, E(e))
                ve.tensor_tensor(hTl[:, :, :], pb[0][:, 0:256].rearrange("p (a b) -> p a b", a=2),
                                 hTh[:, :, :].bitcast(F32), ALU.subtract).then_inc(e_lo, 1)

            def both(e, par, k, n, last=False):
                hidden(e - 1, 1 - par)
                if not last:
                    split_lo(n + 3, 3 * (1 - par), 3 * (1 - par))
                h_low(e - 1)
                if not last:
                    split_lo(n + 4, 3 * (1 - par) + 1, 3 * (1 - par) + 1)
                    x_low(e + 1, 1 - par)
                    split_lo(n + 5, 3 * (1 - par) + 2, 3 * (1 - par) + 2)

            split_lo(N_MOE + 2, 2, 2)
            x_low(0, 0)
            splits_lo(1, N_MOE + 3)
            x_low(1, 1)
            with ve.Fori(0, NE // 2 - 1) as i:
                both(2 * i + 1, 1, i, i * 6 + (N_MOE + 3))
                both(2 * i + 2, 0, i + 1, i * 6 + (N_MOE + 6))
            both(NE - 1, 1, NE // 2 - 1, N_MOE + 3 * (NE - 1), last=True)
            hidden(NE - 1, 1)
            h_low(NE - 1)
            any_ = ve.value_load(ovt[0:1, 0, 0:1], min_val=0, max_val=1)
            with ve.If(any_ > 0):
                with ve.Fori(0, NOVER) as j:
                    used_ = ve.value_load(ovt[0:1, 0, bass.ds(j, 1)], min_val=0, max_val=1)
                    with ve.If(used_ > 0):
                        e = j + NE
                        splits_lo(0, j * 3 + (N_MOE + 3 * NE))
                        x_low(e, 0)
                        hidden(e, 0)
                        h_low(e)
                    with ve.Else():
                        ve.nop()
            with ve.Else():
                ve.nop()
                ve.nop()
            for t in range(NT + 1):
                if t < NT:
                    n, x = rows(t), xr[t % NX]
                    ve.wait_ge(ld_x[t % NX], LXF(t))
                    ve.wait_ge(f_y[t % NX], 32 * (t // NX + 1))
                    for k, y in enumerate((y1, y2)):
                        i_ = ve.scalar_tensor_tensor(out=x[0:n, :], in0=y[t % NX][0:n, :],
                                                     scalar=wgt[0:n, k, t:t + 1], in1=x[0:n, :],
                                                     op0=ALU.mult, op1=ALU.add)
                        if k == 0:
                            ve.drain()
                    i_.then_inc(f_a, 1)
                if t >= 1:
                    u, n, x = t - 1, rows(t - 1), xr[(t - 1) % NX]
                    ve.wait_ge(n_rs, NT + u + 1)
                    if u == 0:
                        ve.wait_ge(ld_n, 32)
                    ve.scalar_tensor_tensor(out=x[0:n, :], in0=x[0:n, :], scalar=rstd[0:n, u:u + 1],
                                            in1=gE[0:n, :], op0=ALU.mult, op1=ALU.mult).then_inc(f_o, 1)
                if t < NT:
                    ve.wait_ge(n_sq, NT + t + 1)
                    ve.tensor_scalar(msq[0:rows(t), t:t + 1], ssum[0:rows(t), t:t + 1], 1.0 / D, EPS,
                                     ALU.mult, ALU.add).then_inc(n_ms, 1)

        @block.gpsimd
        def _(gp):
            gp.wait_ge(init_v, 1)
            for t in range(NT):
                n = rows(t)
                gp.wait_ge(x_ms, t + 1)
                gp.tensor_tensor(rstd[0:n, t:t + 1], msq[0:n, t:t + 1], mhalf[0:n, 0:1], ALU.pow).then_inc(x_rs, 1)
            for k, s in enumerate([st_s, st_pc, st_hm] + st_o + st_y):
                gp.dma_start(pad_d[:, k:k + 1], mhalf[0:1, k:k + 1]).then_inc(s, 16)
            gp.wait_ge(gw_l, 1)
            gp.wait_ge(z_mm, NG)
            gp.dma_start(rowc[:, :, :], rowc_d).then_inc(ld_k, 16)
            with nc.allow_non_contiguous_dma(reason="32 floats"):
                gp.dma_start(mpre[:, 1, :], state_m[0].rearrange("b h -> h b")).then_inc(ld_k, 16)
            gp.wait_ge(gv_s, 2)
            with nc.allow_non_contiguous_dma(reason="36 floats"):
                gp.dma_start(p_m[0].rearrange("b h -> h b"), mout[:, 0:1]).then_inc(st_m, 16)
                gp.dma_start(s_m[0].rearrange("b h -> h b"), mout[:, 1:1 + NB]).then_inc(st_m, 16)
            with gp.Fori(0, MH) as h:
                gp.wait_ge(m_ce, K(h, NPT - 1))
                gp.sem_inc(carry[2], 1)
                gp.dma_start(p_C[0, 0, bass.ds(h, 1)].rearrange("o (c p) e -> p (o c) e", p=128),
                             Ce[:, :, 0:MD]).then_inc(st_pc, 16)
                with nc.allow_non_contiguous_dma(reason="a column of the state"):
                    gp.dma_start(p_n[0, 0, bass.ds(h, 1)].rearrange("o (c p) -> p (o c)", p=128),
                                 Ce[:, :, MD]).then_inc(st_pc, 16)
                for b in range(NB):
                    gp.wait_ge(u_sc, K(h, b))
                    gp.sem_inc(carry[2], 1)
                    gp.dma_start(s_C[0, b, bass.ds(h, 1)].rearrange("o (c p) e -> p (o c) e", p=128),
                                 sC[:, b, :, 0:MD]).then_inc(st_s, 16)
                with nc.allow_non_contiguous_dma(reason="a column of the state"):
                    for c in range(2):
                        gp.dma_start(s_n[0, :, bass.ds(h, 1), c * 128:(c + 1) * 128].rearrange("b o p -> p b o"),
                                     sC[:, :, c, MD:MD + 1]).then_inc(st_s, 16)
                gp.wait_ge(hp_m, h + 1)
                gp.tensor_tensor(pst[:, 5, :], pst[:, 3, :], mhalf[:, 0:NT], ALU.pow).then_inc(hp_r, 1)
                gp.wait_ge(hp_o, h + 2)
                gp.sem_inc(carry[2], 1)
                gp.dma_start(hm_d[0:TP, bass.ds(h * MD, MD)].rearrange("(t p) e -> p t e", p=128),
                             nd[:, 0:NPT, 0:MD]).then_inc(st_hm, 16)
                gp.dma_start(hm_d[TP:T, bass.ds(h * MD, MD)], nd[0:TS, NPT, 0:MD]).then_inc(st_hm, 16)

            with gp.Fori(0, NPT // 2) as i:
                for b in range(2):
                    gp.wait_ge(a_oe, OE(i, b, 3))
                    gp.sem_inc(carry[2], 1)
                    gp.dma_start(o_d[bass.ds(i * 256 + b * 128, 128), :], ot[b][:, :]).then_inc(st_o[b], 16)
            gp.dma_start(p_k[0, 0].rearrange("w g d -> w (g d)"), X[1][:, ZK:ZK + 256]).then_inc(st_pc, 16)
            gp.dma_start(p_v[0, 0].rearrange("w g d -> w (g d)"), X[1][:, ZV:ZV + 256]).then_inc(st_pc, 16)
            gp.wait_ge(b_v, 1)
            for o, c in ((s_k, ZK), (s_v, ZV)):
                gp.dma_start(o[0, :, WIN - DS:WIN].rearrange("b t g d -> b t (g d)"),
                             Xs[:, c:c + 256]).then_inc(st_k, 16)

            def times_norm(t):
                gp.wait_ge(ld_t[t % NX], LDT(t))
                x = tin[t % NX][0:rows(t), :]
                gp.tensor_tensor(x, x, tng[0:rows(t), :], ALU.mult).then_inc(f_gn, 1)

            gp.wait_ge(ld_n, 16)
            for t in range(2):
                times_norm(t)
            gp.wait_ge(b_v, 4)
            for p in range(4):
                gp.dma_start(o_d[TP + 8 * p:TP + 8 * p + 8, :].rearrange("t (g d) -> g t d", d=AD),
                             so[:, p, :]).then_inc(st_k, 16)

            for t in range(2, NT):
                times_norm(t)

            for t in range(NT + 1):
                if t < NT:
                    n = rows(t)
                    gp.wait_ge(n_ms, t + 1)
                    gp.tensor_tensor(rstd[0:n, t:t + 1], msq[0:n, t:t + 1], mhalf[0:n, 0:1], ALU.pow
                                     ).then_inc(n_rs, 1)
                if t >= 1:
                    u = t - 1
                    gp.wait_ge(n_h, u + 1)
                    gp.dma_start(h2_d[tok(u), :], h2[u % 2][0:rows(u), :]).then_inc(st_h[u % 2], 16)

            def column(k, e):
                return idx[:, k, e:e + 1] if isinstance(e, int) else idx[:, k, bass.ds(e, 1)]

            def gather(e, par):
                gp.wait_ge(e_xt, E(e - 2))
                gp.tensor_copy(ixs[par][:, :], column(0, e)
                               ).then_inc(e_ix, 1)
                gp.wait_ge(e_ix, e + 1)
                gp.sem_inc(carry[2], 1)
                gp.indirect_dma_start(out=xg[par][:, :], out_offset=None, in_=h2_d,
                                      in_offset=bass.IndirectOffsetOnAxis(ap=ixs[par][:, 0:1], axis=0),
                                      bounds_check=T - 1, oob_is_err=False).then_inc(e_x[par], 16)

            def store_y(e, par):
                gp.wait_ge(e_yc, E(e))
                gp.tensor_copy(dxs[par][:, :], column(1, e)).then_inc(e_dx, 1)
                gp.wait_ge(e_dx, e + 1)
                gp.sem_inc(carry[2], 1)
                gp.indirect_dma_start(out=ys_d, out_offset=bass.IndirectOffsetOnAxis(ap=dxs[par][:, 0:1], axis=0),
                                      in_=yo[par][:, :], in_offset=None, bounds_check=2 * T - 1,
                                      oob_is_err=False).then_inc(st_y[par], 16)

            gp.wait_ge(r_v, R_END)
            gp.wait_ge(st_x, 16 * NT)
            for i in range(2):
                gp.wait_ge(st_h[i], 16 * ((NT + 1 - i) // 2))
            for x in xg:
                gp.memset(x[:, :], 0.0)
            gp.drain()
            gather(0, 0)
            gather(1, 1)
            gather(2, 0)
            with gp.Fori(0, NE // 2 - 2) as i:
                gather(2 * i + 3, 1)
                store_y(2 * i, 0)
                gather(2 * i + 4, 0)
                store_y(2 * i + 1, 1)
            gather(NE - 1, 1)
            store_y(NE - 4, 0)
            store_y(NE - 3, 1)
            store_y(NE - 2, 0)
            store_y(NE - 1, 1)
            any_ = gp.value_load(ovt[0:1, 0, 0:1], min_val=0, max_val=1)
            with gp.If(any_ > 0):
                with gp.Fori(0, NOVER) as j:
                    used_ = gp.value_load(ovt[0:1, 0, bass.ds(j, 1)], min_val=0, max_val=1)
                    with gp.If(used_ > 0):
                        gather(j + NE, 0)
                        store_y(j + NE, 0)
                        gp.wait_ge(st_y[0], j * 16 + 16 * (NE // 2 + 2))
                    with gp.Else():
                        gp.nop()
            with gp.Else():
                gp.nop()
                gp.nop()
            for i in range(2):
                gp.wait_ge(st_y[i], 16 * (NE // 2 + 1))
            gp.sem_inc(m_end, 1)
            for t in range(NT + 2):
                if t < NT:
                    n = rows(t)
                    if t >= NX:
                        gp.wait_ge(f_a, t - NX + 1)
                    for k, y in enumerate((y1, y2)):
                        gp.indirect_dma_start(out=y[t % NX][0:n, :], out_offset=None, in_=ys_d,
                                              in_offset=bass.IndirectOffsetOnAxis(ap=slot[0:n, k, t:t + 1], axis=0),
                                              bounds_check=2 * T - 1).then_inc(f_y[t % NX], 16)
                if t >= 2:
                    u, n = t - 2, rows(t - 2)
                    gp.wait_ge(n_ms, NT + u + 1)
                    gp.tensor_tensor(rstd[0:n, u:u + 1], msq[0:n, u:u + 1], mhalf[0:n, 0:1], ALU.pow
                                     ).then_inc(n_rs, 1)


def constants():
    cst = np.zeros((128, CSTW), np.float32)

    def put(name, a):
        o, w = OFF[name]
        cst[0:a.shape[0], o:o + w] = a.reshape(a.shape[0], w)

    i, j = np.arange(128)[:, None], np.arange(128)[None, :]
    put("ident", (i == j).astype(np.float32))
    put("ustrict", (i < j).astype(np.float32))
    put("mcaus", np.where(i <= j, 0.0, BIG))
    s, t = np.arange(TS)[:, None], np.arange(TS)[None, :]
    put("msamp", np.where((s <= t) & (s // DS == t // DS), 0.0, BIG))
    cur = np.where(j <= i, 0.0, BIG)
    put("amask", np.concatenate([np.where(j > i, 0.0, BIG), cur], 1))
    put("amask0", np.concatenate([np.full((128, 128), BIG), cur], 1))
    half = AD // 8
    freq = np.power(np.float32(500000.0), -np.arange(0, 2 * half, 2, dtype=np.float32) / np.float32(2 * half))
    pos = np.zeros((128, NT), np.float32)
    pos[:, :NPT] = np.arange(128)[:, None] + 128 * np.arange(NPT)[None, :]
    pos[:TS, NPT] = 4096 + np.arange(TS) % DS
    ang = (pos[:, :, None] * freq.astype(np.float32)).astype(np.float32)
    put("cos", np.cos(ang))
    put("sin", np.sin(ang))
    put("iota", np.broadcast_to(j, (128, 128)).astype(np.float32))
    tid = np.arange(128)[:, None] + 128 * np.arange(NT)[None, :]
    put("valid", (tid < T).astype(np.float32))
    put("tokid", np.where(tid < T, tid + 1, 0).astype(np.float32))
    put("bmq", np.broadcast_to((t // DS == np.arange(NB)[:, None])[None], (128, NB, TS)).astype(np.float32))
    put("bmk", (i // DS == np.arange(NB)[None, :]).astype(np.float32))
    sm = np.full((AG, 4, 2, DS, NB // 2, SMW), BIG, np.float32)
    for b2 in range(2):
        for t_ in range(DS):
            for p in range(NB // 2):
                sm[:, :, b2, t_, p, b2 * WIN + t_ + 1:(b2 + 1) * WIN] = 0.0
                n0 = 2 * WIN + DS * (2 * p + b2)
                sm[:, :, b2, t_, p, n0:n0 + t_ + 1] = 0.0
    rowc = np.zeros((MH, 2, T), np.float32)
    rowc[:, 0] = 1.0
    rowc[:, 0, 0:TP:128] = 0.0
    rowc[:, 0, TP::DS] = 0.0
    rowc[:, 1, TP::DS] = BIG
    return cst, sm.reshape(128, NB // 2, SMW), rowc


_INS = ["x_prompt", "x_sample", "state_C", "state_n", "state_m", "cache_k", "cache_v", "w_in", "b_if",
        "norm_mix", "mlstm_norm", "attn_sinks", "w_proj_a", "w_proj_b", "w_out", "norm_ffn", "w_group",
        "b_group", "w_router", "b_router", "w_gate_e", "w_up_e", "w_down_e", "norm_final"]
_OUTS = [(1, TP, D), (NB, DS, D),
         (1, 1, MH, MD, MD), (1, 1, MH, MD), (1, 1, MH), (1, 1, WIN, AG, AD), (1, 1, WIN, AG, AD),
         (1, NB, MH, MD, MD), (1, NB, MH, MD), (1, NB, MH), (1, NB, WIN, AG, AD), (1, NB, WIN, AG, AD)]


def kernel(**inputs):
    import concourse.bacc as _bacc
    from concourse.bass_utils import run_bass_kernel_spmd as _run

    nc = _bacc.Bacc("TRN2", target_bir_lowering=False, num_devices=1)
    arrays = {f"in_{name}": np.ascontiguousarray(inputs[name]) for name in _INS}
    arrays.update(zip(("in_cst", "in_smask", "in_rowc"), constants()))
    args = [nc.dram_tensor(name, a.shape, mybir.dt.from_np(a.dtype), kind="ExternalInput").ap()
            for name, a in arrays.items()]
    for i, shape in enumerate(_OUTS):
        args.append(nc.dram_tensor(f"out_{i}", shape, F32, kind="ExternalOutput").ap())
    build(nc, *args)
    r = _run(nc, [arrays], core_ids=[0])
    return tuple(r.results[0][f"out_{i}"] for i in range(len(_OUTS)))
```
